# Optimizing a Trainium2 kernel written in Bass

```python
import math
import jax, jax.numpy as jnp
from jax import lax
import numpy as np
import jax
import jax.numpy as jnp

D_MODEL = 1024
BATCH = 1
SEQ = 512
DEPTH = 1

CTX_LEN = 256
GRID_W = 64
D_MIX = D_MODEL
D_ATTN = D_MIX // 2
D_CONV = D_MIX - D_ATTN
HEAD_DIM = 64
N_Q_HEADS = D_ATTN // HEAD_DIM
N_KV_HEADS = 2
GROUP = N_Q_HEADS // N_KV_HEADS
ROPE_AXIS_DIM = HEAD_DIM // 2
ROPE_THETA = 10000.0
Q_BLOCK = 128
CONV_WIDTH = 31
CONV_PAD = (CONV_WIDTH - 1) // 2
EPS = 1e-6

Q_LO, Q_HI = 0, D_ATTN
K_LO, K_HI = Q_HI, Q_HI + N_KV_HEADS * HEAD_DIM
V_LO, V_HI = K_HI, K_HI + N_KV_HEADS * HEAD_DIM
ZA_LO, ZA_HI = V_HI, V_HI + D_ATTN
GLU_LO, GLU_HI = ZA_HI, ZA_HI + 2 * D_CONV
ZC_LO, ZC_HI = GLU_HI, GLU_HI + D_CONV
D_IN = ZC_HI


def rms_norm(x, w):
    xf = x.astype(jnp.float32)
    y = xf * lax.rsqrt(jnp.mean(xf * xf, axis=-1, keepdims=True) + EPS)
    return (y * w.astype(jnp.float32)).astype(x.dtype)

def layer_norm(x, w, b):
    xf = x.astype(jnp.float32)
    mu = jnp.mean(xf, axis=-1, keepdims=True)
    var = jnp.mean(jnp.square(xf - mu), axis=-1, keepdims=True)
    y = (xf - mu) * lax.rsqrt(var + EPS)
    return (y * w.astype(jnp.float32) + b.astype(jnp.float32)).astype(x.dtype)

def grid_angles(n_tokens, dtype):
    rows = n_tokens // GRID_W
    row = jnp.repeat(jnp.arange(rows, dtype=jnp.float32), GRID_W)
    col = jnp.tile(jnp.arange(GRID_W, dtype=jnp.float32), rows)
    freqs = ROPE_THETA ** (-jnp.arange(0, ROPE_AXIS_DIM, 2, dtype=jnp.float32) / ROPE_AXIS_DIM)
    ang_r = row[:, None] * freqs[None, :]
    ang_c = col[:, None] * freqs[None, :]
    return (jnp.cos(ang_r).astype(dtype), jnp.sin(ang_r).astype(dtype),
            jnp.cos(ang_c).astype(dtype), jnp.sin(ang_c).astype(dtype))

def rope_axis(x, cos, sin):
    cos = cos[None, :, None, :]
    sin = sin[None, :, None, :]
    x1, x2 = jnp.split(x, 2, axis=-1)
    return jnp.concatenate([x1 * cos - x2 * sin, x1 * sin + x2 * cos], axis=-1)

def rope_2d(x, angles):
    cr, sr, cc, sc = angles
    return jnp.concatenate([rope_axis(x[..., :ROPE_AXIS_DIM], cr, sr),
                            rope_axis(x[..., ROPE_AXIS_DIM:], cc, sc)], axis=-1)

def qk_heads(p, qn_w, kn_w):
    B, S, _ = p.shape
    q = p[..., Q_LO:Q_HI].reshape(B, S, N_Q_HEADS, HEAD_DIM)
    k = p[..., K_LO:K_HI].reshape(B, S, N_KV_HEADS, HEAD_DIM)
    v = p[..., V_LO:V_HI].reshape(B, S, N_KV_HEADS, HEAD_DIM)
    return rms_norm(q, qn_w), rms_norm(k, kn_w), v

def kv_heads(p_kv, kn_w):
    B, S, _ = p_kv.shape
    kv = p_kv.reshape(B, S, 2, N_KV_HEADS, HEAD_DIM)
    return rms_norm(kv[:, :, 0], kn_w), kv[:, :, 1]

def attend_blocked(q, k, v):
    B, S, _, _ = q.shape
    scale = 1.0 / math.sqrt(HEAD_DIM)
    qb = q.reshape(B, S // Q_BLOCK, Q_BLOCK, N_KV_HEADS, GROUP, HEAD_DIM).transpose(1, 0, 2, 3, 4, 5)

    def one_block(qblk):
        s = jnp.einsum('bqkgd,bskd->bkgqs', qblk, k).astype(jnp.float32) * scale
        pr = jax.nn.softmax(s, axis=-1).astype(v.dtype)
        return jnp.einsum('bkgqs,bskd->bqkgd', pr, v)

    o = lax.map(one_block, qb)
    return o.transpose(1, 0, 2, 3, 4, 5).reshape(B, S, D_ATTN)

def attend_dense(q, k, v):
    B, C, _, _ = q.shape
    qg = q.reshape(B, C, N_KV_HEADS, GROUP, HEAD_DIM)
    s = jnp.einsum('bqkgd,bskd->bkgqs', qg, k).astype(jnp.float32) / math.sqrt(HEAD_DIM)
    pr = jax.nn.softmax(s, axis=-1).astype(v.dtype)
    return jnp.einsum('bkgqs,bskd->bqkgd', pr, v).reshape(B, C, D_ATTN)

def conformer_conv(glu_in, conv_w, conv_b, ln_w, ln_b, w_pw, b_pw):
    a, g = jnp.split(glu_in, 2, axis=-1)
    u = a * jax.nn.sigmoid(g)
    y = lax.conv_general_dilated(u, conv_w[:, None, :].astype(u.dtype), window_strides=(1,),
                                 padding=[(CONV_PAD, CONV_PAD)],
                                 dimension_numbers=('NWC', 'WIO', 'NWC'),
                                 feature_group_count=D_CONV) + conv_b
    y = jax.nn.silu(layer_norm(y, ln_w, ln_b))
    return y @ w_pw + b_pw

def first_inputs(seed: int = 0) -> dict:
    key = jax.random.key(seed)
    ks = jax.random.split(key, 20)
    nrm = jax.random.normal
    f32 = jnp.float32
    return {
        "x": nrm(ks[0], (BATCH, SEQ, D_MODEL), f32),
        "c": nrm(ks[1], (BATCH, D_MODEL), f32),
        "ctx": nrm(ks[2], (BATCH, CTX_LEN, D_MODEL), f32),
        "c_ctx": nrm(ks[3], (D_MODEL,), f32),
        "w_mod": nrm(ks[4], (DEPTH, D_MODEL, 3 * D_MODEL), f32) * D_MODEL ** -0.5,
        "b_mod": nrm(ks[5], (DEPTH, 3 * D_MODEL), f32) * 0.02,
        "norm_w": 1.0 + 0.05 * nrm(ks[6], (DEPTH, D_MODEL), f32),
        "w_in": nrm(ks[7], (DEPTH, D_MODEL, D_IN), f32) * D_MODEL ** -0.5,
        "q_norm_w": 1.0 + 0.05 * nrm(ks[8], (DEPTH, HEAD_DIM), f32),
        "k_norm_w": 1.0 + 0.05 * nrm(ks[9], (DEPTH, HEAD_DIM), f32),
        "conv_w": nrm(ks[10], (DEPTH, CONV_WIDTH, D_CONV), f32) * CONV_WIDTH ** -0.5,
        "conv_b": nrm(ks[11], (DEPTH, D_CONV), f32) * 0.02,
        "conv_ln_w": 1.0 + 0.05 * nrm(ks[12], (DEPTH, D_CONV), f32),
        "conv_ln_b": nrm(ks[13], (DEPTH, D_CONV), f32) * 0.02,
        "w_pw": nrm(ks[14], (DEPTH, D_CONV, D_CONV), f32) * D_CONV ** -0.5,
        "b_pw": nrm(ks[15], (DEPTH, D_CONV), f32) * 0.02,
        "w_out": nrm(ks[16], (DEPTH, D_MIX, D_MODEL), f32) * D_MIX ** -0.5,
    }

def first_block(x, c, ctx, c_ctx, w_mod, b_mod, norm_w, w_in, q_norm_w, k_norm_w,
              conv_w, conv_b, conv_ln_w, conv_ln_b, w_pw, b_pw, w_out):
    S = x.shape[1]
    angles = grid_angles(S, x.dtype)
    h, hc = x, ctx
    for l in range(DEPTH):
        mod = jax.nn.silu(c) @ w_mod[l] + b_mod[l]
        shift, scale, gate = jnp.split(mod, 3, axis=-1)
        mod_c = jax.nn.silu(c_ctx) @ w_mod[l] + b_mod[l]
        shift_c, scale_c, gate_c = jnp.split(mod_c, 3, axis=-1)

        u = rms_norm(h, norm_w[l]) * (1.0 + scale[:, None, :]) + shift[:, None, :]
        uc = rms_norm(hc, norm_w[l]) * (1.0 + scale_c) + shift_c

        p = u @ w_in[l]
        q, k, v = qk_heads(p, q_norm_w[l], k_norm_w[l])
        q = rope_2d(q, angles)
        k = rope_2d(k, angles)

        if l == DEPTH - 1:
            k_c, v_c = kv_heads(uc @ w_in[l][:, K_LO:V_HI], k_norm_w[l])
        else:
            pc = uc @ w_in[l]
            q_c, k_c, v_c = qk_heads(pc, q_norm_w[l], k_norm_w[l])
            attn_c = attend_dense(q_c, k_c, v_c) * jax.nn.silu(pc[..., ZA_LO:ZA_HI])
            conv_c = conformer_conv(pc[..., GLU_LO:GLU_HI], conv_w[l], conv_b[l], conv_ln_w[l],
                                    conv_ln_b[l], w_pw[l], b_pw[l]) * jax.nn.silu(pc[..., ZC_LO:ZC_HI])
            out_c = jnp.concatenate([attn_c, conv_c], axis=-1) @ w_out[l]

        k_all = jnp.concatenate([k_c, k], axis=1)
        v_all = jnp.concatenate([v_c, v], axis=1)
        attn = attend_blocked(q, k_all, v_all) * jax.nn.silu(p[..., ZA_LO:ZA_HI])

        conv = conformer_conv(p[..., GLU_LO:GLU_HI], conv_w[l], conv_b[l], conv_ln_w[l],
                              conv_ln_b[l], w_pw[l], b_pw[l]) * jax.nn.silu(p[..., ZC_LO:ZC_HI])

        out = jnp.concatenate([attn, conv], axis=-1) @ w_out[l]
        h = h + gate[:, None, :] * out
        if l < DEPTH - 1:
            hc = hc + gate_c * out_c
    return h


N_MIXERS = 2
MIX_WIDTH = 3 * D_MODEL // 4
MEM_WIDTH = D_MODEL - MIX_WIDTH
MEM_HEADS = 4
MEM_HEAD_DIM = MEM_WIDTH // MEM_HEADS
MEM_TOKENS = 256
RWKV_HEADS = MIX_WIDTH // HEAD_DIM
DECAY_LORA = 64
ICLR_LORA = 64
GATE_LORA = 128
RWKV_COLS = 3 * MIX_WIDTH + DECAY_LORA + ICLR_LORA + GATE_LORA
RWKV_IN = RWKV_COLS + MEM_WIDTH
DIFF_HEADS = MIX_WIDTH // (2 * HEAD_DIM)
DIFF_IN = 3 * MIX_WIDTH + MEM_WIDTH
D_FF = 4 * D_MODEL
N_RWKV_LAYERS = (DEPTH + N_MIXERS - 1) // N_MIXERS
N_DIFF_LAYERS = DEPTH // N_MIXERS
RMS_EPS = 1e-6
GN_EPS = 64e-5


def rms_norm_2(x, g=None):
    xf = x.astype(jnp.float32)
    y = xf * lax.rsqrt(jnp.mean(jnp.square(xf), axis=-1, keepdims=True) + RMS_EPS)
    if g is not None:
        y = y * g.astype(jnp.float32)
    return y.astype(x.dtype)

def token_shift(z, mu):
    z_prev = jnp.pad(z[:, :-1], ((0, 0), (1, 0), (0, 0)))
    return z + (z_prev - z) * mu

def delta_rule_scan(r, w, k, v, a, b):
    B, T, H, N = r.shape
    xs = tuple(jnp.moveaxis(z.astype(jnp.float32), 1, 0) for z in (r, w, k, v, a, b))

    def step(S, inp):
        r_t, w_t, k_t, v_t, a_t, b_t = inp
        sa = jnp.einsum('bhvk,bhk->bhv', S, a_t)
        S = (S * w_t[:, :, None, :] + sa[..., None] * b_t[:, :, None, :]
             + v_t[..., None] * k_t[:, :, None, :])
        return S, jnp.einsum('bhvk,bhk->bhv', S, r_t)

    S0 = jnp.zeros((B, H, N, N), jnp.float32)
    _, y = lax.scan(step, S0, xs)
    return jnp.moveaxis(y, 0, 1)

def rwkv7_time_mix(h, w_in, mu, w0, w2, a0, a2, g2, k_k, k_a, r_k, lnx_g, lnx_b):
    B, T, _ = h.shape
    H, N = RWKV_HEADS, HEAD_DIM
    proj = h @ w_in
    slab = token_shift(proj[..., :RWKV_COLS], mu)
    q_mem = proj[..., RWKV_COLS:]
    c3 = 3 * MIX_WIDTH
    r, k, v, wd, ad, gd = jnp.split(
        slab, [MIX_WIDTH, 2 * MIX_WIDTH, c3, c3 + DECAY_LORA, c3 + DECAY_LORA + ICLR_LORA], axis=-1)
    log_w = -jax.nn.softplus(-(w0 + jnp.tanh(wd) @ w2)) - 0.5
    decay = jnp.exp(-jnp.exp(log_w.astype(jnp.float32)))
    a = jax.nn.sigmoid(a0 + ad @ a2)
    g = jax.nn.sigmoid(gd) @ g2

    def heads(z):
        return z.reshape(B, T, H, N)

    kk = heads(k * k_k).astype(jnp.float32)
    kk = kk / jnp.maximum(jnp.sqrt(jnp.sum(jnp.square(kk), axis=-1, keepdims=True)), 1e-12)
    k = k * (1.0 + (a - 1.0) * k_a)
    a_h = heads(a).astype(jnp.float32)
    r_h, k_h, v_h = heads(r), heads(k), heads(v)
    y = delta_rule_scan(r_h, heads(decay), k_h, v_h, -kk, kk * a_h)
    mean = jnp.mean(y, axis=-1, keepdims=True)
    var = jnp.mean(jnp.square(y - mean), axis=-1, keepdims=True)
    y = ((y - mean) * lax.rsqrt(var + GN_EPS)).reshape(B, T, MIX_WIDTH)
    y = (y * lnx_g.astype(jnp.float32) + lnx_b.astype(jnp.float32)).astype(h.dtype)
    bonus = (jnp.sum(r_h * k_h * r_k, axis=-1, keepdims=True) * v_h).reshape(B, T, MIX_WIDTH)
    return (y + bonus) * g, q_mem

def alibi_slopes(n):
    return jnp.exp2(-8.0 * jnp.arange(1, n + 1, dtype=jnp.float32) / n)

def causal_diff_attention(q, k, v, lam, slopes):
    B, T, H, _, d = q.shape
    nb = T // Q_BLOCK
    qb = jnp.moveaxis(q.reshape(B, nb, Q_BLOCK, H, 2, d), 1, 0)
    starts = jnp.arange(nb, dtype=jnp.int32) * Q_BLOCK
    k_pos = jnp.arange(T, dtype=jnp.int32)
    scale = d ** -0.5

    def block(args):
        q_blk, start = args
        q_pos = start + jnp.arange(Q_BLOCK, dtype=jnp.int32)
        dist = q_pos[:, None] - k_pos[None, :]
        bias = -slopes[:, None, None] * dist.astype(jnp.float32)[None]
        s = jnp.einsum('bqhcd,bkhcd->bhcqk', q_blk, k).astype(jnp.float32) * scale
        s = jnp.where(dist >= 0, s + bias[None, :, None], -jnp.inf)
        p = jax.nn.softmax(s, axis=-1)
        p = p[:, :, 0] - lam * p[:, :, 1]
        return jnp.einsum('bhqk,bkhe->bqhe', p.astype(v.dtype), v)

    out = lax.map(block, (qb, starts))
    return jnp.moveaxis(out, 0, 1).reshape(B, T, H, 2 * d)

def diff_lambda_init(layer):
    return 0.8 - 0.6 * math.exp(-0.3 * layer)

def diff_attention_mixer(h, w_in, q_g, k_g, lq1, lk1, lq2, lk2, subln_g, lambda_init):
    B, T, _ = h.shape
    H, d = DIFF_HEADS, HEAD_DIM
    proj = h @ w_in
    q = rms_norm_2(proj[..., :MIX_WIDTH].reshape(B, T, H, 2, d), q_g)
    k = rms_norm_2(proj[..., MIX_WIDTH:2 * MIX_WIDTH].reshape(B, T, H, 2, d), k_g)
    v = proj[..., 2 * MIX_WIDTH:3 * MIX_WIDTH].reshape(B, T, H, 2 * d)
    q_mem = proj[..., 3 * MIX_WIDTH:]
    lam = (jnp.exp(jnp.sum(lq1 * lk1).astype(jnp.float32))
           - jnp.exp(jnp.sum(lq2 * lk2).astype(jnp.float32)) + lambda_init)
    o = causal_diff_attention(q, k, v, lam, alibi_slopes(H))
    o = rms_norm_2(o, subln_g) * (1.0 - lambda_init)
    return o.reshape(B, T, MIX_WIDTH), q_mem

def memory_cross_attention(q_mem, k_mem, v_mem, q_g, k_g):
    B, T, _ = q_mem.shape
    q = rms_norm_2(q_mem.reshape(B, T, MEM_HEADS, MEM_HEAD_DIM), q_g)
    k = k_mem * k_g
    s = jnp.einsum('bthd,bmhd->bhtm', q, k).astype(jnp.float32) * MEM_HEAD_DIM ** -0.5
    p = jax.nn.softmax(s, axis=-1).astype(v_mem.dtype)
    return jnp.einsum('bhtm,bmhd->bthd', p, v_mem).reshape(B, T, MEM_WIDTH)

def second_inputs(seed: int = 0) -> dict:
    key = jax.random.key(seed)
    keys = jax.random.split(key, 40)
    counter = [0]

    def next_key():
        counter[0] += 1
        return keys[counter[0] - 1]

    def nrm(shape, scale):
        return jax.random.normal(next_key(), shape, jnp.float32) * scale

    def gain(shape):
        return 1.0 + nrm(shape, 0.05)

    def unif(shape, lo, hi):
        return jax.random.uniform(next_key(), shape, jnp.float32, lo, hi)

    NR, ND = N_RWKV_LAYERS, N_DIFF_LAYERS
    return {
        "x": nrm((BATCH, SEQ, D_MODEL), 1.0),
        "mem": nrm((BATCH, MEM_TOKENS, D_MODEL), 1.0),
        "norm_mix_g": gain((DEPTH, D_MODEL)),
        "norm_ffn_g": gain((DEPTH, D_MODEL)),
        "w_out": nrm((DEPTH, D_MODEL, D_MODEL), D_MODEL ** -0.5),
        "w_ff1": nrm((DEPTH, D_MODEL, D_FF), D_MODEL ** -0.5),
        "w_ff2": nrm((DEPTH, D_FF, D_MODEL), D_FF ** -0.5),
        "mem_norm_g": gain((D_MODEL,)),
        "w_mem_kv": nrm((D_MODEL, 2 * MEM_WIDTH), D_MODEL ** -0.5),
        "mem_q_norm_g": gain((DEPTH, MEM_HEAD_DIM)),
        "mem_k_norm_g": gain((DEPTH, MEM_HEAD_DIM)),
        "rw_in": nrm((NR, D_MODEL, RWKV_IN), D_MODEL ** -0.5),
        "rw_mu": unif((NR, RWKV_COLS), 0.0, 1.0),
        "rw_w0": unif((NR, MIX_WIDTH), -6.0, -1.0),
        "rw_w2": nrm((NR, DECAY_LORA, MIX_WIDTH), 0.5 * DECAY_LORA ** -0.5),
        "rw_a0": nrm((NR, MIX_WIDTH), 0.1),
        "rw_a2": nrm((NR, ICLR_LORA, MIX_WIDTH), ICLR_LORA ** -0.5),
        "rw_g2": nrm((NR, GATE_LORA, MIX_WIDTH), GATE_LORA ** -0.5),
        "rw_k_k": 0.85 + nrm((NR, MIX_WIDTH), 0.05),
        "rw_k_a": gain((NR, MIX_WIDTH)),
        "rw_r_k": nrm((NR, RWKV_HEADS, HEAD_DIM), 0.1),
        "rw_lnx_g": gain((NR, MIX_WIDTH)),
        "rw_lnx_b": nrm((NR, MIX_WIDTH), 0.01),
        "df_in": nrm((ND, D_MODEL, DIFF_IN), D_MODEL ** -0.5),
        "df_q_norm_g": gain((ND, 2, HEAD_DIM)),
        "df_k_norm_g": gain((ND, 2, HEAD_DIM)),
        "df_lq1": nrm((ND, HEAD_DIM), 0.1),
        "df_lk1": nrm((ND, HEAD_DIM), 0.1),
        "df_lq2": nrm((ND, HEAD_DIM), 0.1),
        "df_lk2": nrm((ND, HEAD_DIM), 0.1),
        "df_subln_g": gain((ND, 2 * HEAD_DIM)),
    }

def second_block(x, mem, norm_mix_g, norm_ffn_g, w_out, w_ff1, w_ff2, mem_norm_g, w_mem_kv,
              mem_q_norm_g, mem_k_norm_g, rw_in, rw_mu, rw_w0, rw_w2, rw_a0, rw_a2, rw_g2,
              rw_k_k, rw_k_a, rw_r_k, rw_lnx_g, rw_lnx_b, df_in, df_q_norm_g, df_k_norm_g,
              df_lq1, df_lk1, df_lq2, df_lk2, df_subln_g):
    B, M, _ = mem.shape
    kv = rms_norm_2(mem, mem_norm_g) @ w_mem_kv
    k_mem = rms_norm_2(kv[..., :MEM_WIDTH].reshape(B, M, MEM_HEADS, MEM_HEAD_DIM))
    v_mem = kv[..., MEM_WIDTH:].reshape(B, M, MEM_HEADS, MEM_HEAD_DIM)

    for layer in range(DEPTH):
        j = layer // N_MIXERS
        h = rms_norm_2(x, norm_mix_g[layer])
        if layer % N_MIXERS == 0:
            mix, q_mem = rwkv7_time_mix(h, rw_in[j], rw_mu[j], rw_w0[j], rw_w2[j], rw_a0[j],
                                        rw_a2[j], rw_g2[j], rw_k_k[j], rw_k_a[j], rw_r_k[j],
                                        rw_lnx_g[j], rw_lnx_b[j])
        else:
            mix, q_mem = diff_attention_mixer(h, df_in[j], df_q_norm_g[j], df_k_norm_g[j],
                                              df_lq1[j], df_lk1[j], df_lq2[j], df_lk2[j],
                                              df_subln_g[j], diff_lambda_init(layer))
        mem_out = memory_cross_attention(q_mem, k_mem, v_mem, mem_q_norm_g[layer],
                                         mem_k_norm_g[layer])
        x = x + jnp.concatenate([mix, mem_out], axis=-1) @ w_out[layer]
        u = rms_norm_2(x, norm_ffn_g[layer]) @ w_ff1[layer]
        x = x + jnp.square(jax.nn.relu(u)) @ w_ff2[layer]
    return x


def setup_inputs(seed=0):
    out = dict(first_inputs(seed))
    for name, value in second_inputs(seed + 1).items():
        if name != "x":
            out[name + "_2"] = value
    return out


def reference(
    x, c, ctx, c_ctx, w_mod, b_mod, norm_w, w_in, q_norm_w, k_norm_w, conv_w, conv_b, conv_ln_w,
    conv_ln_b, w_pw, b_pw, w_out, mem_2, norm_mix_g_2, norm_ffn_g_2, w_out_2, w_ff1_2, w_ff2_2,
    mem_norm_g_2, w_mem_kv_2, mem_q_norm_g_2, mem_k_norm_g_2, rw_in_2, rw_mu_2, rw_w0_2,
    rw_w2_2, rw_a0_2, rw_a2_2, rw_g2_2, rw_k_k_2, rw_k_a_2, rw_r_k_2, rw_lnx_g_2, rw_lnx_b_2,
    df_in_2, df_q_norm_g_2, df_k_norm_g_2, df_lq1_2, df_lk1_2, df_lq2_2, df_lk2_2, df_subln_g_2,
):
    x = first_block(
        x, c, ctx, c_ctx, w_mod, b_mod, norm_w, w_in, q_norm_w, k_norm_w, conv_w, conv_b,
        conv_ln_w, conv_ln_b, w_pw, b_pw, w_out,
    )
    return second_block(
        x, mem_2, norm_mix_g_2, norm_ffn_g_2, w_out_2, w_ff1_2, w_ff2_2, mem_norm_g_2,
        w_mem_kv_2, mem_q_norm_g_2, mem_k_norm_g_2, rw_in_2, rw_mu_2, rw_w0_2, rw_w2_2, rw_a0_2,
        rw_a2_2, rw_g2_2, rw_k_k_2, rw_k_a_2, rw_r_k_2, rw_lnx_g_2, rw_lnx_b_2, df_in_2,
        df_q_norm_g_2, df_k_norm_g_2, df_lq1_2, df_lk1_2, df_lq2_2, df_lk2_2, df_subln_g_2,
    )


_drawn_inputs = setup_inputs


def setup_inputs(seed=0):
    import zlib

    import numpy as np

    out = dict(_drawn_inputs(seed))
    spreads = {}
    factors = {'ctx': 3.117,
     'b_mod': 2.964,
     'q_norm_w': 8.0,
     'k_norm_w': 8.0,
     'conv_b': 7.034,
     'conv_ln_w': 3.613,
     'conv_ln_b': 8.0,
     'b_pw': 5.864,
     'mem_norm_g_2': 8.0,
     'mem_q_norm_g_2': 8.0,
     'mem_k_norm_g_2': 8.0,
     'rw_w2_2': 4.837,
     'rw_a0_2': 3.578,
     'rw_k_k_2': 11.239,
     'rw_lnx_g_2': 11.696,
     'rw_lnx_b_2': 55.264,
     'norm_ffn_g_2': 3.637,
     'rw_r_k_2': 3.107}
    for name, (base, spread) in spreads.items():
        noise = np.random.default_rng([zlib.crc32(name.encode()), seed]).standard_normal(out[name].shape)
        drawn = base * np.exp(spread * noise) if base else spread * noise
        out[name] = jnp.asarray(drawn.astype(out[name].dtype))
    for name, factor in factors.items():
        out[name] = (out[name] * factor).astype(out[name].dtype)
    return out
```

```python
from contextlib import ExitStack

import numpy as np

import concourse.bass as bass
from concourse import mybir

F32 = mybir.dt.float32
ALU = mybir.AluOpType
ACT = mybir.ActivationFunctionType
AX = mybir.AxisListType.X

P = 128
D = 1024
DK = D // P
S = 512
SC = 256
SM = 256
DH = 64
NQ = 4
CK = 4
TAPS = 31
PAD = (TAPS - 1) // 2
SKEYS = SC + S
KT = SKEYS // P
MT = SM // P
NP = 6
C = 64
NC = S // C
G = 4
NG = NC // G
LEVELS = (2, 4, 8, 16, 32)
FF = 4096 // P
GRID_W = 64
EPS = 1e-6
GN_EPS = 64e-5
DECAY = float(np.exp(-0.5))
KK_LEAST = 1e-24
KK_SCALE = 2.0 ** 16
SIG_MOST = 1e18
RING = 6
UNITS = NQ * 2 * (S // P)
MUNITS = 2 * 2 * (S // P)

VEC = [("norm_w", 8), ("b_shift", 8), ("b_scale", 8), ("b_gate", 8), ("qn", 1), ("kn", 1),
       ("conv_b", 4), ("ln_w", 4), ("ln_b", 4), ("b_pw", 4), ("conv_w", 4 * TAPS), ("mu", 20),
       ("w0", 6), ("a0", 6), ("k_k", 6), ("k_a", 6), ("r_k", 6), ("lnx_g", 6), ("lnx_b", 6),
       ("g_mix", 8), ("g_ffn", 8), ("g_mem", 8), ("mqn", 1), ("mkn", 1), ("cc", 16)]
AT = {}
_n = 0
for _k, _w in VEC:
    AT[_k] = _n
    _n += _w
NVEC = _n
LORA_AT, G2_AT = NVEC, NVEC + 768
NSMALL = NVEC + 2 * 768
MU_WDAD, MU_GD, MU_PAIR = 0, 1, 2

TAB = [("cos", S), ("sin", S), ("reset", S), ("rot", P), ("heads", P), ("ones", P), ("ident", P),
       ("before", P), ("upto", P), ("m1", P), ("m1t", P)] + [(f"m{b}", P) for b in LEVELS]
TAT = {}
_n = 0
for _k, _w in TAB:
    TAT[_k] = (_n, _w)
    _n += _w
NTAB = _n

BLOCKS = (["kmem0", "kmem1", "vmem0", "vmem1"]
          + [f"shift{k}" for k in range(DK)] + [f"scale{k}" for k in range(DK)]
          + [f"{x}{i}" for i in range(CK) for x in "ag"]
          + ["k", "v"] + [f"q{j}" for j in range(NQ)] + [f"zc{i}" for i in range(CK)]
          + [f"za{j}" for j in range(NQ)] + ["pw0", "pw1"] + [f"gate{k}" for k in range(DK)]
          + [f"out{m}" for m in range(DK)]
          + ["wdad", "gd", "qm0", "qm1"] + [f"{x}_{p}" for p in range(NP) for x in "krv"]
          + [f"mix{m}" for m in range(DK)] + [f"up{m}" for m in range(FF)]
          + [f"down{m}_{k}" for m in range(DK) for k in range(4)])
BLOCK_AT = {n: i for i, n in enumerate(BLOCKS)}


def psum_order():
    o = [(n, 1, None) for n in ("mem_sum", "ctx_sum", "x_sum", "kmem0", "kmem1", "hs0", "hs1", "vmem")]

    def add(*names):
        o.extend((n, 1, None) for n in names)

    for g in ("shift", "scale"):
        add(f"{g}_lo", f"{g}_hi", f"{g}_t")
    for i in range(CK):
        add(f"a{i}", f"g{i}")
    add("kx", "kc", "hs2", "rot0", "hs3", "v_lo", "v_hi")
    for j in range(NQ):
        add(f"q{j}", f"hs{4 + j}", f"rot{1 + j}")
    add(*(f"zc{i}" for i in range(CK)), *(f"za{j}" for j in range(NQ)))
    pair = 0
    for u in range(UNITS + 1):
        if u < UNITS:
            o.append((f"s{u}", 2, pair % 3 * 2))
            pair += 1
        if u:
            o.append((f"pt{u - 1}", 2, pair % 3 * 2))
            pair += 1
            if (u - 1) % 8 == 0:
                o.append((f"o{(u - 1) // 8}", 1, 6 + (u - 1) // 8 % 2))
    add("cmean", "cvar", *(f"pw{i}" for i in range(CK)), "gate_lo", "gate_hi", "gate_t")
    add(*(f"out{m}" for m in range(DK)), "h1_sum", "wdad", "gd", "qm0", "hs8", "qm1", "hs9")
    single = 0
    for u in range(MUNITS + 1):
        if u < MUNITS:
            o.append((f"e{u}", 1, single % 6))
            single += 1
        if u:
            o.append((f"et{u - 1}", 1, single % 6))
            single += 1
            if (u - 1) % 8 == 0:
                o.append((f"mo{(u - 1) // 8}", 1, 6 + (u - 1) // 8))
    add(*(f"{x}_0" for x in "krvwA"))
    for p in range(NP):
        add(f"kks_{p}", f"bon_{p}")
        if p + 1 < NP:
            add(*(f"{x}_{p + 1}" for x in "krvwA"))
        for x in ("nt", "nn", "mak", "mrb", "mrk", "ta", "tb", "tk", "tv"):
            add(*(f"{x}_{p}_{g}" for g in range(NG)))
        for b in LEVELS:
            add(*(f"xp{b}_{p}_{g}" for g in range(NG)))
            for g in range(NG):
                if b != LEVELS[-1]:
                    add(f"xn{b}_{p}_{g}")
                add(f"xt{b}_{p}_{g}")
        for x in ("mv", "w", "u", "gt", "rp", "f"):
            add(*(f"{x}_{p}_{g}" for g in range(NG)))
        for g in range(NG):
            add(*(f"h_{p}_{g}_{c}" for c in range(G) if g * G + c < NC - 1), f"y_{p}_{g}")
        add(f"gm_{p}", f"gv_{p}", f"gg_{p}")
    add(*(f"mix{m}" for m in range(DK)), "h2_sum")
    add(*(f"up{m}" for m in range(FF)), *(f"down{m}" for m in range(DK)))
    return o


def psum_plan():
    last, count, at, plan = [None] * 8, [0] * 8, 0, {}
    for name, n, pinned in psum_order():
        here = at % 8 if pinned is None else pinned
        count[here] += 1
        before = []
        for b in range(here, here + n):
            if last[b] is not None and last[b] not in before:
                before.append(last[b])
            last[b] = name
        assert name not in plan, name
        plan[name] = (here, n, count[here], before)
        at = here + n
    return plan


def last_product(block):
    for g in ("shift", "scale", "gate"):
        if block.startswith(g):
            return None
    return {"vmem0": "vmem", "vmem1": "vmem", "k": "kc", "v": "v_hi", "pw0": "pw1",
            "pw1": "pw3"}.get(block, block.split("_")[0] if block.startswith("down") else block)


def build(nc, small, tables, xT, ctxT, memT, weights, outT):
    plan = psum_plan()
    with ExitStack() as ctx:
        def sb(name, *shape):
            return ctx.enter_context(nc.sbuf_tensor(name, list(shape), F32))

        def sem(name):
            return ctx.enter_context(nc.semaphore(name))

        ring = sb("ring", P, RING, D)
        X = sb("residual", P, DK, S)
        U = sb("normed", P, DK, S)
        CAT = sb("mixed", P, DK, S)
        TB = sb("tables_sb", P, NTAB)
        SV = sb("small_sb", P, NSMALL)
        KMEM = sb("kmem", P, 2, SM)
        VMEM = sb("vmem", P, MT, SM)
        SG = sb("sigmoids", P, 2, S)
        HS = sb("head_squares", P, 2, S)
        HR = sb("head_rstd", P, 2, S)
        RS = sb("rstd", P, 2, S)
        QW = sb("weighted", P, S)
        T12 = sb("t1_t2", P, 2, S)
        T1, T2 = T12[:, 0, :], T12[:, 1, :]
        MODROW = T12[:].rearrange("p a b -> p (a b)")
        MOD = sb("mod_cols", P, 3, DK, 2)
        SMALLT = sb("small_temps", P, 256)
        WORKW = 22656
        work = sb("work", P, WORKW)
        psum = ctx.enter_context(nc.psum_tensor("psum", [P, 8 * S], F32))

        def region(at, *shape):
            n = int(np.prod(shape))
            v = work[:, at:at + n]
            assert at + n <= WORKW
            if len(shape) == 2:
                return v.rearrange("p (a b) -> p a b", a=shape[0])
            if len(shape) == 3:
                return v.rearrange("p (a b c) -> p a b c", a=shape[0], b=shape[1])
            return v

        SQ = region(0, DK, S)
        CV = region(4 * S, CK, S)
        MEM = region(8 * S, DK, SM)
        CTX = region(12 * S, DK, SC)
        PR = region(8 * S, 2, SKEYS)
        PT = region(8 * S + 2 * SKEYS, 2, SKEYS)
        at = 16 * S
        GLU = region(at, CK, S + 2 * PAD); at += CK * (S + 2 * PAD)
        QZ = region(at, 2, NQ, S); at += 2 * NQ * S
        KTT = region(at, SKEYS); at += SKEYS
        VT = region(at, KT, P); at += SKEYS
        ZC = region(at, CK, S); at += CK * S
        ZA = region(at, NQ, S); at += NQ * S
        at = 0
        ABD, BBD, KBD, RBD, VBD = (region(i * NC * P, NC, P) for i in range(5)); at += 5 * NC * P
        K0, R0, V0, LG, EL, AV, KKN, BV = (region(at + i * S, S) for i in range(8)); at += 8 * S
        TZ = region(at, 2, S); at += 2 * S
        SGD = region(at, S); at += S
        H = region(at, G + 1, P); at += (G + 1) * P
        half = at
        HB = [[region(half + (g * 11 + i) * G * P, G, P) for i in range(11)] for g in range(NG)]
        NT, MAK, MRB, MRK, TA, TBT, TK, TV, XN, XT, XP = (
            [HB[g][i] for g in range(NG)] for i in range(11))
        MV, WB, UB, FB, GT, RP = XP, NT, XN, XT, MAK, TA
        QMZ = region(half, 2, 2, S)
        MPR = region(half + 4 * S, 2, SM)
        MPT = region(half + 5 * S, 2, SM)
        FU = region(0, FF, S)

        def col(name, i=0, rows=slice(0, P)):
            return SV[rows, AT[name] + i:AT[name] + i + 1]

        def cols(name, i, n):
            return SV[:, AT[name] + i:AT[name] + i + n]

        def tab(name):
            return TB[:, TAT[name][0]:TAT[name][0] + TAT[name][1]]

        def tab4(name):
            return tab(name)[:, None, :].to_broadcast([P, G, P])

        NEG = SMALLT[:, 0:12]
        KA1 = SMALLT[:, 12:18]
        MU1 = SMALLT[:, 18:38]
        SILU_C = SMALLT[:, 38:54].rearrange("p (k w) -> p k w", k=DK)
        SILU_E = SMALLT[:, 54:70]
        ROWMAX = SMALLT[:, 72:74]
        NEGMAX = SMALLT[:, 80:82]
        ROWSUM = SMALLT[:, 82:84]
        ROWINV = SMALLT[:, 84:86]
        ELC = SMALLT[:, 96:96 + NC]

        full = [sem(f"psum_full{b}") for b in range(8)]
        free = [sem(f"psum_free{b}") for b in range(8)]
        slot = [sem(f"slot_loaded{i}") for i in range(RING)]
        tables_in, small_in, mem_in, x_in, ctx_in = map(
            sem, ("tables_in", "small_in", "mem_in", "x_in", "ctx_in"))
        mod_block_used = sem("mod_block_used")
        squares, rstd, normed = sem("squares_ready"), sem("rstd_ready"), sem("normed_ready")
        c_exp, c_den, c_sig, c_ready = map(sem, ("c_exp", "c_den", "c_sigmoid", "c_silu_ready"))
        mod_ready = sem("modulation_ready")
        consts_ready = sem("derived_columns_ready")
        sig_exp, sig_den, sig_out = map(sem, ("sigmoid_exp", "sigmoid_denominator", "sigmoid_ready"))
        head_sq, head_rs = sem("head_squares_ready"), sem("head_rstd_ready")
        q_ready, k_ready = sem("q_ready"), sem("k_ready")
        zeroed = sem("zeroed")
        negmax, probs_scaled, pt_used = sem("negmax_ready"), sem("probs_scaled"), sem("row_sums")
        conv_out, conv_sq, conv_rs, conv_ln, conv_act = map(
            sem, ("conv_out", "conv_squares", "conv_rstd", "conv_normed", "conv_act"))
        partial = sem("shift_partial")
        low_used = sem("tanh_placed")
        scan_done, exps_done = sem("log_decays_ready"), sem("decays_ready")
        kk_sq, kk_rs, bonus_in = sem("kk_squares"), sem("kk_rstd"), sem("bonus_in")
        bd_ready, v_ready = sem("bd_ready"), sem("v_blocks_ready")
        x_first, h_first = sem("inverse_started"), sem("state_placed")
        gn_sq, gn_rs = sem("gn_squares"), sem("gn_rstd")
        hidden = sem("hidden_ready")
        out_stored = sem("out_stored")
        act_step, vec_step = sem("act_step"), sem("vec_step")

        def bank(name, w=None, rows=slice(0, P)):
            b, n, _, _ = plan[name]
            return psum[rows, b * S:b * S + (w or n * S)]

        def bank4(name):
            return bank(name).rearrange("p (g t) -> p g t", g=G)

        def is_full(name):
            return full[plan[name][0]], plan[name][2]

        def is_free(name):
            return free[plan[name][0]], plan[name][2]

        def full_inc(ins, name):
            ins.then_inc(full[plan[name][0]], 1)

        def free_inc(ins, name):
            ins.then_inc(free[plan[name][0]], 1)

        sigmoids = ([(f"g{i}", True, is_free(f"a{i}")) for i in range(CK)]
                    + [(f"zc{i}", False, is_free(f"zc{i}")) for i in range(CK)]
                    + [(f"za{j}", False, is_free(f"za{j}")) for j in range(NQ)]
                    + [(f"conv{i}", False, (conv_act, i + 1)) for i in range(CK)]
                    + [("wd", False, (low_used, 1)), ("gd_sig", False, None)]
                    + [(f"{x}_{p}", True, None) for p in range(NP) for x in "wA"])
        sig_at, kept = {}, 0
        for n, (name, frees, _) in enumerate(sigmoids):
            kept += not frees
            sig_at[name] = (n, is_free(name) if frees else (sig_exp, kept))
        heads = ([("kmem0", is_free("kmem0")), ("kmem1", is_free("kmem1")), ("kx", (k_ready, 1)),
                  ("kc", is_free("kc"))] + [(f"q{j}", (q_ready, j + 1)) for j in range(NQ)]
                 + [("qm0", is_free("qm0")), ("qm1", is_free("qm1"))])
        head_at = {name: n for n, (name, _) in enumerate(heads)}

        block = ctx.enter_context(nc.Block())

        @block.sync
        def _(sp):
            sp.dma_start(TB[:], tables).then_inc(tables_in, 16)
            sp.dma_start(MEM, memT).then_inc(mem_in, 16)
            sp.dma_start(SV[:], small).then_inc(small_in, 16)
            sp.dma_start(CTX, ctxT).then_inc(ctx_in, 16)
            mod_seen = 0
            for b, name in enumerate(BLOCKS):
                if b == 2:
                    sp.dma_start(X[:], xT).then_inc(x_in, 16)
                if b >= RING:
                    before = last_product(BLOCKS[b - RING])
                    if before is None:
                        mod_seen += 1
                        sp.wait_ge(mod_block_used, mod_seen)
                    else:
                        sp.wait_ge(*is_full(before))
                sp.dma_start(ring[:, b % RING, :], weights[b]).then_inc(slot[b % RING], 16)
            for m in range(DK):
                sp.wait_ge(*is_free(f"down{m}"))
                sp.dma_start(outT[:, m, :], X[:, m, :]).then_inc(out_stored, 16)
            sp.wait_ge(out_stored, 16 * DK)

        @block.gpsimd
        def _(pool):
            pool.memset(GLU, 0.0).then_inc(zeroed, 1)
            pool.memset(QZ, 0.0).then_inc(zeroed, 1)
            pool.wait_ge(*is_free(f"out{DK - 1}"))
            pool.memset(TZ, 0.0).then_inc(zeroed, 1)
            pool.memset(QMZ, 0.0).then_inc(zeroed, 1)
            pool.wait_ge(*is_full("h1_sum"))
            for z in (ABD, BBD, KBD, RBD, VBD):
                pool.memset(z, 0.0).then_inc(zeroed, 1)

        @block.tensor
        def _(pe):
            order = iter(psum_order())

            def take(name, w=None, rows=slice(0, P)):
                assert next(order)[0] == name, name
                for before in plan[name][3]:
                    pe.wait_ge(*is_free(before))
                return bank(name, w, rows)

            def loaded(name):
                b = BLOCK_AT[name]
                pe.wait_ge(slot[b % RING], 16 * (b // RING + 1))
                return ring[:, b % RING, :]

            def sum_over(name, src, n, w):
                out = take(name, w)
                for k in range(n):
                    last = pe.matmul(out, tab("ones"), src(k), start=k == 0, stop=k == n - 1)
                full_inc(last, name)

            def project(block_name, name, src, w=S):
                wt = loaded(block_name)
                out = take(name, w)
                for k in range(DK):
                    last = pe.matmul(out, wt[:, k * P:(k + 1) * P], src(k), start=k == 0, stop=k == DK - 1)
                full_inc(last, name)

            def one(name, stationary, moving, w=S):
                full_inc(pe.matmul(take(name, w), stationary, moving, start=True, stop=True), name)

            def head_sums(n, w=S):
                pe.wait_ge(head_sq, n + 1)
                one(f"hs{n}", tab("heads"), HS[:, n % 2, 0:w], w)

            def rotate(n, name):
                pe.wait_ge(*is_free(name))
                one(f"rot{n}", tab("rot"), QW[:])

            def modulation(g):
                lo, hi = take(f"{g}_lo", rows=slice(0, 2)), take(f"{g}_hi", rows=slice(0, 2))
                for k in range(DK):
                    wt = loaded(f"{g}{k}")
                    a = pe.matmul(lo, SILU_C[:, k, :], wt[:, 0:S], start=k == 0, stop=k == DK - 1)
                    b = pe.matmul(hi, SILU_C[:, k, :], wt[:, S:D], start=k == 0, stop=k == DK - 1)
                    if k < DK - 1:
                        b.then_inc(mod_block_used, 1)
                full_inc(a, f"{g}_lo")
                full_inc(b, f"{g}_hi")
                pe.wait_ge(*is_free(f"{g}_lo"))
                pe.wait_ge(*is_free(f"{g}_hi"))
                out = take(f"{g}_t", 2 * DK)
                for k in range(DK):
                    last = pe.transpose(out[:, 2 * k:2 * k + 2], MODROW[0:2, k * P:(k + 1) * P],
                                        tab("ident")[0:2, 0:2])
                    if k == 0:
                        last.then_inc(mod_block_used, 1)
                full_inc(last, f"{g}_t")

            pe.wait_ge(tables_in, 16)
            pe.wait_ge(squares, 1)
            sum_over("mem_sum", lambda k: SQ[:, k, 0:SM], DK, SM)
            pe.wait_ge(squares, 2)
            sum_over("ctx_sum", lambda k: SQ[:, k, SM:SM + SC], DK, SC)
            pe.wait_ge(squares, 3)
            sum_over("x_sum", lambda k: SQ[:, k, :], DK, S)
            pe.wait_ge(normed, 1)
            for i in range(2):
                project(f"kmem{i}", f"kmem{i}", lambda k: MEM[:, k, :], SM)
            head_sums(0, SM)
            head_sums(1, SM)
            out = take("vmem")
            wts = [loaded("vmem0"), loaded("vmem1")]
            for t in range(MT):
                for k in range(DK):
                    last = pe.matmul(out[:, t * SM:(t + 1) * SM], MEM[:, k, t * P:(t + 1) * P],
                                     wts[k // 4][:, (k % 4) * SM:(k % 4 + 1) * SM],
                                     start=k == 0, stop=k == DK - 1)
            full_inc(last, "vmem")
            pe.wait_ge(c_ready, 1)
            modulation("shift")
            modulation("scale")
            pe.wait_ge(normed, 2)
            for i in range(CK):
                project(f"a{i}", f"a{i}", lambda k: U[:, k, :])
                project(f"g{i}", f"g{i}", lambda k: U[:, k, :])
            project("k", "kx", lambda k: U[:, k, :])
            project("k", "kc", lambda k: CTX[:, k, :], SC)
            head_sums(2)
            rotate(0, "kx")
            head_sums(3, SC)
            wt = loaded("v")
            for name, tiles in (("v_lo", range(4)), ("v_hi", range(4, KT))):
                out = take(name, len(tiles) * P)
                for n, t in enumerate(tiles):
                    for k in range(DK):
                        src = (CTX[:, k, t * P:(t + 1) * P] if t < SC // P
                               else U[:, k, (t - SC // P) * P:(t - SC // P + 1) * P])
                        last = pe.matmul(out[:, n * P:(n + 1) * P], src, wt[:, k * P:(k + 1) * P],
                                         start=k == 0, stop=k == DK - 1)
                full_inc(last, name)
            for j in range(NQ):
                project(f"q{j}", f"q{j}", lambda k: U[:, k, :])
                head_sums(4 + j)
                rotate(1 + j, f"q{j}")
            for i in range(CK):
                project(f"zc{i}", f"zc{i}", lambda k: U[:, k, :])
            for j in range(NQ):
                project(f"za{j}", f"za{j}", lambda k: U[:, k, :])

            def turn(name, tiles, src):
                out = take(name, tiles * P)
                for t in range(tiles):
                    last = pe.transpose(out[:, t * P:(t + 1) * P], src[:, t * P:(t + 1) * P], tab("ident"))
                full_inc(last, name)

            pe.wait_ge(k_ready, 1)
            pe.wait_ge(*is_free("kc"))
            pe.wait_ge(*is_free("v_hi"))
            for u in range(UNITS + 1):
                if u < UNITS:
                    j, h, qt = u // 8, u // 4 % 2, u % 4
                    pe.wait_ge(q_ready, j + 1)
                    s = take(f"s{u}")
                    q = QZ[:, h, j, qt * P:(qt + 1) * P]
                    pe.matmul(s[:, 0:S], q, KTT[:, 0:S], start=True, stop=True)
                    full_inc(pe.matmul(s[:, S:SKEYS], q, KTT[:, S:SKEYS], start=True, stop=True), f"s{u}")
                if u:
                    v = u - 1
                    j, h, qt = v // 8, v // 4 % 2, v % 4
                    pe.wait_ge(probs_scaled, v + 1)
                    turn(f"pt{v}", KT, PR[:, v % 2, :])
                    if v % 8 == 0:
                        o = take(f"o{j}")
                    pe.wait_ge(*is_free(f"pt{v}"))
                    for t in range(KT):
                        last = pe.matmul(o[h * DH:(h + 1) * DH, qt * P:(qt + 1) * P],
                                         VT[:, t, h * DH:(h + 1) * DH],
                                         PT[:, v % 2, t * P:(t + 1) * P], start=t == 0, stop=t == KT - 1)
                    if v % 8 == 7:
                        full_inc(last, f"o{j}")
            pe.wait_ge(conv_out, CK)
            sum_over("cmean", lambda k: CV[:, k, :], CK, S)
            pe.wait_ge(conv_sq, 1)
            sum_over("cvar", lambda k: SQ[:, k, :], CK, S)
            pe.wait_ge(conv_act, CK)
            for i in range(CK):
                wt = loaded(f"pw{i // 2}")
                out = take(f"pw{i}")
                for k in range(CK):
                    at = (i % 2 * CK + k) * P
                    last = pe.matmul(out, wt[:, at:at + P], CV[:, k, :], start=k == 0, stop=k == CK - 1)
                full_inc(last, f"pw{i}")
            modulation("gate")
            pe.wait_ge(*is_free(f"o{NQ - 1}"))
            pe.wait_ge(*is_free(f"pw{CK - 1}"))
            for m in range(DK):
                project(f"out{m}", f"out{m}", lambda k: CAT[:, k, :])

            pe.wait_ge(squares, 4)
            sum_over("h1_sum", lambda k: SQ[:, k, :], DK, S)
            pe.wait_ge(normed, 3)
            project("wdad", "wdad", lambda k: U[:, k, :])
            project("gd", "gd", lambda k: U[:, k, :])
            for i in range(2):
                project(f"qm{i}", f"qm{i}", lambda k: U[:, k, :])
                head_sums(8 + i)
            pe.wait_ge(*is_free("kmem1"))
            pe.wait_ge(*is_free("vmem"))
            for u in range(MUNITS + 1):
                if u < MUNITS:
                    j, h, qt = u // 8, u // 4 % 2, u % 4
                    pe.wait_ge(*is_free(f"qm{j}"))
                    one(f"e{u}", QMZ[:, h, j, qt * P:(qt + 1) * P], KMEM[:, j, :], SM)
                if u:
                    v = u - 1
                    j, h, qt = v // 8, v // 4 % 2, v % 4
                    pe.wait_ge(probs_scaled, UNITS + v + 1)
                    turn(f"et{v}", MT, MPR[:, v % 2, :])
                    if v % 8 == 0:
                        o = take(f"mo{j}")
                    pe.wait_ge(*is_free(f"et{v}"))
                    for t in range(MT):
                        last = pe.matmul(o[h * DH:(h + 1) * DH, qt * P:(qt + 1) * P],
                                         VMEM[:, t, (2 * j + h) * DH:(2 * j + h + 1) * DH],
                                         MPT[:, v % 2, t * P:(t + 1) * P], start=t == 0, stop=t == MT - 1)
                    if v % 8 == 7:
                        full_inc(last, f"mo{j}")

            def pair_projections(p):
                for x in "krv":
                    project(f"{x}_{p}", f"{x}_{p}", lambda k: U[:, k, :])
                pe.wait_ge(low_used, 1)
                for x, src in (("w", TZ[:, 0, :]), ("A", TZ[:, 1, :])):
                    one(f"{x}_{p}", SV[:, LORA_AT + p * P:LORA_AT + (p + 1) * P], src)

            def four(name, *terms):
                out = take(name).rearrange("p (g t) -> p g t", g=G)
                for c in range(G):
                    for n, (stationary, moving) in enumerate(terms):
                        last = pe.matmul(out[:, c, :], stationary[:, c, :], moving[:, c, :],
                                         start=n == 0, stop=n == len(terms) - 1)
                full_inc(last, name)

            def part(x, g):
                return x[:, g * G:(g + 1) * G, :]

            pair_projections(0)
            for p in range(NP):
                pe.wait_ge(kk_sq, p + 1)
                one(f"kks_{p}", tab("heads"), HS[:, 0, :])
                pe.wait_ge(bonus_in, p + 1)
                one(f"bon_{p}", tab("heads"), T2)
                if p + 1 < NP:
                    pair_projections(p + 1)
                pe.wait_ge(bd_ready, p + 1)
                for x, a, b in (("nt", BBD, ABD), ("nn", ABD, BBD), ("mak", KBD, ABD), ("mrb", BBD, RBD),
                                ("mrk", KBD, RBD)):
                    for g in range(NG):
                        four(f"{x}_{p}_{g}", (part(a, g), part(b, g)))
                for x, a in (("ta", ABD), ("tb", BBD), ("tk", KBD), ("tv", VBD)):
                    if x == "tv":
                        pe.wait_ge(v_ready, p + 1)
                    for g in range(NG):
                        out = take(f"{x}_{p}_{g}").rearrange("p (g t) -> p g t", g=G)
                        for c in range(G):
                            last = pe.transpose(out[:, c, :], a[:, g * G + c, :], tab("ident"))
                        full_inc(last, f"{x}_{p}_{g}")
                prev = None
                for b in LEVELS:
                    for g in range(NG):
                        if prev is None:
                            pe.wait_ge(x_first, NG * p + g + 1)
                        else:
                            pe.wait_ge(*is_free(f"xt{prev}_{p}_{g}"))
                        four(f"xp{b}_{p}_{g}", (NT[g], XN[g]))
                    for g in range(NG):
                        pe.wait_ge(*is_free(f"xp{b}_{p}_{g}"))
                        if b != LEVELS[-1]:
                            four(f"xn{b}_{p}_{g}", (XT[g], XP[g]))
                        four(f"xt{b}_{p}_{g}", (XP[g], XT[g]))
                    prev = b
                for g in range(NG):
                    pe.wait_ge(*is_free(f"mak_{p}_{g}"))
                    pe.wait_ge(*is_free(f"tv_{p}_{g}"))
                    four(f"mv_{p}_{g}", (MAK[g], TV[g]))
                for g in range(NG):
                    pe.wait_ge(*is_free(f"xt{prev}_{p}_{g}"))
                    pe.wait_ge(*is_free(f"ta_{p}_{g}"))
                    four(f"w_{p}_{g}", (XT[g], TA[g]))
                for g in range(NG):
                    pe.wait_ge(*is_free(f"mv_{p}_{g}"))
                    four(f"u_{p}_{g}", (XT[g], MV[g]))
                for g in range(NG):
                    pe.wait_ge(*is_free(f"w_{p}_{g}"))
                    pe.wait_ge(*is_free(f"tb_{p}_{g}"))
                    four(f"gt_{p}_{g}", (WB[g], TBT[g]))
                for g in range(NG):
                    pe.wait_ge(*is_free(f"mrb_{p}_{g}"))
                    four(f"rp_{p}_{g}", (WB[g], MRB[g]))
                for g in range(NG):
                    pe.wait_ge(*is_free(f"u_{p}_{g}"))
                    pe.wait_ge(*is_free(f"tk_{p}_{g}"))
                    four(f"f_{p}_{g}", (TBT[g], UB[g]), (TK[g], TV[g]))
                for g in range(NG):
                    for c in range(G):
                        if c == 0:
                            pe.wait_ge(h_first, NG * p + g + 1)
                            pe.wait_ge(*is_free(f"gt_{p}_{g}"))
                        else:
                            pe.wait_ge(*is_free(f"h_{p}_{g}_{c - 1}"))
                        if g * G + c < NC - 1:
                            one(f"h_{p}_{g}_{c}", GT[g][:, c, :], H[:, c, :], P)
                    pe.wait_ge(*is_free(f"rp_{p}_{g}"))
                    pe.wait_ge(*is_free(f"mrk_{p}_{g}"))
                    four(f"y_{p}_{g}", (H, RP[g]), (UB[g], MRB[g]), (TV[g], MRK[g]))
                pe.wait_ge(*is_free(f"y_{p}_{NG - 1}"))
                one(f"gm_{p}", tab("heads"), CAT[:, p, :])
                pe.wait_ge(gn_sq, p + 1)
                one(f"gv_{p}", tab("heads"), HS[:, 1, :])
                pe.wait_ge(sig_out, sig_at["gd_sig"][0] + 1)
                one(f"gg_{p}", SV[:, G2_AT + p * P:G2_AT + (p + 1) * P], SGD)
            pe.wait_ge(*is_free(f"gg_{NP - 1}"))
            pe.wait_ge(*is_free("mo0"))
            pe.wait_ge(*is_free("mo1"))
            for m in range(DK):
                project(f"mix{m}", f"mix{m}", lambda k: CAT[:, k, :])
            pe.wait_ge(squares, 5)
            sum_over("h2_sum", lambda k: SQ[:, k, :], DK, S)
            pe.wait_ge(normed, 4)
            for m in range(FF):
                project(f"up{m}", f"up{m}", lambda k: U[:, k, :])
            for m in range(DK):
                out = take(f"down{m}")
                for kb in range(FF // DK):
                    wt = loaded(f"down{m}_{kb}")
                    if m == 0:
                        pe.wait_ge(hidden, (kb + 1) * DK)
                    for k in range(DK):
                        t = kb * DK + k
                        last = pe.matmul(out, wt[:, k * P:(k + 1) * P], FU[:, t, :], start=t == 0, stop=t == FF - 1)
                full_inc(last, f"down{m}")

        @block.scalar
        def _(act):
            steps = [0]

            def link(ins):
                steps[0] += 1
                ins.then_inc(act_step, 1)
                act.wait_ge(act_step, steps[0])

            def rms(name, out, w, scale, eps, done):
                act.wait_ge(*is_full(name))
                free_inc(act.activation(out, bank(name, w), ACT.Ln, bias=eps, scale=scale), name)
                act.wait_ge(*is_free(name))
                act.activation(out, out, ACT.Exp, scale=-0.5).then_inc(done, 1)

            def sigmoid(name, src, out=None, bias=0.0, scale=-1.0, rows=slice(0, P)):
                n, exp_done = sig_at[name]
                e = SG[rows, n % 2, :]
                if n >= 2 and sigmoids[n - 2][2] is not None:
                    act.wait_ge(*sigmoids[n - 2][2])
                act.activation(e, src, ACT.Exp, bias=bias, scale=scale).then_inc(exp_done[0], 1)
                act.wait_ge(sig_den, n + 1)
                link(act.activation(e, e, ACT.Ln))
                act.activation(e if out is None else out, e, ACT.Exp, scale=-1.0).then_inc(sig_out, 1)

            def head_norm(name, w=S, weight=None, rot_before=None):
                n = head_at[name]
                act.wait_ge(*is_full(name))
                act.activation(HS[:, n % 2, 0:w], bank(name, w), ACT.Square).then_inc(head_sq, 1)
                if weight is not None:
                    if rot_before is not None:
                        act.wait_ge(*is_free(rot_before))
                    free_inc(act.activation(QW[:, 0:w], bank(name, w), ACT.Copy, scale=weight), name)
                if n >= 2:
                    act.wait_ge(*heads[n - 2][1])
                rms(f"hs{n}", HR[:, n % 2, 0:w], w, 1.0 / DH, EPS, head_rs)

            def copy_out(name, out, w=None, before=None):
                act.wait_ge(*is_full(name))
                free_inc(act.activation(out, bank(name, w) if len(out.shape) == 2 else bank4(name), ACT.Copy), name)

            act.preload_act_table_set("natural_log_exp_and_others")
            act.wait_ge(mem_in, 16)
            act.activation(SQ[:, :, 0:SM], MEM, ACT.Square).then_inc(squares, 1)
            act.wait_ge(ctx_in, 16)
            act.activation(SQ[:, :, SM:SM + SC], CTX, ACT.Square).then_inc(squares, 1)
            rms("mem_sum", RS[:, 0, 0:SM], SM, 1.0 / D, EPS, rstd)
            rms("ctx_sum", RS[:, 1, 0:SC], SC, 1.0 / D, EPS, rstd)
            act.wait_ge(x_in, 16)
            act.activation(SQ, X[:], ACT.Square).then_inc(squares, 1)
            act.wait_ge(normed, 1)
            rms("x_sum", RS[:, 0, :], S, 1.0 / D, EPS, rstd)
            act.wait_ge(small_in, 16)
            act.activation(SILU_E, cols("cc", 0, 2 * DK), ACT.Exp, scale=-1.0).then_inc(c_exp, 1)
            act.wait_ge(c_den, 1)
            link(act.activation(SILU_E, SILU_E, ACT.Ln))
            act.activation(SILU_E, SILU_E, ACT.Exp, scale=-1.0).then_inc(c_sig, 1)
            head_norm("kmem0", SM)
            head_norm("kmem1", SM)
            copy_out("vmem", VMEM[:].rearrange("p a b -> p (a b)"))

            def modulation_rows(g, turned=None):
                if turned:
                    act.wait_ge(*is_full(turned))
                for i, h in enumerate(("lo", "hi")):
                    act.wait_ge(*is_full(f"{g}_{h}"))
                    free_inc(act.activation(MODROW[0:2, i * S:(i + 1) * S], bank(f"{g}_{h}", S, slice(0, 2)),
                                            ACT.Copy), f"{g}_{h}")

            modulation_rows("shift")
            modulation_rows("scale", "shift_t")
            for i in range(CK):
                act.wait_ge(*is_full(f"g{i}"))
                sigmoid(f"g{i}", bank(f"g{i}"))
            head_norm("kx", weight=col("kn"))
            head_norm("kc", SC)
            flat = VT.rearrange("p a b -> p (a b)")
            copy_out("v_lo", flat[:, 0:4 * P], 4 * P)
            copy_out("v_hi", flat[:, 4 * P:SKEYS], SKEYS - 4 * P)
            for j in range(NQ):
                head_norm(f"q{j}", weight=col("qn"), rot_before=f"rot{j}")
            for name in [f"zc{i}" for i in range(CK)] + [f"za{j}" for j in range(NQ)]:
                act.wait_ge(*is_full(name))
                sigmoid(name, bank(name))

            def attention(units, base, s_name, t_name, probs, turned, w):
                for u in range(units + 1):
                    if u < units:
                        act.wait_ge(negmax, base + u + 1)
                        if u >= 2:
                            act.wait_ge(*is_full(f"{t_name}{u - 2}"))
                        ins = act.activation(probs[:, u % 2, :], bank(f"{s_name}{u}", w), ACT.Exp,
                                             bias=NEGMAX[:, u % 2:u % 2 + 1], scale=DH ** -0.5,
                                             accum_out=ROWSUM[:, u % 2:u % 2 + 1])
                        free_inc(ins, f"{s_name}{u}")
                    if u:
                        copy_out(f"{t_name}{u - 1}", turned[:, (u - 1) % 2, :], w)

            attention(UNITS, 0, "s", "pt", PR, PT, SKEYS)
            act.wait_ge(*is_free("cmean"))
            act.activation(SQ[:, 0:CK, :], CV, ACT.Square).then_inc(conv_sq, 1)
            rms("cvar", RS[:, 1, :], S, 1.0 / (CK * P), EPS, conv_rs)
            for i in range(CK):
                act.wait_ge(conv_ln, i + 1)
                sigmoid(f"conv{i}", CV[:, i, :])
            modulation_rows("gate", "scale_t")

            def square_residual(kind):
                for m in range(DK):
                    act.wait_ge(*is_free(f"{kind}{m}"))
                    ins = act.activation(SQ[:, m, :], X[:, m, :], ACT.Square)
                ins.then_inc(squares, 1)

            square_residual("out")
            rms("h1_sum", RS[:, 0, :], S, 1.0 / D, EPS, rstd)

            def shift_start(name, n, out):
                act.wait_ge(*is_full(name))
                act.activation(out, bank(name), ACT.Copy, scale=MU1[:, n:n + 1]).then_inc(partial, 1)

            act.wait_ge(consts_ready, 1)
            shift_start("wdad", MU_WDAD, T1)
            shift_start("gd", MU_GD, T2)
            act.wait_ge(*is_free("wdad"))
            sigmoid("wd", T1[0:DH, :], scale=-2.0, rows=slice(0, DH))
            act.wait_ge(*is_free("gd"))
            sigmoid("gd_sig", T2, out=SGD)
            head_norm("qm0")
            head_norm("qm1")
            attention(MUNITS, UNITS, "e", "et", MPR, MPT, SM)

            def pair_inputs(p):
                if p:
                    act.wait_ge(bd_ready, p)
                    act.wait_ge(v_ready, p)
                for i, (x, out) in enumerate((("k", K0), ("r", R0), ("v", V0))):
                    shift_start(f"{x}_{p}", MU_PAIR + 3 * p + i, out)
                for i, (x, out) in enumerate((("w", EL), ("A", AV))):
                    act.wait_ge(*is_full(f"{x}_{p}"))
                    sigmoid(f"{x}_{p}", bank(f"{x}_{p}"), out=out, bias=NEG[:, i * NP + p:i * NP + p + 1])

            pair_inputs(0)
            for p in range(NP):
                act.wait_ge(*is_free(f"k_{p}"))
                act.activation(HS[:, 0, :], K0, ACT.Square, scale=col("k_k", p)).then_inc(kk_sq, 1)
                act.wait_ge(scan_done, p + 1)
                act.activation(T1, T1, ACT.Exp, scale=-DECAY)
                link(act.activation(EL, LG, ACT.Exp, scale=-DECAY))
                act.activation(LG, LG, ACT.Exp, scale=DECAY).then_inc(exps_done, 1)
                act.wait_ge(*is_free(f"kks_{p}"))
                link(act.activation(HR[:, 0, :], HR[:, 0, :], ACT.Ln, scale=KK_SCALE))
                act.activation(HR[:, 0, :], HR[:, 0, :], ACT.Exp, scale=-0.5,
                               bias=float(0.5 * np.log(KK_SCALE))).then_inc(kk_rs, 1)
                act.wait_ge(*is_free(f"v_{p}"))
                if p:
                    act.wait_ge(*is_full(f"tv_{p - 1}_{NG - 1}"))
                else:
                    act.wait_ge(zeroed, 9)
                v3 = V0.rearrange("p (c t) -> p c t", c=NC)
                act.activation(VBD[0:DH, :, 0:DH], v3[0:DH], ACT.Copy)
                act.activation(VBD[DH:P, :, DH:P], v3[DH:P], ACT.Copy).then_inc(v_ready, 1)
                if p + 1 < NP:
                    pair_inputs(p + 1)
                for x, out in (("ta", TA), ("tb", TBT), ("tk", TK), ("tv", TV), ("mv", MV), ("w", WB), ("u", UB)):
                    for g in range(NG):
                        copy_out(f"{x}_{p}_{g}", out[g])
                act.wait_ge(*is_free(f"gm_{p}"))
                act.activation(HS[:, 1, :], CAT[:, p, :], ACT.Square).then_inc(gn_sq, 1)
                rms(f"gv_{p}", HR[:, 1, :], S, 1.0 / DH, GN_EPS, gn_rs)
            square_residual("mix")
            rms("h2_sum", RS[:, 1, :], S, 1.0 / D, EPS, rstd)
            for m in range(FF):
                act.wait_ge(*is_full(f"up{m}"))
                free_inc(act.activation(FU[:, m, :], bank(f"up{m}"), ACT.Relu), f"up{m}")
                act.wait_ge(*is_free(f"up{m}"))
                act.activation(FU[:, m, :], FU[:, m, :], ACT.Square).then_inc(hidden, 1)

        @block.vector
        def _(vec):
            steps = [0]

            def link(ins):
                steps[0] += 1
                ins.then_inc(vec_step, 1)
                vec.wait_ge(vec_step, steps[0])

            def scaled_product(out, a, scalar, b, op=ALU.mult):
                return vec.scalar_tensor_tensor(out=out, in0=a, scalar=scalar, in1=b, op0=op, op1=ALU.mult)

            def scaled_sum(out, a, scalar, b, op=ALU.mult):
                return vec.scalar_tensor_tensor(out=out, in0=a, scalar=scalar, in1=b, op0=op, op1=ALU.add)

            def denominator(name, rows=slice(0, P)):
                n, exp_done = sig_at[name]
                vec.wait_ge(*exp_done)
                e = SG[rows, n % 2, :]
                vec.tensor_scalar(e, e, SIG_MOST, 1.0, ALU.min, ALU.add).then_inc(sig_den, 1)

            def sigmoid_of(name, rows=slice(0, P)):
                n, _ = sig_at[name]
                vec.wait_ge(sig_out, n + 1)
                return SG[rows, n % 2, :]

            vec.wait_ge(small_in, 16)
            link(vec.tensor_scalar(NEG, cols("w0", 0, 2 * NP), -1.0, None, ALU.mult))
            link(vec.tensor_scalar(KA1, cols("k_a", 0, NP), -1.0, 1.0, ALU.mult, ALU.add))
            vec.tensor_scalar(MU1, cols("mu", 0, 20), -1.0, 1.0, ALU.mult, ALU.add).then_inc(consts_ready, 1)
            vec.wait_ge(rstd, 1)
            for k in range(DK):
                ins = scaled_product(MEM[:, k, :], MEM[:, k, :], col("g_mem", k), RS[:, 0, 0:SM])
            ins.then_inc(normed, 1)
            vec.wait_ge(c_exp, 1)
            vec.tensor_scalar(SILU_E, SILU_E, SIG_MOST, 1.0, ALU.min, ALU.add).then_inc(c_den, 1)
            vec.wait_ge(rstd, 2)
            for k in range(DK):
                vec.tensor_tensor(CTX[:, k, :], CTX[:, k, :], RS[:, 1, 0:SC], ALU.mult)
            vec.wait_ge(c_sig, 1)
            vec.tensor_tensor(SILU_C, cols("cc", 0, 2 * DK).rearrange("p (k w) -> p k w", k=DK),
                              SILU_E.rearrange("p (k w) -> p k w", k=DK), ALU.mult).then_inc(c_ready, 1)
            vec.wait_ge(rstd, 3)
            for k in range(DK):
                ins = vec.tensor_tensor(U[:, k, :], X[:, k, :], RS[:, 0, :], ALU.mult)
            link(ins)
            for i in range(2):
                vec.wait_ge(head_rs, i + 1)
                free_inc(scaled_product(KMEM[:, i, :], bank(f"kmem{i}", SM), col("mkn"), HR[:, i, 0:SM]), f"kmem{i}")

            def modulation_columns(g, i, bias):
                vec.wait_ge(*is_full(f"{g}_t"))
                b = cols(bias, 0, DK)[:, :, None].to_broadcast([P, DK, 2])
                free_inc(vec.tensor_tensor(MOD[:, i], bank(f"{g}_t", 2 * DK).rearrange("p (k w) -> p k w", k=DK),
                                           b, ALU.add), f"{g}_t")

            modulation_columns("shift", 0, "b_shift")
            modulation_columns("scale", 1, "b_scale")
            vec.wait_ge(*is_free("scale_t"))
            link(scaled_product(MOD[:, 1], MOD[:, 1], 1.0,
                                cols("norm_w", 0, DK)[:, :, None].to_broadcast([P, DK, 2]), ALU.add))
            for k in range(DK):
                vec.tensor_scalar(U[:, k, :], U[:, k, :], MOD[:, 1, k, 0:1], MOD[:, 0, k, 0:1], ALU.mult, ALU.add)
            for k in range(DK):
                ins = vec.tensor_scalar(CTX[:, k, :], CTX[:, k, :], MOD[:, 1, k, 1:2], MOD[:, 0, k, 1:2],
                                        ALU.mult, ALU.add)
            ins.then_inc(normed, 1)
            vec.wait_ge(zeroed, 1)
            for i in range(CK):
                denominator(f"g{i}")
                s = sigmoid_of(f"g{i}")
                vec.wait_ge(*is_full(f"a{i}"))
                free_inc(vec.tensor_tensor(GLU[:, i, PAD:PAD + S], bank(f"a{i}"), s, ALU.mult), f"a{i}")
                vec.wait_ge(*is_free(f"a{i}"))
                sums = (CV[:, i, :], T1)
                for t in range(TAPS):
                    w = col("conv_w", i * TAPS + t)
                    src = GLU[:, i, t:t + S]
                    if t >= 2:
                        vec.wait_ge(vec_step, steps[0] - 1)
                    if t == 0:
                        ins = vec.tensor_scalar(sums[0], src, w, col("conv_b", i), ALU.mult, ALU.add)
                    elif t == 1:
                        ins = vec.tensor_scalar(sums[1], src, w, None, ALU.mult)
                    else:
                        ins = scaled_sum(sums[t % 2], src, w, sums[t % 2])
                    ins.then_inc(vec_step, 1)
                    steps[0] += 1
                vec.wait_ge(vec_step, steps[0])
                vec.tensor_tensor(CV[:, i, :], CV[:, i, :], T1, ALU.add).then_inc(conv_out, 1)

            def rotary(n, rs):
                link(vec.tensor_tensor(T1, QW[:], tab("cos"), ALU.mult))
                vec.wait_ge(*is_full(f"rot{n}"))
                free_inc(vec.tensor_tensor(T2, bank(f"rot{n}"), tab("sin"), ALU.mult), f"rot{n}")
                vec.wait_ge(*is_free(f"rot{n}"))
                link(vec.tensor_tensor(T1, T1, T2, ALU.add))
                vec.wait_ge(head_rs, rs + 1)

            vec.wait_ge(conv_out, CK)
            vec.wait_ge(*is_free("kx"))
            rotary(0, 2)
            vec.tensor_tensor(KTT[:, SC:SKEYS], T1, HR[:, 0, :], ALU.mult).then_inc(k_ready, 1)
            vec.wait_ge(head_rs, 4)
            free_inc(scaled_product(KTT[:, 0:SC], bank("kc", SC), col("kn"), HR[:, 1, 0:SC]), "kc")
            vec.wait_ge(zeroed, 2)
            for j in range(NQ):
                vec.wait_ge(*((q_ready, j) if j else (k_ready, 1)))
                vec.wait_ge(*is_free(f"q{j}"))
                rotary(1 + j, 4 + j)
                vec.tensor_tensor(QZ[0:DH, 0, j, :], T1[0:DH, :], HR[0:DH, j % 2, :], ALU.mult)
                vec.tensor_tensor(QZ[DH:P, 1, j, :], T1[DH:P, :], HR[DH:P, j % 2, :], ALU.mult).then_inc(q_ready, 1)
            for z, out, n in (("zc", ZC, CK), ("za", ZA, NQ)):
                for i in range(n):
                    denominator(f"{z}{i}")
                    s = sigmoid_of(f"{z}{i}")
                    free_inc(vec.tensor_tensor(out[:, i, :], bank(f"{z}{i}"), s, ALU.mult), f"{z}{i}")

            def attention(units, s_name, probs, w, finish):
                for u in range(units + 1):
                    if u < units:
                        vec.wait_ge(*is_full(f"{s_name}{u}"))
                        link(vec.tensor_reduce(ROWMAX[:, u % 2:u % 2 + 1], bank(f"{s_name}{u}", w), AX, ALU.max))
                        vec.tensor_scalar(NEGMAX[:, u % 2:u % 2 + 1], ROWMAX[:, u % 2:u % 2 + 1], -DH ** -0.5, None,
                                          ALU.mult).then_inc(negmax, 1)
                    if u:
                        v = u - 1
                        vec.wait_ge(*is_free(f"{s_name}{v}"))
                        link(vec.reciprocal(ROWINV[:, v % 2:v % 2 + 1], ROWSUM[:, v % 2:v % 2 + 1]))
                        vec.tensor_scalar(probs[:, v % 2, :], probs[:, v % 2, :], ROWINV[:, v % 2:v % 2 + 1], None,
                                          ALU.mult).then_inc(probs_scaled, 1)
                        if v % 8 == 0 and v:
                            finish(v // 8 - 1)
                finish(units // 8 - 1)

            def gated_heads(j):
                vec.wait_ge(*is_full(f"o{j}"))
                free_inc(vec.tensor_tensor(CAT[:, j, :], bank(f"o{j}"), ZA[:, j, :], ALU.mult), f"o{j}")

            vec.wait_ge(*is_free("za3"))
            attention(UNITS, "s", PR, SKEYS, gated_heads)
            vec.wait_ge(*is_full("cmean"))
            for i in range(CK):
                ins = scaled_sum(CV[:, i, :], bank("cmean"), -1.0 / (CK * P), CV[:, i, :])
            free_inc(ins, "cmean")
            vec.wait_ge(conv_rs, 1)
            for i in range(CK):
                link(scaled_product(CV[:, i, :], CV[:, i, :], col("ln_w", i), RS[:, 1, :]))
                vec.tensor_scalar(CV[:, i, :], CV[:, i, :], col("ln_b", i), None, ALU.add).then_inc(conv_ln, 1)
            for i in range(CK):
                denominator(f"conv{i}")
                s = sigmoid_of(f"conv{i}")
                vec.tensor_tensor(CV[:, i, :], CV[:, i, :], s, ALU.mult).then_inc(conv_act, 1)
            for i in range(CK):
                vec.wait_ge(*is_full(f"pw{i}"))
                free_inc(scaled_product(CAT[:, NQ + i, :], bank(f"pw{i}"), col("b_pw", i), ZC[:, i, :], ALU.add),
                         f"pw{i}")
            modulation_columns("gate", 2, "b_gate")
            vec.wait_ge(*is_free("gate_t"))
            for m in range(DK):
                vec.wait_ge(*is_full(f"out{m}"))
                free_inc(scaled_sum(X[:, m, :], bank(f"out{m}"), MOD[:, 2, m, 0:1], X[:, m, :]), f"out{m}")

            def normalise(n, row, gain):
                vec.wait_ge(rstd, n)
                for k in range(DK):
                    ins = scaled_product(U[:, k, :], X[:, k, :], col(gain, k), RS[:, row, :])
                ins.then_inc(normed, 1)

            normalise(4, 0, "g_mix")

            def shift_end(name, n, m, out):
                vec.wait_ge(partial, n)
                return scaled_sum(out[:, 1:S], bank(name)[:, 0:S - 1], col("mu", m), out[:, 1:S])

            free_inc(shift_end("wdad", 1, MU_WDAD, T1), "wdad")
            vec.wait_ge(*is_free("wdad"))
            vec.wait_ge(zeroed, 3)
            vec.tensor_copy(TZ[DH:P, 1, :], T1[DH:P, :])
            free_inc(shift_end("gd", 2, MU_GD, T2), "gd")
            denominator("wd", slice(0, DH))
            s = sigmoid_of("wd", slice(0, DH))
            vec.tensor_scalar(TZ[0:DH, 0, :], s, 2.0, -1.0, ALU.mult, ALU.add).then_inc(low_used, 1)
            denominator("gd_sig")
            vec.wait_ge(zeroed, 4)
            for i in range(2):
                vec.wait_ge(head_rs, 9 + i)
                scaled_product(QMZ[0:DH, 0, i, :], bank(f"qm{i}", S, slice(0, DH)), col("mqn", 0, slice(0, DH)),
                               HR[0:DH, i, :])
                free_inc(scaled_product(QMZ[DH:P, 1, i, :], bank(f"qm{i}", S, slice(DH, P)),
                                        col("mqn", 0, slice(DH, P)), HR[DH:P, i, :]), f"qm{i}")

            def memory_heads(j):
                vec.wait_ge(*is_full(f"mo{j}"))
                free_inc(vec.tensor_copy(CAT[:, NP + j, :], bank(f"mo{j}")), f"mo{j}")

            attention(MUNITS, "e", MPR, SM, memory_heads)

            def pair_inputs(p):
                for i, (x, out) in enumerate((("k", K0), ("r", R0), ("v", V0))):
                    free_inc(shift_end(f"{x}_{p}", 3 + 3 * p + i, MU_PAIR + 3 * p + i, out), f"{x}_{p}")
                denominator(f"w_{p}")
                denominator(f"A_{p}")

            def blocks_of(out, make):
                a = make(out[0:DH, :, 0:DH], slice(0, DH))
                return make(out[DH:P, :, DH:P], slice(DH, P))

            def chunks(x, rows):
                return x[rows, :].rearrange("p (c t) -> p c t", c=NC)

            pair_inputs(0)
            for p in range(NP):
                vec.wait_ge(sig_out, sig_at[f"w_{p}"][0] + 1)
                link(vec.tensor_tensor_scan(LG, tab("reset"), EL, 0.0, ALU.mult, ALU.add))
                vec.tensor_tensor(T1, LG, EL, ALU.subtract).then_inc(scan_done, 1)
                vec.wait_ge(*is_full(f"kks_{p}"))
                free_inc(vec.tensor_scalar(HR[:, 0, :], bank(f"kks_{p}"), KK_LEAST, None, ALU.max), f"kks_{p}")
                vec.wait_ge(sig_out, sig_at[f"A_{p}"][0] + 1)
                link(vec.tensor_scalar(QW[:], AV, col("k_a", p), KA1[:, p:p + 1], ALU.mult, ALU.add))
                link(vec.tensor_tensor(QW[:], QW[:], K0, ALU.mult))
                scaled_product(T2, R0, col("r_k", p), QW[:]).then_inc(bonus_in, 1)
                vec.wait_ge(kk_rs, p + 1)
                link(scaled_product(KKN, K0, col("k_k", p), HR[:, 0, :]))
                vec.wait_ge(*is_full(f"bon_{p}"))
                free_inc(vec.tensor_tensor(BV, bank(f"bon_{p}"), V0, ALU.mult), f"bon_{p}")
                vec.wait_ge(exps_done, p + 1)
                vec.tensor_copy(ELC, EL[:, C - 1:S:C])
                if p:
                    vec.wait_ge(*is_full(f"tv_{p - 1}_{NG - 1}"))
                else:
                    vec.wait_ge(zeroed, 9)
                link(blocks_of(ABD, lambda o, r: vec.scalar_tensor_tensor(
                    out=o, in0=chunks(KKN, r), scalar=-1.0, in1=chunks(T1, r), op0=ALU.mult, op1=ALU.mult)))
                link(vec.tensor_tensor(KKN, KKN, AV, ALU.mult))
                blocks_of(BBD, lambda o, r: vec.tensor_tensor(o, chunks(KKN, r), chunks(LG, r), ALU.mult))
                blocks_of(KBD, lambda o, r: vec.tensor_tensor(o, chunks(QW[:], r), chunks(LG, r), ALU.mult))
                blocks_of(RBD, lambda o, r: vec.tensor_tensor(o, chunks(R0, r), chunks(EL, r), ALU.mult)
                          ).then_inc(bd_ready, 1)
                if p + 1 < NP:
                    pair_inputs(p + 1)
                for g in range(NG):
                    vec.wait_ge(*is_full(f"nt_{p}_{g}"))
                    free_inc(vec.tensor_tensor(NT[g], bank4(f"nt_{p}_{g}"), tab4("before"), ALU.mult), f"nt_{p}_{g}")
                for g in range(NG):
                    vec.wait_ge(*is_full(f"nn_{p}_{g}"))
                    free_inc(vec.tensor_tensor(XN[g], bank4(f"nn_{p}_{g}"), tab4("m1"), ALU.mult), f"nn_{p}_{g}")
                    vec.wait_ge(*is_free(f"nt_{p}_{g}"))
                    link(vec.tensor_tensor(XT[g], NT[g], tab4("m1t"), ALU.mult))
                    vec.tensor_tensor(XN[g], XN[g], tab4("ident"), ALU.add)
                    vec.tensor_tensor(XT[g], XT[g], tab4("ident"), ALU.add).then_inc(x_first, 1)
                for x, out, mask in (("mak", MAK, "before"), ("mrb", MRB, "upto"), ("mrk", MRK, "upto")):
                    for g in range(NG):
                        vec.wait_ge(*is_full(f"{x}_{p}_{g}"))
                        free_inc(vec.tensor_tensor(out[g], bank4(f"{x}_{p}_{g}"), tab4(mask), ALU.mult),
                                 f"{x}_{p}_{g}")
                for b in LEVELS:
                    for g in range(NG):
                        name = f"xp{b}_{p}_{g}"
                        vec.wait_ge(*is_full(name))
                        free_inc(vec.tensor_tensor(XP[g], bank4(name), tab4(f"m{b}"), ALU.mult), name)
                    for g in range(NG):
                        if b != LEVELS[-1]:
                            name = f"xn{b}_{p}_{g}"
                            vec.wait_ge(*is_full(name))
                            free_inc(vec.tensor_tensor(XN[g], bank4(name), XN[g], ALU.add), name)
                        name = f"xt{b}_{p}_{g}"
                        vec.wait_ge(*is_full(name))
                        free_inc(vec.tensor_tensor(XT[g], bank4(name), XT[g], ALU.add), name)
                for g in range(NG):
                    vec.wait_ge(*is_full(f"gt_{p}_{g}"))
                    free_inc(vec.tensor_tensor(GT[g], bank4(f"gt_{p}_{g}"), tab4("ident"), ALU.add), f"gt_{p}_{g}")
                for g in range(NG):
                    vec.wait_ge(*is_full(f"rp_{p}_{g}"))
                    free_inc(vec.tensor_tensor(RP[g], bank4(f"rp_{p}_{g}"), RBD[:, g * G:(g + 1) * G, :], ALU.add),
                             f"rp_{p}_{g}")
                for g in range(NG):
                    vec.wait_ge(*is_full(f"f_{p}_{g}"))
                    free_inc(vec.tensor_tensor(FB[g], bank4(f"f_{p}_{g}"),
                                               ELC[:, g * G:(g + 1) * G, None].to_broadcast([P, G, P]), ALU.mult),
                             f"f_{p}_{g}")
                    vec.wait_ge(*is_free(f"f_{p}_{g}"))
                for g in range(NG):
                    if g == 0:
                        if p:
                            vec.wait_ge(*is_full(f"y_{p - 1}_{NG - 1}"))
                        vec.memset(H[:, 0, :], 0.0).then_inc(h_first, 1)
                    else:
                        vec.wait_ge(*is_full(f"y_{p}_{g - 1}"))
                        vec.tensor_copy(H[:, 0, :], H[:, G, :]).then_inc(h_first, 1)
                    for c in range(G):
                        if g * G + c == NC - 1:
                            break
                        name = f"h_{p}_{g}_{c}"
                        vec.wait_ge(*is_full(name))
                        n = g * G + c
                        free_inc(scaled_sum(H[:, c + 1, :], bank(name, P), ELC[:, n:n + 1], FB[g][:, c, :]), name)
                    if c == G - 1 and g + 1 < NG:
                        vec.wait_ge(*is_free(name))
                    name = f"y_{p}_{g}"
                    vec.wait_ge(*is_full(name))
                    y = CAT[:, p, g * G * C:(g + 1) * G * C].rearrange("p (c t) -> p c t", c=G)
                    vec.tensor_copy(y[0:DH], bank4(name)[0:DH, :, 0:DH])
                    free_inc(vec.tensor_copy(y[DH:P], bank4(name)[DH:P, :, DH:P]), name)
                o = CAT[:, p, :]
                vec.wait_ge(*is_full(f"gm_{p}"))
                free_inc(scaled_sum(o, bank(f"gm_{p}"), -1.0 / DH, o), f"gm_{p}")
                vec.wait_ge(gn_rs, p + 1)
                link(scaled_product(o, o, col("lnx_g", p), HR[:, 1, :]))
                link(scaled_sum(o, o, col("lnx_b", p), BV, ALU.add))
                vec.wait_ge(*is_full(f"gg_{p}"))
                free_inc(vec.tensor_tensor(o, bank(f"gg_{p}"), o, ALU.mult), f"gg_{p}")
            for m in range(DK):
                vec.wait_ge(*is_full(f"mix{m}"))
                free_inc(vec.tensor_tensor(X[:, m, :], bank(f"mix{m}"), X[:, m, :], ALU.add), f"mix{m}")
            normalise(5, 1, "g_ffn")
            for m in range(DK):
                vec.wait_ge(*is_full(f"down{m}"))
                free_inc(vec.tensor_tensor(X[:, m, :], bank(f"down{m}"), X[:, m, :], ALU.add), f"down{m}")


def tables_of_shapes():
    t = {}
    tok = np.arange(S)
    dim = np.arange(P) % DH
    half = DH // 2
    freq = (10000.0 ** (-(np.arange(0, half, 2, dtype=np.float32)) / np.float32(half))).astype(np.float32)
    pos = np.where((dim < half)[:, None], (tok // GRID_W)[None, :], (tok % GRID_W)[None, :]).astype(np.float32)
    ang = pos * freq[dim % (half // 2)][:, None]
    t["cos"], t["sin"] = np.cos(ang), np.sin(ang)
    t["reset"] = np.broadcast_to((tok % C != 0).astype(np.float32), (P, S))
    rot = np.zeros((P, P), np.float32)
    for d in range(P):
        if d % half < half // 2:
            rot[d + half // 2, d] = -1.0
            rot[d, d + half // 2] = 1.0
    t["rot"] = rot
    r, c = np.arange(P)[:, None], np.arange(P)[None, :]
    same = r // DH == c // DH
    t["heads"] = same
    t["ones"] = np.ones((P, P))
    t["ident"] = r == c
    t["before"] = same & (r < c)
    t["upto"] = same & (r <= c)

    def band(b):
        return (r // (2 * b) == c // (2 * b)) & (r // b % 2 == 1) & (c // b % 2 == 0)

    t["m1"], t["m1t"] = band(1), band(1).T
    for b in LEVELS:
        t[f"m{b}"] = band(b)
    return np.ascontiguousarray(np.concatenate([np.asarray(t[k], np.float32) for k, _ in TAB], axis=1))


def feature_major(x):
    return np.ascontiguousarray(x.T.reshape(-1, P, x.shape[0]).transpose(1, 0, 2))


def stationary(w, rows=None):
    w = w if rows is None else w[rows]
    return w.reshape(-1, P, w.shape[1]).transpose(1, 0, 2).reshape(P, -1)


def kernel(**inputs):
    import concourse.bacc as bacc
    from concourse.bass_utils import run_bass_kernel_spmd

    a = {k: np.asarray(v) for k, v in inputs.items()}
    w_in, w_mod, rw_in = a["w_in"][0], a["w_mod"][0], a["rw_in_2"][0]
    w_pw, w_out, w_kv = a["w_pw"][0], a["w_out"][0], a["w_mem_kv_2"]
    w_mix, w_up, w_down = a["w_out_2"][0], a["w_ff1_2"][0], a["w_ff2_2"][0]
    DA = NQ * P
    K_AT, V_AT, ZA_AT = DA, DA + P, DA + 2 * P
    A_AT = ZA_AT + DA
    G_AT, ZC_AT = A_AT + CK * P, A_AT + 2 * CK * P
    MW = NP * P

    def pair(j):
        return np.concatenate([np.arange(j * DH, (j + 1) * DH), np.arange((NQ + j) * DH, (NQ + j + 1) * DH)])

    out_rows = np.concatenate([pair(j) for j in range(NQ)] + [np.arange(DA, D)])

    def block(name):
        if name.startswith("kmem"):
            return stationary(w_kv[:, int(name[4]) * P:(int(name[4]) + 1) * P])
        if name.startswith("vmem"):
            h = int(name[4])
            return stationary(w_kv[h * 4 * P:(h + 1) * 4 * P, SM:2 * SM])
        for i, g in enumerate(("shift", "scale", "gate")):
            if name.startswith(g):
                k = int(name[len(g):])
                return w_mod[k * P:(k + 1) * P, i * D:(i + 1) * D]
        if name == "wdad":
            return stationary(rw_in[:, 3 * MW:3 * MW + P])
        if name == "gd":
            return stationary(rw_in[:, 3 * MW + P:3 * MW + 2 * P])
        if name[:2] == "qm":
            at = 3 * MW + (2 + int(name[2])) * P
            return stationary(rw_in[:, at:at + P])
        if name[1:2] == "_":
            at = "krv".index(name[0])
            at = (1, 0, 2)[at] * MW + int(name[2]) * P
            return stationary(rw_in[:, at:at + P])
        if name == "k":
            return stationary(w_in[:, K_AT:K_AT + P])
        if name == "v":
            return stationary(w_in[:, V_AT:V_AT + P])
        if name[:2] == "zc":
            at = ZC_AT + int(name[2]) * P
            return stationary(w_in[:, at:at + P])
        if name[:2] == "za":
            return stationary(w_in[:, ZA_AT + pair(int(name[2]))])
        if name[:2] == "pw":
            i = int(name[2])
            return np.concatenate([stationary(w_pw[:, m * P:(m + 1) * P]) for m in (2 * i, 2 * i + 1)], axis=1)
        if name.startswith("out"):
            m = int(name[3])
            return stationary(w_out[:, m * P:(m + 1) * P], out_rows)
        if name.startswith("mix"):
            m = int(name[3])
            return stationary(w_mix[:, m * P:(m + 1) * P])
        if name.startswith("up"):
            m = int(name[2:])
            return stationary(w_up[:, m * P:(m + 1) * P])
        if name.startswith("down"):
            m, k = map(int, name[4:].split("_"))
            return stationary(w_down[k * D:(k + 1) * D, m * P:(m + 1) * P])
        if name[0] == "q":
            return stationary(w_in[:, pair(int(name[1]))])
        at = (A_AT if name[0] == "a" else G_AT) + int(name[1]) * P
        return stationary(w_in[:, at:at + P])

    weights = np.stack([block(n) for n in BLOCKS])

    def columns(x):
        return x.reshape(-1, P).T

    two = np.concatenate
    mu = a["rw_mu_2"][0]
    mus = [mu[3 * MW:3 * MW + P], mu[3 * MW + P:3 * MW + 2 * P]]
    for p in range(NP):
        mus += [mu[at * MW + p * P:at * MW + (p + 1) * P] for at in (1, 0, 2)]
    b_mod = a["b_mod"][0]
    conv_w = a["conv_w"][0]
    vec = {
        "norm_w": columns(a["norm_w"][0]), "b_shift": columns(b_mod[0:D]), "b_scale": columns(b_mod[D:2 * D]),
        "b_gate": columns(b_mod[2 * D:]), "qn": columns(two([a["q_norm_w"][0]] * 2)),
        "kn": columns(two([a["k_norm_w"][0]] * 2)), "conv_b": columns(a["conv_b"][0]),
        "ln_w": columns(a["conv_ln_w"][0]), "ln_b": columns(a["conv_ln_b"][0]), "b_pw": columns(a["b_pw"][0]),
        "conv_w": conv_w.T.reshape(CK, P, TAPS).transpose(1, 0, 2).reshape(P, -1),
        "mu": np.stack(mus, axis=1), "w0": columns(a["rw_w0_2"][0]), "a0": columns(a["rw_a0_2"][0]),
        "k_k": columns(a["rw_k_k_2"][0]), "k_a": columns(a["rw_k_a_2"][0]),
        "r_k": columns(a["rw_r_k_2"][0].reshape(-1)), "lnx_g": columns(a["rw_lnx_g_2"][0]),
        "lnx_b": columns(a["rw_lnx_b_2"][0]), "g_mix": columns(a["norm_mix_g_2"][0]),
        "g_ffn": columns(a["norm_ffn_g_2"][0]), "g_mem": columns(a["mem_norm_g_2"]),
        "mqn": columns(two([a["mem_q_norm_g_2"][0]] * 2)), "mkn": columns(two([a["mem_k_norm_g_2"][0]] * 2)),
        "cc": np.stack([a["c"][0], a["c_ctx"]], axis=1).reshape(DK, P, 2).transpose(1, 0, 2).reshape(P, -1),
    }
    lora = two([a["rw_w2_2"][0], a["rw_a2_2"][0]], axis=0)
    small = two([vec[k] for k, _ in VEC] + [lora, a["rw_g2_2"][0]], axis=1)
    sent = {"small": small, "tables": tables_of_shapes(), "xT": feature_major(a["x"][0]),
            "ctxT": feature_major(a["ctx"][0]), "memT": feature_major(a["mem_2"][0]), "weights": weights}
    sent = {k: np.ascontiguousarray(v) for k, v in sent.items()}
    nc = bacc.Bacc("TRN2", target_bir_lowering=False, num_devices=1)
    args = {k: nc.dram_tensor(k, v.shape, F32, kind="ExternalInput").ap() for k, v in sent.items()}
    out = nc.dram_tensor("outT", (P, DK, S), F32, kind="ExternalOutput").ap()
    build(nc, outT=out, **args)
    r = run_bass_kernel_spmd(nc, [sent], core_ids=[0])
    got = r.results[0]["outT"]
    return np.ascontiguousarray(got.transpose(1, 0, 2).reshape(D, S).T)[None]
```

```python
from contextlib import ExitStack

import numpy as np

import concourse.bass as bass
from concourse import mybir

F32 = mybir.dt.float32
F32R = mybir.dt.float32r
ALU = mybir.AluOpType
ACT = mybir.ActivationFunctionType
AX = mybir.AxisListType.X

P = 128
D = 1024
DK = D // P
S = 512
SC = 256
SM = 256
DH = 64
NQ = 4
CK = 4
TAPS = 31
PAD = (TAPS - 1) // 2
SKEYS = SC + S
KT = SKEYS // P
MT = SM // P
NP = 6
C = 64
NC = S // C
G = 4
NG = NC // G
LEVELS = (2, 4, 8, 16, 32)
FF = 4096 // P
HALVES = 2
FH_TILES = FF // HALVES
DOWN_BLOCKS = FH_TILES // DK
GRID_W = 64
EPS = 1e-6
GN_EPS = 64e-5
DECAY = float(np.exp(-0.5))
KK_LEAST = 1e-24
KK_SCALE = 2.0 ** 16
SIG_MOST = 1e18
RING = 6
SBUF_AT, SBUF_WORDS = 4128, 57344
UNITS = NQ * 2 * (S // P)
MUNITS = 2 * 2 * (S // P)
AHEAD = 2
MAHEAD = 3
BESIDE_ATTENTION = {3: "gate_t", 4: "cmean", 6: "cvar", 20: "pw0", 21: "pw1", 22: "pw2", 23: "pw3"}

VEC = [("norm_w", 8), ("b_shift", 8), ("b_scale", 8), ("b_gate", 8), ("qn", 1), ("kn", 1),
       ("conv_b", 4), ("ln_w", 4), ("ln_b", 4), ("b_pw", 4), ("conv_w", 4 * TAPS), ("mu", 20),
       ("w0", 6), ("a0", 6), ("k_k", 6), ("k_a", 6), ("r_k", 6), ("lnx_g", 6), ("lnx_b", 6),
       ("g_mix", 8), ("g_ffn", 8), ("g_mem", 8), ("mqn", 1), ("mkn", 1), ("cc", 16)]
AT = {}
_n = 0
for _k, _w in VEC:
    AT[_k] = _n
    _n += _w
NVEC = _n
LORA_AT, G2_AT = NVEC, NVEC + 768
NSMALL = NVEC + 2 * 768
MU_WDAD, MU_GD, MU_PAIR = 0, 1, 2

TAB = [("cos", S), ("sin", S), ("reset", S), ("rot", P), ("heads", P), ("ones", P), ("ident", P),
       ("before", P), ("upto", P), ("m1", P), ("m1t", P)] + [(f"m{b}", P) for b in LEVELS]
TAT = {}
_n = 0
for _k, _w in TAB:
    TAT[_k] = (_n, _w)
    _n += _w
NTAB = _n

BLOCKS = (["kmem0", "kmem1"]
          + [f"shift{k}" for k in range(DK)] + [f"scale{k}" for k in range(DK)] + ["vmem0", "vmem1"]
          + [f"{x}{i}" for i in range(CK) for x in "ag"]
          + ["k", "v"] + [f"q{j}" for j in range(NQ)] + [f"zc{i}" for i in range(CK)]
          + [f"za{j}" for j in range(NQ)] + [f"gate{k}" for k in range(DK)] + ["pw0", "pw1"]
          + [f"out{m}" for m in range(DK)]
          + ["wdad", "gd", "qm0", "qm1"] + [f"{x}_{p}" for p in range(NP) for x in "krv"]
          + [f"mix{m}" for m in range(DK)]
          + [n for h in range(HALVES)
             for n in ([f"up{m}" for m in range(h * FH_TILES, (h + 1) * FH_TILES)]
                       + [f"down{h}_{m}_{b}" for m in range(DK) for b in range(DOWN_BLOCKS)])])
BLOCK_AT = {n: i for i, n in enumerate(BLOCKS)}
SPLIT = [n for n in BLOCKS if n.startswith(("mix", "up", "down"))]
SPLIT_AT = {n: i for i, n in enumerate(SPLIT)}
CAT_ORDER = (0, 1, 2, 3, 6, 7, 4, 5)


BESIDE_CHAIN = [[("k", 0, 2)], [("k", 2, 4)], [("k", 4, 6)], [("k", 6, DK)], [("r", 0, 1)], [("r", 1, 4)],
                [("r", 4, DK)]]
assert len(BESIDE_CHAIN) == NC - 1


def beside_level(p, b):
    last = {LEVELS[0]: ["gm"], LEVELS[1]: ["gv"], LEVELS[3]: ["gg"]}.get(b, []) if p else []
    following = {LEVELS[1]: ["v"], LEVELS[2]: ["bon"]}.get(b, []) if p + 1 < NP else []
    return [f"{x}_{p - 1}" for x in last] + [f"{x}_{p + 1}" for x in following]


def psum_order():
    o = [(n, 1, None) for n in ("mem_sum", "ctx_sum", "x_sum", "kmem0", "kmem1", "hs0", "hs1")]

    def add(*names):
        o.extend((n, 1, None) for n in names)

    add("shift_lo", "shift_hi", "scale_lo", "scale_hi", "shift_t", "vmem", "scale_t")
    for i in range(CK):
        add(f"a{i}", f"g{i}")
    add("kx", "kc", "hs2", "rot0", "hs3", "v_lo", "v_hi")
    for j in range(NQ):
        add(f"q{j}", f"hs{4 + j}", f"rot{1 + j}")
    add(*(f"zc{i}" for i in range(CK)), *(f"za{j}" for j in range(NQ)))
    add("gate_lo", "gate_hi")
    pair = 0
    for i in range(UNITS + AHEAD + 1):
        if i < UNITS:
            o.append((f"s{i}", 2, pair % 3 * 2))
            pair += 1
        if 0 <= i - AHEAD < UNITS:
            o.append((f"pt{i - AHEAD}", 2, pair % 3 * 2))
            pair += 1
        if i in BESIDE_ATTENTION:
            o.append((BESIDE_ATTENTION[i], 1, 7))
        v = i - AHEAD - 1
        if v >= 0 and v % 8 == 0:
            o.append((f"o{v // 8}", 1, 6 + v // 8 % 2))
    add(*(f"out{m}" for m in range(DK)), "h1_sum", "wdad", "gd", "qm0", "hs8", "qm1", "hs9")
    single = 0
    for i in range(MUNITS + MAHEAD + 1):
        if i < MUNITS:
            o.append((f"e{i}", 1, single % 6))
            single += 1
        if 0 <= i - MAHEAD < MUNITS:
            o.append((f"et{i - MAHEAD}", 1, single % 6))
            single += 1
        v = i - MAHEAD - 1
        if v >= 0 and v % 8 == 0:
            o.append((f"mo{v // 8}", 1, 6 + v // 8))
    add(*(f"{x}_0" for x in "wAkrv"), "kks_0", "bon_0", *(f"{x}_1" for x in "wAkr"), "kks_1")
    for p in range(NP):
        for x in ("nt", "nn", "ta", "tb", "tk", "tv", "mak", "mrb", "mrk"):
            add(*(f"{x}_{p}_{g}" for g in range(NG)))
        for b in LEVELS:
            add(*(f"xp{b}_{p}_{g}" for g in range(NG)), *beside_level(p, b))
            for g in range(NG):
                if b != LEVELS[-1]:
                    add(f"xn{b}_{p}_{g}")
                add(f"xt{b}_{p}_{g}")
        for x in ("mv", "w", "u", "gt", "rp", "f"):
            add(*(f"{x}_{p}_{g}" for g in range(NG)))
        if p + 2 < NP:
            add(f"w_{p + 2}", f"A_{p + 2}")
        for n in range(NC - 1):
            add(f"h_{p}_{n}")
            if n == G:
                add(f"y_{p}_0")
            add(*(f"{x}_{p + 2}" for x, lo, hi in BESIDE_CHAIN[n] if lo == 0 and p + 2 < NP))
        add(f"y_{p}_1")
        if p + 2 < NP:
            add(f"kks_{p + 2}")
    add(f"gm_{NP - 1}", f"gv_{NP - 1}", f"gg_{NP - 1}")
    add(*(f"mix{m}" for m in range(DK)), "h2_sum")
    for h in range(HALVES):
        add(*(f"up{m}" for m in range(h * FH_TILES, (h + 1) * FH_TILES)), *(f"down{h}_{m}" for m in range(DK)))
    return o


def psum_plan():
    last, count, at, plan = [None] * 8, [0] * 8, 0, {}
    for name, n, pinned in psum_order():
        here = at % 8 if pinned is None else pinned
        count[here] += 1
        before = []
        for b in range(here, here + n):
            if last[b] is not None and last[b] not in before:
                before.append(last[b])
            last[b] = name
        assert name not in plan, name
        plan[name] = (here, n, count[here], before)
        at = here + n
    return plan


def last_product(block):
    for g in ("shift", "scale", "gate"):
        if block.startswith(g):
            return f"{g}_hi" if block.endswith(str(DK - 1)) else None
    return {"vmem0": "vmem", "vmem1": "vmem", "k": "kc", "v": "v_hi", "pw0": "pw1",
            "pw1": "pw3"}.get(block, block)


def build(nc, small, tables, xT, ctxT, memT, weights, outT):
    plan = psum_plan()
    with ExitStack() as ctx:
        room = [SBUF_AT]
        placed = {}

        def sb(name, *shape):
            words = int(np.prod(shape[1:]))
            placed[name] = room[0]
            t = nc.alloc_sbuf_tensor_at(name, list(shape), F32, offset=4 * room[0])
            room[0] += -(-words // 8) * 8
            assert room[0] <= SBUF_WORDS
            return t

        def over(name, base, at, *shape):
            return nc.alloc_sbuf_tensor_at(name, list(shape), F32R, offset=4 * (placed[base] + at))

        def sem(name):
            return ctx.enter_context(nc.semaphore(name))

        ring = sb("ring", P, RING, D)
        X = sb("residual", P, DK, S)
        U = sb("normed", P, DK, S)
        CAT = sb("mixed", P, DK, S)
        TB = sb("tables_sb", P, NTAB)
        SV = sb("small_sb", P, NSMALL)
        KVM = sb("memory_keys_values", P, (2 + MT) * SM)
        KMEM = KVM[:, 0:2 * SM].rearrange("p (a b) -> p a b", a=2)
        VMEM = KVM[:, 2 * SM:].rearrange("p (a b) -> p a b", a=MT)
        SG = sb("sigmoids", P, 2, S)
        HS = sb("head_squares", P, 2, S)
        HR = sb("head_rstd", P, 2, S)
        RS = sb("rstd", P, 2, S)
        QW = sb("weighted", P, S)
        T12 = sb("t1_t2", P, 2, S)
        T1, T2 = T12[:, 0, :], T12[:, 1, :]
        MOD = sb("mod_cols", P, 3, DK, 2)
        SMALLT = sb("small_temps", P, 256)
        WORKW = 22656
        work = sb("work", P, WORKW)
        psum = ctx.enter_context(nc.psum_tensor("psum", [P, 8 * S], F32))

        def region(at, *shape):
            n = int(np.prod(shape))
            v = work[:, at:at + n]
            assert at + n <= WORKW
            if len(shape) == 2:
                return v.rearrange("p (a b) -> p a b", a=shape[0])
            if len(shape) == 3:
                return v.rearrange("p (a b c) -> p a b c", a=shape[0], b=shape[1])
            return v

        SQ = region(0, DK, S)
        CV = region(4 * S, CK, S)
        MEM = region(8 * S, DK, SM)
        CTX = region(12 * S, DK, SC)
        PR = region(8 * S, AHEAD + 1, SKEYS)
        PT = region(8 * S + (AHEAD + 1) * SKEYS, 2, SKEYS)
        at = 16 * S
        GLU = region(at, CK, S + 2 * PAD); at += CK * (S + 2 * PAD)
        QZ = region(at, 2, NQ, S); at += 2 * NQ * S
        KTT = region(at, SKEYS); at += SKEYS
        VT = region(at, KT, P); at += SKEYS
        ZC = region(at, CK, S); at += CK * S
        ZA = region(at, NQ, S); at += NQ * S
        CT = region(at, S); at += S
        MODROW = [T12[:].rearrange("p a b -> p (a b)"), region(at, D)]
        at = 0
        ABD, BBD, KBD, RBD0, VBD = (region(i * NC * P, NC, P) for i in range(5)); at += 5 * NC * P
        RBD = [RBD0, KVM[:].rearrange("p (a b) -> p a b", a=NC)]
        K0, R0, V0, LG, EL, AV, KKN, BV0 = (region(at + i * S, S) for i in range(8)); at += 8 * S
        TZ = region(at, 2, S); at += 2 * S
        SGD = region(at, S); at += S
        BV = [BV0, TB[:, TAT["cos"][0]:TAT["cos"][0] + S]]
        H = [region(at, G, P), TB[:, TAT["sin"][0]:TAT["sin"][0] + S].rearrange("p (a b) -> p a b", a=G)]
        at += G * P
        half = at
        HB = [[region(half + (g * 11 + i) * G * P, G, P) for i in range(11)] for g in range(NG)]
        NT, MAK, MRB, MRK, TA, TBT, TK, TV, XN, XT, XP = (
            [HB[g][i] for g in range(NG)] for i in range(11))
        MV, WB, UB, FB, GT, RP = XP, NT, XN, XT, MAK, TA
        QMZ = region(half, 2, 2, S)
        MPR = region(half + 4 * S, MAHEAD + 1, SM)
        MPT = region(half + 6 * S, 2, SM)
        CATH = over("mixed_high", "work", 0, P, DK, S)
        CATL = over("mixed_low", "work", DK * S, P, DK, S)
        SQ2 = region(half, DK, S)
        WH = over("weights_high", "work", 2 * FH_TILES * S, P, 2, D)
        WL = over("weights_low", "work", 2 * FH_TILES * S + 2 * D, P, 2, D)
        FS = region(0, FH_TILES, S)
        FL = over("hidden_low", "work", 0, P, FH_TILES, S)
        FH = over("hidden_high", "work", FH_TILES * S, P, FH_TILES, S)
        UH = over("normed_high", "mixed", 0, P, DK, S)
        UL = over("normed_low", "normed", 0, P, DK, S)
        assert half + DK * S <= 2 * FH_TILES * S and 2 * FH_TILES * S + 4 * D <= WORKW

        def col(name, i=0, rows=slice(0, P)):
            return SV[rows, AT[name] + i:AT[name] + i + 1]

        def cols(name, i, n):
            return SV[:, AT[name] + i:AT[name] + i + n]

        def tab(name):
            return TB[:, TAT[name][0]:TAT[name][0] + TAT[name][1]]

        def tab4(name):
            return tab(name)[:, None, :].to_broadcast([P, G, P])

        NEG = SMALLT[:, 0:12]
        KA1 = SMALLT[:, 12:18]
        MU1 = SMALLT[:, 18:38]
        SILU_C = SMALLT[:, 38:54].rearrange("p (k w) -> p k w", k=DK)
        SILU_E = SMALLT[:, 54:70]
        ROWMAX, NEGMAX, ROWSUM, ROWINV = (SMALLT[:, 72 + 4 * i:76 + 4 * i] for i in range(4))
        ELC = [SMALLT[:, 96 + i * NC:96 + (i + 1) * NC] for i in range(2)]

        full = [sem(f"psum_full{b}") for b in range(8)]
        free = [sem(f"psum_free{b}") for b in range(8)]
        slot = [sem(f"slot_loaded{i}") for i in range(RING)]
        tables_in, small_in, mem_in, x_in, ctx_in = map(
            sem, ("tables_in", "small_in", "mem_in", "x_in", "ctx_in"))
        mod_block_used = sem("mod_block_used")
        squares, rstd, normed = sem("squares_ready"), sem("rstd_ready"), sem("normed_ready")
        res_squares = sem("residual_squares_ready")
        c_exp, c_den, c_sig, c_ready = map(sem, ("c_exp", "c_den", "c_sigmoid", "c_silu_ready"))
        mod_ready = sem("modulation_ready")
        consts_ready = sem("derived_columns_ready")
        sig_exp, sig_den, sig_out = map(sem, ("sigmoid_exp", "sigmoid_denominator", "sigmoid_ready"))
        head_sq, head_rs = sem("head_squares_ready"), sem("head_rstd_ready")
        q_ready, k_ready = sem("q_ready"), sem("k_ready")
        zeroed = sem("zeroed")
        negmax, probs_scaled, pt_used = sem("negmax_ready"), sem("probs_scaled"), sem("row_sums")
        conv_out, conv_sq, conv_rs, conv_ln, conv_act = map(
            sem, ("conv_out", "conv_squares", "conv_rstd", "conv_normed", "conv_act"))
        partial = sem("shift_partial")
        low_used = sem("tanh_placed")
        scan_done, exps_done = sem("log_decays_ready"), sem("decays_ready")
        kk_sq, kk_rs, bonus_in = sem("kk_squares"), sem("kk_rstd"), sem("bonus_in")
        bd_ready, v_ready = sem("a_b_blocks_ready"), sem("v_blocks_ready")
        k_blocks, r_ready, key_step, gn_done = map(sem, ("k_blocks_ready", "r_blocks_ready", "key_step", "gn_done"))
        x_first = sem("inverse_started")
        gn_sq, gn_rs = sem("gn_squares"), sem("gn_rstd")
        w_high, w_low, half_used = map(sem, ("weights_high_ready", "weights_low_ready", "first_down_block_used"))
        cat_high, cat_low = sem("mixed_high_ready"), sem("mixed_low_ready")
        u_high, u_low = sem("normed_high_ready"), sem("normed_low_ready")
        h_relu, h_high, h_low = map(sem, ("hidden_relu", "hidden_high_ready", "hidden_low_ready"))
        out_stored = sem("out_stored")
        act_step, vec_step = sem("act_step"), sem("vec_step")

        def bank(name, w=None, rows=slice(0, P)):
            b, n, _, _ = plan[name]
            return psum[rows, b * S:b * S + (w or n * S)]

        def bank4(name):
            return bank(name).rearrange("p (g t) -> p g t", g=G)

        def is_full(name):
            return full[plan[name][0]], plan[name][2]

        def is_free(name):
            return free[plan[name][0]], plan[name][2]

        def split_used(q):
            name = SPLIT[q]
            if not name.startswith("down"):
                return is_full(name)
            product, b = name.rsplit("_", 1)
            if int(b) == DOWN_BLOCKS - 1:
                return is_full(product)
            firsts = [n for n in SPLIT if n.startswith("down") and not n.endswith(f"_{DOWN_BLOCKS - 1}")]
            return half_used, firsts.index(name) + 1

        def full_inc(ins, name):
            ins.then_inc(full[plan[name][0]], 1)

        def free_inc(ins, name):
            ins.then_inc(free[plan[name][0]], 1)

        sigmoids = ([(f"g{i}", True, is_free(f"a{i}")) for i in range(CK)]
                    + [(f"zc{i}", False, is_free(f"zc{i}")) for i in range(CK)]
                    + [(f"za{j}", False, is_free(f"za{j}")) for j in range(NQ)]
                    + [(f"conv{i}", False, (conv_act, i + 1)) for i in range(CK)]
                    + [("wd", False, (low_used, 1)), ("gd_sig", False, None)]
                    + [(f"{x}_{p}", True, None) for p in range(NP) for x in "wA"])
        sig_at, kept = {}, 0
        for n, (name, frees, _) in enumerate(sigmoids):
            kept += not frees
            sig_at[name] = (n, is_free(name) if frees else (sig_exp, kept))
        heads = ([("kmem0", is_free("kmem0")), ("kmem1", is_free("kmem1")), ("kx", (k_ready, 1)),
                  ("kc", is_free("kc"))] + [(f"q{j}", (q_ready, j + 1)) for j in range(NQ)]
                 + [("qm0", is_free("qm0")), ("qm1", is_free("qm1"))])
        head_at = {name: n for n, (name, _) in enumerate(heads)}

        block = ctx.enter_context(nc.Block())

        @block.sync
        def _(sp):
            sp.dma_start(TB[:], tables).then_inc(tables_in, 16)
            sp.dma_start(MEM, memT).then_inc(mem_in, 16)
            sp.dma_start(SV[:], small).then_inc(small_in, 16)
            sp.dma_start(CTX, ctxT).then_inc(ctx_in, 16)
            mod_seen = 0
            for b, name in enumerate(BLOCKS):
                if b == 2:
                    sp.dma_start(X[:], xT).then_inc(x_in, 16)
                if b >= RING:
                    before = last_product(BLOCKS[b - RING])
                    if before in SPLIT_AT:
                        sp.wait_ge(w_low, SPLIT_AT[before] + 1)
                    elif before is None:
                        mod_seen += 1
                        sp.wait_ge(mod_block_used, mod_seen)
                    else:
                        sp.wait_ge(*is_full(before))
                sp.dma_start(ring[:, b % RING, :], weights[b]).then_inc(slot[b % RING], 16)
            for m in range(DK):
                sp.wait_ge(*is_free(f"down{HALVES - 1}_{m}"))
                sp.dma_start(outT[:, m, :], X[:, m, :]).then_inc(out_stored, 16)
            sp.wait_ge(out_stored, 16 * DK)

        @block.gpsimd
        def _(pool):
            pool.memset(GLU, 0.0).then_inc(zeroed, 1)
            pool.memset(QZ, 0.0).then_inc(zeroed, 1)
            pool.wait_ge(*is_free(f"out{DK - 1}"))
            pool.memset(TZ, 0.0).then_inc(zeroed, 1)
            pool.memset(QMZ, 0.0).then_inc(zeroed, 1)
            pool.wait_ge(*is_full("h1_sum"))
            for z in (ABD, BBD, KBD, RBD[0], VBD, H[0][:, 0, :]):
                pool.memset(z, 0.0).then_inc(zeroed, 1)
            pool.wait_ge(*is_full("mo1"))
            pool.memset(RBD[1], 0.0).then_inc(zeroed, 1)
            pool.wait_ge(zeroed, 11)
            for p in range(NP):
                pool.wait_ge(bonus_in, p + 1)
                pool.wait_ge(exps_done, p + 1)
                if p:
                    pool.wait_ge(*is_full(f"mrk_{p - 1}_{NG - 1}"))
                for rows, cs in ((slice(0, DH), slice(0, DH)), (slice(DH, P), slice(DH, P))):
                    k3, l3 = (x[rows, :].rearrange("p (c t) -> p c t", c=NC) for x in (QW[:], LG))
                    ins = pool.tensor_tensor(KBD[rows, :, cs], k3, l3, ALU.mult)
                ins.then_inc(k_blocks, 1)

        @block.tensor
        def _(pe):
            order = iter(psum_order())

            def take(name, w=None, rows=slice(0, P)):
                assert next(order)[0] == name, name
                for before in plan[name][3]:
                    pe.wait_ge(*is_free(before))
                return bank(name, w, rows)

            def loaded(name):
                b = BLOCK_AT[name]
                pe.wait_ge(slot[b % RING], 16 * (b // RING + 1))
                return ring[:, b % RING, :]

            def sum_over(name, src, n, w, each=None):
                out = take(name, w)
                for k in range(n):
                    if each:
                        pe.wait_ge(each[0], each[1] + k)
                    last = pe.matmul(out, tab("ones"), src(k), start=k == 0, stop=k == n - 1)
                full_inc(last, name)

            def project(block_name, name, src, w=S, each=None):
                wt = loaded(block_name)
                out = take(name, w)
                for k in range(DK):
                    if each:
                        pe.wait_ge(each[0], each[1] + k)
                    last = pe.matmul(out, wt[:, k * P:(k + 1) * P], src(k), start=k == 0, stop=k == DK - 1)
                full_inc(last, name)

            def one(name, stationary, moving, w=S):
                full_inc(pe.matmul(take(name, w), stationary, moving, start=True, stop=True), name)

            def head_sums(n, w=S):
                pe.wait_ge(head_sq, n + 1)
                one(f"hs{n}", tab("heads"), HS[:, n % 2, 0:w], w)

            def rotate(n, name):
                pe.wait_ge(*is_free(name))
                one(f"rot{n}", tab("rot"), QW[:])

            def modulation(g):
                lo, hi = take(f"{g}_lo", rows=slice(0, 2)), take(f"{g}_hi", rows=slice(0, 2))
                for k in range(DK):
                    wt = loaded(f"{g}{k}")
                    a = pe.matmul(lo, SILU_C[:, k, :], wt[:, 0:S], start=k == 0, stop=k == DK - 1)
                    b = pe.matmul(hi, SILU_C[:, k, :], wt[:, S:D], start=k == 0, stop=k == DK - 1)
                    if k < DK - 1:
                        b.then_inc(mod_block_used, 1)
                full_inc(a, f"{g}_lo")
                full_inc(b, f"{g}_hi")

            def modulation_turn(g, rows):
                pe.wait_ge(*is_free(f"{g}_lo"))
                pe.wait_ge(*is_free(f"{g}_hi"))
                out = take(f"{g}_t", 2 * DK)
                for k in range(DK):
                    last = pe.transpose(out[:, 2 * k:2 * k + 2], rows[0:2, k * P:(k + 1) * P],
                                        tab("ident")[0:2, 0:2])
                full_inc(last, f"{g}_t")

            pe.wait_ge(tables_in, 16)
            pe.wait_ge(squares, 1)
            sum_over("mem_sum", lambda k: SQ[:, k, 0:SM], DK, SM)
            pe.wait_ge(squares, 2)
            sum_over("ctx_sum", lambda k: SQ[:, k, SM:SM + SC], DK, SC)
            pe.wait_ge(squares, 3)
            sum_over("x_sum", lambda k: SQ[:, k, :], DK, S)
            pe.wait_ge(normed, 1)
            for i in range(2):
                project(f"kmem{i}", f"kmem{i}", lambda k: MEM[:, k, :], SM)
            head_sums(0, SM)
            head_sums(1, SM)
            pe.wait_ge(c_ready, 1)
            modulation("shift")
            modulation("scale")
            modulation_turn("shift", MODROW[0])
            out = take("vmem")
            wts = [loaded("vmem0"), loaded("vmem1")]
            for t in range(MT):
                for k in range(DK):
                    last = pe.matmul(out[:, t * SM:(t + 1) * SM], MEM[:, k, t * P:(t + 1) * P],
                                     wts[k // 4][:, (k % 4) * SM:(k % 4 + 1) * SM],
                                     start=k == 0, stop=k == DK - 1)
            full_inc(last, "vmem")
            modulation_turn("scale", MODROW[1])
            for i in range(CK):
                project(f"a{i}", f"a{i}", lambda k: U[:, k, :], each=(normed, 2) if i == 0 else None)
                project(f"g{i}", f"g{i}", lambda k: U[:, k, :])
            project("k", "kx", lambda k: U[:, k, :])
            pe.wait_ge(normed, 2 + DK)
            project("k", "kc", lambda k: CTX[:, k, :], SC)
            head_sums(2)
            rotate(0, "kx")
            head_sums(3, SC)
            wt = loaded("v")
            for name, tiles in (("v_lo", range(4)), ("v_hi", range(4, KT))):
                out = take(name, len(tiles) * P)
                for n, t in enumerate(tiles):
                    for k in range(DK):
                        src = (CTX[:, k, t * P:(t + 1) * P] if t < SC // P
                               else U[:, k, (t - SC // P) * P:(t - SC // P + 1) * P])
                        last = pe.matmul(out[:, n * P:(n + 1) * P], src, wt[:, k * P:(k + 1) * P],
                                         start=k == 0, stop=k == DK - 1)
                full_inc(last, name)
            for j in range(NQ):
                project(f"q{j}", f"q{j}", lambda k: U[:, k, :])
                head_sums(4 + j)
                rotate(1 + j, f"q{j}")
            for i in range(CK):
                project(f"zc{i}", f"zc{i}", lambda k: U[:, k, :])
            for j in range(NQ):
                project(f"za{j}", f"za{j}", lambda k: U[:, k, :])

            def turn(name, tiles, src):
                out = take(name, tiles * P)
                for t in range(tiles):
                    last = pe.transpose(out[:, t * P:(t + 1) * P], src[:, t * P:(t + 1) * P], tab("ident"))
                full_inc(last, name)

            def beside_attention(i):
                name = BESIDE_ATTENTION.get(i)
                if name == "gate_t":
                    modulation_turn("gate", MODROW[0])
                if name == "cmean":
                    pe.wait_ge(conv_out, CK)
                    sum_over("cmean", lambda k: CV[:, k, :], CK, S)
                if name == "cvar":
                    pe.wait_ge(conv_sq, 1)
                    sum_over("cvar", lambda k: SQ[:, k, :], CK, S)
                if name in [f"pw{n}" for n in range(CK)]:
                    n = int(name[2])
                    pe.wait_ge(conv_act, CK)
                    wt = loaded(f"pw{n // 2}")
                    out = take(name)
                    for k in range(CK):
                        at = (n % 2 * CK + k) * P
                        last = pe.matmul(out, wt[:, at:at + P], CV[:, k, :], start=k == 0, stop=k == CK - 1)
                    full_inc(last, name)

            modulation("gate")
            pe.wait_ge(k_ready, 1)
            pe.wait_ge(*is_free("kc"))
            pe.wait_ge(*is_free("v_hi"))
            for i in range(UNITS + AHEAD + 1):
                if i < UNITS:
                    j, h, qt = i // 8, i // 4 % 2, i % 4
                    pe.wait_ge(q_ready, j + 1)
                    s = take(f"s{i}")
                    q = QZ[:, h, j, qt * P:(qt + 1) * P]
                    pe.matmul(s[:, 0:S], q, KTT[:, 0:S], start=True, stop=True)
                    full_inc(pe.matmul(s[:, S:SKEYS], q, KTT[:, S:SKEYS], start=True, stop=True), f"s{i}")
                v = i - AHEAD
                if 0 <= v < UNITS:
                    pe.wait_ge(probs_scaled, v + 1)
                    turn(f"pt{v}", KT, PR[:, v % (AHEAD + 1), :])
                beside_attention(i)
                v = i - AHEAD - 1
                if v >= 0:
                    j, h, qt = v // 8, v // 4 % 2, v % 4
                    if v % 8 == 0:
                        o = take(f"o{j}")
                    pe.wait_ge(*is_free(f"pt{v}"))
                    for t in range(KT):
                        last = pe.matmul(o[h * DH:(h + 1) * DH, qt * P:(qt + 1) * P],
                                         VT[:, t, h * DH:(h + 1) * DH],
                                         PT[:, v % 2, t * P:(t + 1) * P], start=t == 0, stop=t == KT - 1)
                    if v % 8 == 7:
                        full_inc(last, f"o{j}")
            pe.wait_ge(*is_free(f"o{NQ - 1}"))
            pe.wait_ge(*is_free(f"pw{CK - 1}"))
            for m in range(DK):
                project(f"out{m}", f"out{m}", lambda k: CAT[:, k, :])

            sum_over("h1_sum", lambda k: SQ[:, k, :], DK, S, each=(res_squares, 1))
            project("wdad", "wdad", lambda k: U[:, k, :], each=(normed, 3 + DK))
            project("gd", "gd", lambda k: U[:, k, :])
            for i in range(2):
                project(f"qm{i}", f"qm{i}", lambda k: U[:, k, :])
                head_sums(8 + i)
            pe.wait_ge(*is_free("kmem1"))
            pe.wait_ge(*is_free("vmem"))
            for i in range(MUNITS + MAHEAD + 1):
                if i < MUNITS:
                    j, h, qt = i // 8, i // 4 % 2, i % 4
                    pe.wait_ge(*is_free(f"qm{j}"))
                    one(f"e{i}", QMZ[:, h, j, qt * P:(qt + 1) * P], KMEM[:, j, :], SM)
                v = i - MAHEAD
                if 0 <= v < MUNITS:
                    pe.wait_ge(probs_scaled, UNITS + v + 1)
                    turn(f"et{v}", MT, MPR[:, v % (MAHEAD + 1), :])
                v = i - MAHEAD - 1
                if v >= 0:
                    j, h, qt = v // 8, v // 4 % 2, v % 4
                    if v % 8 == 0:
                        o = take(f"mo{j}")
                    pe.wait_ge(*is_free(f"et{v}"))
                    for t in range(MT):
                        last = pe.matmul(o[h * DH:(h + 1) * DH, qt * P:(qt + 1) * P],
                                         VMEM[:, t, (2 * j + h) * DH:(2 * j + h + 1) * DH],
                                         MPT[:, v % 2, t * P:(t + 1) * P], start=t == 0, stop=t == MT - 1)
                    if v % 8 == 7:
                        full_inc(last, f"mo{j}")

            outs = {}

            def project_part(x, p, lo, hi):
                wt = loaded(f"{x}_{p}")
                if lo == 0:
                    outs[x] = take(f"{x}_{p}")
                for k in range(lo, hi):
                    last = pe.matmul(outs[x], wt[:, k * P:(k + 1) * P], U[:, k, :], start=k == 0, stop=k == DK - 1)
                if hi == DK:
                    full_inc(last, f"{x}_{p}")

            def low_rank(p):
                pe.wait_ge(low_used, 1)
                for x, src in (("w", TZ[:, 0, :]), ("A", TZ[:, 1, :])):
                    one(f"{x}_{p}", SV[:, LORA_AT + p * P:LORA_AT + (p + 1) * P], src)

            def kk_sum(p):
                pe.wait_ge(kk_sq, p + 1)
                one(f"kks_{p}", tab("heads"), HS[:, 0, :])

            def bonus_sum(p):
                pe.wait_ge(bonus_in, p + 1)
                one(f"bon_{p}", tab("heads"), T2)

            def gn_mean(p):
                pe.wait_ge(*is_free(f"y_{p}_{NG - 1}"))
                one(f"gm_{p}", tab("heads"), CAT[:, p, :])

            def gn_square(p):
                pe.wait_ge(gn_sq, p + 1)
                one(f"gv_{p}", tab("heads"), HS[:, 1, :])

            def gate_low_rank(p):
                pe.wait_ge(sig_out, sig_at["gd_sig"][0] + 1)
                one(f"gg_{p}", SV[:, G2_AT + p * P:G2_AT + (p + 1) * P], SGD)

            def four(name, *terms):
                out = take(name).rearrange("p (g t) -> p g t", g=G)
                for c in range(G):
                    for n, (stationary, moving) in enumerate(terms):
                        last = pe.matmul(out[:, c, :], stationary[:, c, :], moving[:, c, :],
                                         start=n == 0, stop=n == len(terms) - 1)
                full_inc(last, name)

            def part(x, g):
                return x[:, g * G:(g + 1) * G, :]

            for p in range(2):
                low_rank(p)
                for x in "krv"[:3 - p]:
                    project_part(x, p, 0, DK)
                kk_sum(p)
                if p == 0:
                    bonus_sum(0)
            for p in range(NP):
                pe.wait_ge(bd_ready, p + 1)
                pe.wait_ge(k_blocks, p + 1)
                pe.wait_ge(r_ready, p + 1)
                for x, a, b in (("nt", BBD, ABD), ("nn", ABD, BBD)):
                    for g in range(NG):
                        four(f"{x}_{p}_{g}", (part(a, g), part(b, g)))
                for x, a in (("ta", ABD), ("tb", BBD), ("tk", KBD), ("tv", VBD)):
                    if x == "tv":
                        pe.wait_ge(v_ready, p + 1)
                    for g in range(NG):
                        out = take(f"{x}_{p}_{g}").rearrange("p (g t) -> p g t", g=G)
                        for c in range(G):
                            last = pe.transpose(out[:, c, :], a[:, g * G + c, :], tab("ident"))
                        full_inc(last, f"{x}_{p}_{g}")
                for x, a, b in (("mak", KBD, ABD), ("mrb", BBD, RBD[p % 2]), ("mrk", KBD, RBD[p % 2])):
                    for g in range(NG):
                        four(f"{x}_{p}_{g}", (part(a, g), part(b, g)))
                prev = None
                for b in LEVELS:
                    for g in range(NG):
                        if prev is None:
                            pe.wait_ge(x_first, NG * p + g + 1)
                        else:
                            pe.wait_ge(*is_free(f"xt{prev}_{p}_{g}"))
                        four(f"xp{b}_{p}_{g}", (NT[g], XN[g]))
                    if p and b == LEVELS[0]:
                        gn_mean(p - 1)
                    if p and b == LEVELS[1]:
                        gn_square(p - 1)
                    if p and b == LEVELS[3]:
                        gate_low_rank(p - 1)
                    if p + 1 < NP and b == LEVELS[1]:
                        project_part("v", p + 1, 0, DK // 2)
                    if p + 1 < NP and b == LEVELS[2]:
                        bonus_sum(p + 1)
                    for g in range(NG):
                        pe.wait_ge(*is_free(f"xp{b}_{p}_{g}"))
                        if b != LEVELS[-1]:
                            four(f"xn{b}_{p}_{g}", (XT[g], XP[g]))
                        four(f"xt{b}_{p}_{g}", (XP[g], XT[g]))
                        if p + 1 < NP and b == LEVELS[1] and g == 0:
                            project_part("v", p + 1, DK // 2, DK)
                    prev = b
                for g in range(NG):
                    pe.wait_ge(*is_free(f"mak_{p}_{g}"))
                    pe.wait_ge(*is_free(f"tv_{p}_{g}"))
                    four(f"mv_{p}_{g}", (MAK[g], TV[g]))
                for g in range(NG):
                    pe.wait_ge(*is_free(f"xt{prev}_{p}_{g}"))
                    pe.wait_ge(*is_free(f"ta_{p}_{g}"))
                    four(f"w_{p}_{g}", (XT[g], TA[g]))
                for g in range(NG):
                    pe.wait_ge(*is_free(f"mv_{p}_{g}"))
                    four(f"u_{p}_{g}", (XT[g], MV[g]))
                for g in range(NG):
                    pe.wait_ge(*is_free(f"w_{p}_{g}"))
                    pe.wait_ge(*is_free(f"tb_{p}_{g}"))
                    four(f"gt_{p}_{g}", (WB[g], TBT[g]))
                for g in range(NG):
                    pe.wait_ge(*is_free(f"mrb_{p}_{g}"))
                    four(f"rp_{p}_{g}", (WB[g], MRB[g]))
                for g in range(NG):
                    pe.wait_ge(*is_free(f"u_{p}_{g}"))
                    pe.wait_ge(*is_free(f"tk_{p}_{g}"))
                    four(f"f_{p}_{g}", (TBT[g], UB[g]), (TK[g], TV[g]))
                def outputs(g):
                    pe.wait_ge(*is_free(f"rp_{p}_{g}"))
                    pe.wait_ge(*is_free(f"mrk_{p}_{g}"))
                    four(f"y_{p}_{g}", (H[g], RP[g]), (UB[g], MRB[g]), (TV[g], MRK[g]))

                if p + 2 < NP:
                    low_rank(p + 2)
                for n in range(NC - 1):
                    g, c = divmod(n, G)
                    if c == 0:
                        pe.wait_ge(*is_free(f"gt_{p}_{g}"))
                    if n:
                        pe.wait_ge(*is_free(f"h_{p}_{n - 1}"))
                    else:
                        pe.wait_ge(zeroed, 10)
                    one(f"h_{p}_{n}", GT[g][:, c, :], H[g][:, c, :], P)
                    if n == G:
                        outputs(0)
                    if p + 2 < NP:
                        for x, lo, hi in BESIDE_CHAIN[n]:
                            project_part(x, p + 2, lo, hi)
                pe.wait_ge(*is_free(f"h_{p}_{NC - 2}"))
                outputs(1)
                if p + 2 < NP:
                    kk_sum(p + 2)
            gn_mean(NP - 1)
            gn_square(NP - 1)
            gate_low_rank(NP - 1)

            def split_product(block_name, out, high, low, order=range(DK), first=True, last=True, each=None):
                q = SPLIT_AT[block_name]
                pe.wait_ge(w_high, q + 1)
                pe.wait_ge(w_low, q + 1)
                for n, k in enumerate(order):
                    if each:
                        each(n, k)
                    wh, wl = (w[:, q % 2, k * P:(k + 1) * P] for w in (WH, WL))
                    pe.matmul(out, wh, high(k), start=first and n == 0, stop=False)
                    pe.matmul(out, wh, low(k), start=False, stop=False)
                    ins = pe.matmul(out, wl, high(k), start=False, stop=last and n == DK - 1)
                return ins

            def mixed_tile(n, k):
                pe.wait_ge(cat_low, n + 1)

            def normed_tile(n, k):
                pe.wait_ge(u_low, n + 1)

            for m in range(DK):
                full_inc(split_product(f"mix{m}", take(f"mix{m}"), lambda k: CATH[:, k, :], lambda k: CATL[:, k, :],
                                       order=CAT_ORDER, each=mixed_tile if m == 0 else None), f"mix{m}")
            sum_over("h2_sum", lambda k: SQ2[:, k, :], DK, S, each=(res_squares, 1 + DK))
            for h in range(HALVES):
                for m in range(h * FH_TILES, (h + 1) * FH_TILES):
                    full_inc(split_product(f"up{m}", take(f"up{m}"), lambda k: UH[:, k, :], lambda k: UL[:, k, :],
                                           each=normed_tile if m == 0 else None), f"up{m}")
                for m in range(DK):
                    out = take(f"down{h}_{m}")
                    for b in range(DOWN_BLOCKS):
                        def hidden_tile(n, k):
                            pe.wait_ge(h_low, h * FH_TILES + b * DK + n + 1)

                        ins = split_product(f"down{h}_{m}_{b}", out, lambda k: FH[:, b * DK + k, :],
                                            lambda k: FL[:, b * DK + k, :], first=b == 0, last=b == DOWN_BLOCKS - 1,
                                            each=hidden_tile if m == 0 else None)
                        if b < DOWN_BLOCKS - 1:
                            ins.then_inc(half_used, 1)
                    full_inc(ins, f"down{h}_{m}")

        @block.scalar
        def _(act):
            steps = [0]

            def link(ins):
                steps[0] += 1
                ins.then_inc(act_step, 1)
                act.wait_ge(act_step, steps[0])

            def rms(name, out, w, scale, eps, done):
                act.wait_ge(*is_full(name))
                free_inc(act.activation(out, bank(name, w), ACT.Ln, bias=eps, scale=scale), name)
                act.wait_ge(*is_free(name))
                act.activation(out, out, ACT.Exp, scale=-0.5).then_inc(done, 1)

            def sigmoid(name, src, out=None, bias=0.0, scale=-1.0, rows=slice(0, P)):
                n, exp_done = sig_at[name]
                e = SG[rows, n % 2, :]
                if n >= 2 and sigmoids[n - 2][2] is not None:
                    act.wait_ge(*sigmoids[n - 2][2])
                act.activation(e, src, ACT.Exp, bias=bias, scale=scale).then_inc(exp_done[0], 1)
                act.wait_ge(sig_den, n + 1)
                link(act.activation(e, e, ACT.Ln))
                act.activation(e if out is None else out, e, ACT.Exp, scale=-1.0).then_inc(sig_out, 1)

            def head_norm(name, w=S, weight=None, rot_before=None):
                n = head_at[name]
                act.wait_ge(*is_full(name))
                act.activation(HS[:, n % 2, 0:w], bank(name, w), ACT.Square).then_inc(head_sq, 1)
                if weight is not None:
                    if rot_before is not None:
                        act.wait_ge(*is_free(rot_before))
                    free_inc(act.activation(QW[:, 0:w], bank(name, w), ACT.Copy, scale=weight), name)
                if n >= 2:
                    act.wait_ge(*heads[n - 2][1])
                rms(f"hs{n}", HR[:, n % 2, 0:w], w, 1.0 / DH, EPS, head_rs)

            def copy_out(name, out, w=None, before=None):
                act.wait_ge(*is_full(name))
                free_inc(act.activation(out, bank(name, w) if len(out.shape) == 2 else bank4(name), ACT.Copy), name)

            act.preload_act_table_set("natural_log_exp_and_others")
            act.wait_ge(mem_in, 16)
            act.activation(SQ[:, :, 0:SM], MEM, ACT.Square).then_inc(squares, 1)
            act.wait_ge(ctx_in, 16)
            act.activation(SQ[:, :, SM:SM + SC], CTX, ACT.Square).then_inc(squares, 1)
            rms("mem_sum", RS[:, 0, 0:SM], SM, 1.0 / D, EPS, rstd)
            rms("ctx_sum", RS[:, 1, 0:SC], SC, 1.0 / D, EPS, rstd)
            act.wait_ge(x_in, 16)
            act.activation(SQ, X[:], ACT.Square).then_inc(squares, 1)
            act.wait_ge(normed, 1)
            rms("x_sum", RS[:, 0, :], S, 1.0 / D, EPS, rstd)
            act.wait_ge(small_in, 16)
            act.activation(SILU_E, cols("cc", 0, 2 * DK), ACT.Exp, scale=-1.0).then_inc(c_exp, 1)
            act.wait_ge(c_den, 1)
            link(act.activation(SILU_E, SILU_E, ACT.Ln))
            act.activation(SILU_E, SILU_E, ACT.Exp, scale=-1.0).then_inc(c_sig, 1)
            head_norm("kmem0", SM)
            head_norm("kmem1", SM)

            def modulation_rows(g, rows):
                for i, h in enumerate(("lo", "hi")):
                    act.wait_ge(*is_full(f"{g}_{h}"))
                    free_inc(act.activation(rows[0:2, i * S:(i + 1) * S], bank(f"{g}_{h}", S, slice(0, 2)),
                                            ACT.Copy), f"{g}_{h}")

            modulation_rows("shift", MODROW[0])
            modulation_rows("scale", MODROW[1])
            copy_out("vmem", VMEM.rearrange("p a b -> p (a b)"))
            for i in range(CK):
                act.wait_ge(*is_full(f"g{i}"))
                sigmoid(f"g{i}", bank(f"g{i}"))
            head_norm("kx", weight=col("kn"))
            head_norm("kc", SC)
            flat = VT.rearrange("p a b -> p (a b)")
            copy_out("v_lo", flat[:, 0:4 * P], 4 * P)
            copy_out("v_hi", flat[:, 4 * P:SKEYS], SKEYS - 4 * P)
            for j in range(NQ):
                head_norm(f"q{j}", weight=col("qn"), rot_before=f"rot{j}")
            for name in [f"zc{i}" for i in range(CK)] + [f"za{j}" for j in range(NQ)]:
                act.wait_ge(*is_full(name))
                sigmoid(name, bank(name))

            def exp_scores(i, base, s_name, t_name, probs, n, w):
                act.wait_ge(negmax, base + i + 1)
                if i >= n:
                    act.wait_ge(*is_full(f"{t_name}{i - n}"))
                free_inc(act.activation(probs[:, i % n, :], bank(f"{s_name}{i}", w), ACT.Exp,
                                        bias=NEGMAX[:, i % 4:i % 4 + 1], scale=DH ** -0.5,
                                        accum_out=ROWSUM[:, i % 4:i % 4 + 1]), f"{s_name}{i}")

            act.wait_ge(q_ready, NQ)
            modulation_rows("gate", MODROW[0])
            for i in range(UNITS + AHEAD):
                if i < UNITS:
                    exp_scores(i, 0, "s", "pt", PR, AHEAD + 1, SKEYS)
                if i >= AHEAD:
                    copy_out(f"pt{i - AHEAD}", PT[:, i % 2, :], SKEYS)
                if i == 5:
                    act.wait_ge(*is_free("cmean"))
                    act.activation(SQ[:, 0:CK, :], CV, ACT.Square).then_inc(conv_sq, 1)
                if i == 7:
                    rms("cvar", RS[:, 1, :], S, 1.0 / (CK * P), EPS, conv_rs)
                if 12 <= i < 12 + CK:
                    act.wait_ge(conv_ln, i - 11)
                    sigmoid(f"conv{i - 12}", CV[:, i - 12, :])

            for m in range(DK):
                act.wait_ge(*is_free(f"out{m}"))
                act.activation(SQ[:, m, :], X[:, m, :], ACT.Square).then_inc(res_squares, 1)
            rms("h1_sum", RS[:, 0, :], S, 1.0 / D, EPS, rstd)

            def shift_start(name, n, out):
                act.wait_ge(*is_full(name))
                act.activation(out, bank(name), ACT.Copy, scale=MU1[:, n:n + 1]).then_inc(partial, 1)

            act.wait_ge(consts_ready, 1)
            shift_start("wdad", MU_WDAD, T1)
            shift_start("gd", MU_GD, T2)
            act.wait_ge(*is_free("wdad"))
            sigmoid("wd", T1[0:DH, :], scale=-2.0, rows=slice(0, DH))
            act.wait_ge(*is_free("gd"))
            sigmoid("gd_sig", T2, out=SGD)
            head_norm("qm0")
            head_norm("qm1")
            for i in range(MUNITS + MAHEAD):
                if i < MUNITS:
                    exp_scores(i, UNITS, "e", "et", MPR, MAHEAD + 1, SM)
                if i >= MAHEAD:
                    copy_out(f"et{i - MAHEAD}", MPT[:, (i - MAHEAD) % 2, :], SM)

            def pair_inputs(p):
                if p:
                    act.wait_ge(bd_ready, p)
                    act.wait_ge(r_ready, p)
                for i, (x, out) in enumerate((("w", EL), ("A", AV))):
                    act.wait_ge(*is_full(f"{x}_{p}"))
                    sigmoid(f"{x}_{p}", bank(f"{x}_{p}"), out=out, bias=NEG[:, i * NP + p:i * NP + p + 1])
                shift_start(f"k_{p}", MU_PAIR + 3 * p, K0)
                act.wait_ge(scan_done, p + 1)
                act.activation(T1, T1, ACT.Exp, scale=-DECAY)
                link(act.activation(EL, LG, ACT.Exp, scale=-DECAY))
                act.activation(LG, LG, ACT.Exp, scale=DECAY).then_inc(exps_done, 1)
                act.wait_ge(*is_free(f"k_{p}"))
                if p:
                    act.wait_ge(*is_full(f"kks_{p - 1}"))
                act.activation(HS[:, 0, :], K0, ACT.Square, scale=col("k_k", p)).then_inc(kk_sq, 1)
                shift_start(f"r_{p}", MU_PAIR + 3 * p + 1, R0)
                act.wait_ge(*is_free(f"kks_{p}"))
                link(act.activation(HR[:, 0, :], HR[:, 0, :], ACT.Ln, scale=KK_SCALE))
                act.activation(HR[:, 0, :], HR[:, 0, :], ACT.Exp, scale=-0.5,
                               bias=float(0.5 * np.log(KK_SCALE))).then_inc(kk_rs, 1)

            def pair_values(p):
                if p:
                    act.wait_ge(v_ready, p)
                shift_start(f"v_{p}", MU_PAIR + 3 * p + 2, V0)
                act.wait_ge(*is_free(f"v_{p}"))
                if p:
                    act.wait_ge(*is_full(f"tv_{p - 1}_{NG - 1}"))
                else:
                    act.wait_ge(zeroed, 9)
                v3 = V0.rearrange("p (c t) -> p c t", c=NC)
                act.activation(VBD[0:DH, :, 0:DH], v3[0:DH], ACT.Copy)
                act.activation(VBD[DH:P, :, DH:P], v3[DH:P], ACT.Copy).then_inc(v_ready, 1)

            def group_norm(p):
                act.wait_ge(*is_free(f"gm_{p}"))
                act.activation(HS[:, 1, :], CAT[:, p, :], ACT.Square).then_inc(gn_sq, 1)
                rms(f"gv_{p}", HR[:, 1, :], S, 1.0 / DH, GN_EPS, gn_rs)

            pair_inputs(0)
            pair_values(0)
            pair_inputs(1)
            for p in range(NP):
                for x, out in (("ta", TA), ("tb", TBT), ("tk", TK), ("tv", TV)):
                    for g in range(NG):
                        copy_out(f"{x}_{p}_{g}", out[g])
                if p:
                    group_norm(p - 1)
                if p + 1 < NP:
                    pair_values(p + 1)
                for x, out in (("mv", MV), ("w", WB), ("u", UB)):
                    for g in range(NG):
                        copy_out(f"{x}_{p}_{g}", out[g])
                if p + 2 < NP:
                    pair_inputs(p + 2)

            def mixed_high(k):
                act.activation(CATH[:, k, :], CAT[:, k, :], ACT.Copy).then_inc(cat_high, 1)

            act.wait_ge(*is_full(f"mrk_{NP - 1}_{NG - 1}"))
            for k in CAT_ORDER[:-1]:
                act.wait_ge(*(is_free(f"gg_{k}") if k < NP else is_free(f"mo{k - NP}")))
                mixed_high(k)
            group_norm(NP - 1)

            def weights_high(q):
                if q >= 2:
                    act.wait_ge(*split_used(q - 2))
                else:
                    act.wait_ge(*is_full(f"y_{NP - 1}_{NG - 1}"))
                b = BLOCK_AT[SPLIT[q]]
                act.wait_ge(slot[b % RING], 16 * (b // RING + 1))
                act.activation(WH[:, q % 2, :], ring[:, b % RING, :], ACT.Copy).then_inc(w_high, 1)

            weights_high(0)
            act.wait_ge(*is_free(f"gg_{NP - 1}"))
            mixed_high(CAT_ORDER[-1])
            for q in range(len(SPLIT)):
                name = SPLIT[q - 1] if q else ""
                if name.startswith("mix"):
                    m = int(name[3:])
                    act.wait_ge(*is_free(name))
                    act.activation(SQ2[:, m, :], X[:, m, :], ACT.Square).then_inc(res_squares, 1)
                    if m == DK - 1:
                        rms("h2_sum", RS[:, 1, :], S, 1.0 / D, EPS, rstd)
                        for k in range(DK):
                            act.wait_ge(normed, 3 + 2 * DK + k)
                            act.activation(UH[:, k, :], U[:, k, :], ACT.Copy).then_inc(u_high, 1)
                if name.startswith("up"):
                    m = int(name[2:])
                    t = m % FH_TILES
                    act.wait_ge(*is_full(name))
                    free_inc(act.activation(FS[:, t, :], bank(name), ACT.Relu), name)
                    act.wait_ge(*is_free(name))
                    act.activation(FS[:, t, :], FS[:, t, :], ACT.Square).then_inc(h_relu, 1)
                    act.wait_ge(h_relu, m + 1)
                    act.activation(FH[:, t, :], FS[:, t, :], ACT.Copy).then_inc(h_high, 1)
                if q + 1 < len(SPLIT):
                    weights_high(q + 1)

        @block.vector
        def _(vec):
            steps = [0]

            def link(ins):
                steps[0] += 1
                ins.then_inc(vec_step, 1)
                vec.wait_ge(vec_step, steps[0])

            def scaled_product(out, a, scalar, b, op=ALU.mult):
                return vec.scalar_tensor_tensor(out=out, in0=a, scalar=scalar, in1=b, op0=op, op1=ALU.mult)

            def scaled_sum(out, a, scalar, b, op=ALU.mult):
                return vec.scalar_tensor_tensor(out=out, in0=a, scalar=scalar, in1=b, op0=op, op1=ALU.add)

            def denominator(name, rows=slice(0, P)):
                n, exp_done = sig_at[name]
                vec.wait_ge(*exp_done)
                e = SG[rows, n % 2, :]
                vec.tensor_scalar(e, e, SIG_MOST, 1.0, ALU.min, ALU.add).then_inc(sig_den, 1)

            def sigmoid_of(name, rows=slice(0, P)):
                n, _ = sig_at[name]
                vec.wait_ge(sig_out, n + 1)
                return SG[rows, n % 2, :]

            vec.wait_ge(small_in, 16)
            link(vec.tensor_scalar(NEG, cols("w0", 0, 2 * NP), -1.0, None, ALU.mult))
            link(vec.tensor_scalar(KA1, cols("k_a", 0, NP), -1.0, 1.0, ALU.mult, ALU.add))
            vec.tensor_scalar(MU1, cols("mu", 0, 20), -1.0, 1.0, ALU.mult, ALU.add).then_inc(consts_ready, 1)
            vec.wait_ge(rstd, 1)
            for k in range(DK):
                ins = scaled_product(MEM[:, k, :], MEM[:, k, :], col("g_mem", k), RS[:, 0, 0:SM])
            ins.then_inc(normed, 1)
            vec.wait_ge(c_exp, 1)
            vec.tensor_scalar(SILU_E, SILU_E, SIG_MOST, 1.0, ALU.min, ALU.add).then_inc(c_den, 1)
            vec.wait_ge(rstd, 2)
            for k in range(DK):
                vec.tensor_tensor(CTX[:, k, :], CTX[:, k, :], RS[:, 1, 0:SC], ALU.mult)
            vec.wait_ge(c_sig, 1)
            vec.tensor_tensor(SILU_C, cols("cc", 0, 2 * DK).rearrange("p (k w) -> p k w", k=DK),
                              SILU_E.rearrange("p (k w) -> p k w", k=DK), ALU.mult).then_inc(c_ready, 1)
            vec.wait_ge(rstd, 3)
            for k in range(DK):
                ins = vec.tensor_tensor(U[:, k, :], X[:, k, :], RS[:, 0, :], ALU.mult)
            link(ins)
            for i in range(2):
                vec.wait_ge(head_rs, i + 1)
                free_inc(scaled_product(KMEM[:, i, :], bank(f"kmem{i}", SM), col("mkn"), HR[:, i, 0:SM]), f"kmem{i}")

            def modulation_columns(g, i, bias):
                vec.wait_ge(*is_full(f"{g}_t"))
                b = cols(bias, 0, DK)[:, :, None].to_broadcast([P, DK, 2])
                free_inc(vec.tensor_tensor(MOD[:, i], bank(f"{g}_t", 2 * DK).rearrange("p (k w) -> p k w", k=DK),
                                           b, ALU.add), f"{g}_t")

            modulation_columns("shift", 0, "b_shift")
            modulation_columns("scale", 1, "b_scale")
            vec.wait_ge(*is_free("scale_t"))
            link(scaled_product(MOD[:, 1], MOD[:, 1], 1.0,
                                cols("norm_w", 0, DK)[:, :, None].to_broadcast([P, DK, 2]), ALU.add))
            for k in range(DK):
                vec.tensor_scalar(U[:, k, :], U[:, k, :], MOD[:, 1, k, 0:1], MOD[:, 0, k, 0:1], ALU.mult, ALU.add
                                  ).then_inc(normed, 1)
            for k in range(DK):
                ins = vec.tensor_scalar(CTX[:, k, :], CTX[:, k, :], MOD[:, 1, k, 1:2], MOD[:, 0, k, 1:2],
                                        ALU.mult, ALU.add)
            ins.then_inc(normed, 1)
            vec.wait_ge(zeroed, 1)
            def glu(i):
                denominator(f"g{i}")
                s = sigmoid_of(f"g{i}")
                vec.wait_ge(*is_full(f"a{i}"))
                free_inc(vec.tensor_tensor(GLU[:, i, PAD:PAD + S], bank(f"a{i}"), s, ALU.mult), f"a{i}")

            def convolve(i, lo, hi):
                vec.wait_ge(*is_free(f"a{i}"))
                sums = (CV[:, i, :], CT)
                for t in range(lo, hi):
                    w = col("conv_w", i * TAPS + t)
                    src = GLU[:, i, t:t + S]
                    if t == 1 and i:
                        vec.wait_ge(conv_out, i)
                    if t >= 2:
                        vec.wait_ge(vec_step, steps[0] - 1)
                    if t == 0:
                        ins = vec.tensor_scalar(sums[0], src, w, col("conv_b", i), ALU.mult, ALU.add)
                    elif t == 1:
                        ins = vec.tensor_scalar(sums[1], src, w, None, ALU.mult)
                    else:
                        ins = scaled_sum(sums[t % 2], src, w, sums[t % 2])
                    ins.then_inc(vec_step, 1)
                    steps[0] += 1
                if hi == TAPS:
                    vec.wait_ge(vec_step, steps[0])
                    vec.tensor_tensor(CV[:, i, :], CV[:, i, :], CT, ALU.add).then_inc(conv_out, 1)

            glu(0)
            convolve(0, 0, 20)
            glu(1)
            convolve(0, 20, TAPS)
            convolve(1, 0, 10)
            glu(2)
            convolve(1, 10, 25)
            glu(3)
            convolve(1, 25, TAPS)

            def rotary(n, rs):
                link(vec.tensor_tensor(T1, QW[:], tab("cos"), ALU.mult))
                vec.wait_ge(*is_full(f"rot{n}"))
                free_inc(vec.tensor_tensor(T2, bank(f"rot{n}"), tab("sin"), ALU.mult), f"rot{n}")
                vec.wait_ge(*is_free(f"rot{n}"))
                link(vec.tensor_tensor(T1, T1, T2, ALU.add))
                vec.wait_ge(head_rs, rs + 1)

            vec.wait_ge(*is_free("kx"))
            rotary(0, 2)
            vec.tensor_tensor(KTT[:, SC:SKEYS], T1, HR[:, 0, :], ALU.mult).then_inc(k_ready, 1)
            vec.wait_ge(head_rs, 4)
            free_inc(scaled_product(KTT[:, 0:SC], bank("kc", SC), col("kn"), HR[:, 1, 0:SC]), "kc")
            vec.wait_ge(zeroed, 2)
            convolve(2, 0, 14)
            for j in range(NQ):
                vec.wait_ge(*((q_ready, j) if j else (k_ready, 1)))
                vec.wait_ge(*is_free(f"q{j}"))
                rotary(1 + j, 4 + j)
                vec.tensor_tensor(QZ[0:DH, 0, j, :], T1[0:DH, :], HR[0:DH, j % 2, :], ALU.mult)
                vec.tensor_tensor(QZ[DH:P, 1, j, :], T1[DH:P, :], HR[DH:P, j % 2, :], ALU.mult).then_inc(q_ready, 1)
                convolve(2, 14 + 4 * j, min(18 + 4 * j, 30))
            convolve(2, 30, TAPS)
            for z, out, n in (("zc", ZC, CK), ("za", ZA, NQ)):
                for i in range(n):
                    at = i if z == "zc" else CK + i
                    convolve(3, 4 * at, min(4 * at + 4, TAPS))
                    denominator(f"{z}{i}")
                    s = sigmoid_of(f"{z}{i}")
                    free_inc(vec.tensor_tensor(out[:, i, :], bank(f"{z}{i}"), s, ALU.mult), f"{z}{i}")

            def row_max(i, s_name, w):
                vec.wait_ge(*is_full(f"{s_name}{i}"))
                one = slice(i % 4, i % 4 + 1)
                link(vec.tensor_reduce(ROWMAX[:, one], bank(f"{s_name}{i}", w), AX, ALU.max))
                vec.tensor_scalar(NEGMAX[:, one], ROWMAX[:, one], -DH ** -0.5, None, ALU.mult).then_inc(negmax, 1)

            def divide(i, s_name, probs, n):
                vec.wait_ge(*is_free(f"{s_name}{i}"))
                one = slice(i % 4, i % 4 + 1)
                link(vec.reciprocal(ROWINV[:, one], ROWSUM[:, one]))
                vec.tensor_scalar(probs[:, i % n, :], probs[:, i % n, :], ROWINV[:, one], None,
                                  ALU.mult).then_inc(probs_scaled, 1)

            def gated_heads(j):
                vec.wait_ge(*is_full(f"o{j}"))
                free_inc(vec.tensor_tensor(CAT[:, j, :], bank(f"o{j}"), ZA[:, j, :], ALU.mult), f"o{j}")

            vec.wait_ge(*is_free("za3"))
            for i in range(UNITS + 1):
                if i < UNITS:
                    row_max(i, "s", SKEYS)
                if i:
                    divide(i - 1, "s", PR, AHEAD + 1)
                if i >= 8 + AHEAD + 1 and (i - AHEAD - 1) % 8 == 0:
                    gated_heads((i - AHEAD - 1) // 8 - 1)
                if i == 4:
                    modulation_columns("gate", 2, "b_gate")
                if i == 5:
                    vec.wait_ge(*is_full("cmean"))
                    for n in range(CK):
                        ins = scaled_sum(CV[:, n, :], bank("cmean"), -1.0 / (CK * P), CV[:, n, :])
                    free_inc(ins, "cmean")
                if 8 <= i < 8 + CK:
                    n = i - 8
                    vec.wait_ge(conv_rs, 1)
                    link(scaled_product(CV[:, n, :], CV[:, n, :], col("ln_w", n), RS[:, 1, :]))
                    vec.tensor_scalar(CV[:, n, :], CV[:, n, :], col("ln_b", n), None, ALU.add).then_inc(conv_ln, 1)
                if 13 <= i < 13 + CK:
                    n = i - 13
                    denominator(f"conv{n}")
                    s = sigmoid_of(f"conv{n}")
                    vec.tensor_tensor(CV[:, n, :], CV[:, n, :], s, ALU.mult).then_inc(conv_act, 1)
                if 21 <= i < 21 + CK:
                    n = i - 21
                    vec.wait_ge(*is_full(f"pw{n}"))
                    free_inc(scaled_product(CAT[:, NQ + n, :], bank(f"pw{n}"), col("b_pw", n), ZC[:, n, :], ALU.add),
                             f"pw{n}")
            gated_heads(NQ - 1)
            vec.wait_ge(*is_free("gate_t"))
            for m in range(DK):
                vec.wait_ge(*is_full(f"out{m}"))
                free_inc(scaled_sum(X[:, m, :], bank(f"out{m}"), MOD[:, 2, m, 0:1], X[:, m, :]), f"out{m}")

            def normalise(n, row, gain):
                vec.wait_ge(rstd, n)
                for k in range(DK):
                    scaled_product(U[:, k, :], X[:, k, :], col(gain, k), RS[:, row, :]).then_inc(normed, 1)

            normalise(4, 0, "g_mix")

            def shift_end(name, n, m, out):
                vec.wait_ge(partial, n)
                return scaled_sum(out[:, 1:S], bank(name)[:, 0:S - 1], col("mu", m), out[:, 1:S])

            free_inc(shift_end("wdad", 1, MU_WDAD, T1), "wdad")
            vec.wait_ge(*is_free("wdad"))
            vec.wait_ge(zeroed, 3)
            vec.tensor_copy(TZ[DH:P, 1, :], T1[DH:P, :])
            free_inc(shift_end("gd", 2, MU_GD, T2), "gd")
            denominator("wd", slice(0, DH))
            s = sigmoid_of("wd", slice(0, DH))
            vec.tensor_scalar(TZ[0:DH, 0, :], s, 2.0, -1.0, ALU.mult, ALU.add).then_inc(low_used, 1)
            denominator("gd_sig")
            vec.wait_ge(zeroed, 4)
            for i in range(2):
                vec.wait_ge(head_rs, 9 + i)
                scaled_product(QMZ[0:DH, 0, i, :], bank(f"qm{i}", S, slice(0, DH)), col("mqn", 0, slice(0, DH)),
                               HR[0:DH, i, :])
                free_inc(scaled_product(QMZ[DH:P, 1, i, :], bank(f"qm{i}", S, slice(DH, P)),
                                        col("mqn", 0, slice(DH, P)), HR[DH:P, i, :]), f"qm{i}")

            def memory_heads(j):
                vec.wait_ge(*is_full(f"mo{j}"))
                free_inc(vec.tensor_copy(CAT[:, NP + j, :], bank(f"mo{j}")), f"mo{j}")

            for i in range(MUNITS + 1):
                if i < MUNITS:
                    row_max(i, "e", SM)
                if i:
                    divide(i - 1, "e", MPR, MAHEAD + 1)
                if i == 8 + MAHEAD + 1:
                    memory_heads(0)
            memory_heads(1)

            def pair_input(p, x):
                i = "krv".index(x)
                free_inc(shift_end(f"{x}_{p}", 3 + 3 * p + i, MU_PAIR + 3 * p + i, (K0, R0, V0)[i]), f"{x}_{p}")

            def blocks_of(out, make):
                a = make(out[0:DH, :, 0:DH], slice(0, DH))
                return make(out[DH:P, :, DH:P], slice(DH, P))

            def chunks(x, rows):
                return x[rows, :].rearrange("p (c t) -> p c t", c=NC)

            def running_sums(p):
                vec.wait_ge(sig_out, sig_at[f"w_{p}"][0] + 1)
                if p:
                    vec.wait_ge(k_blocks, p)
                link(vec.tensor_tensor_scan(LG, tab("reset"), EL, 0.0, ALU.mult, ALU.add))
                vec.tensor_tensor(T1, LG, EL, ALU.subtract).then_inc(scan_done, 1)

            def changed_key(p):
                vec.wait_ge(sig_out, sig_at[f"A_{p}"][0] + 1)
                link(vec.tensor_scalar(QW[:], AV, col("k_a", p), KA1[:, p:p + 1], ALU.mult, ALU.add))
                vec.wait_ge(*is_free(f"k_{p}"))
                link(vec.tensor_tensor(QW[:], QW[:], K0, ALU.mult))
                vec.wait_ge(*is_free(f"r_{p}"))
                scaled_product(T2, R0, col("r_k", p), QW[:]).then_inc(bonus_in, 1)

            def least_norm(p):
                vec.wait_ge(*is_full(f"kks_{p}"))
                free_inc(vec.tensor_scalar(HR[:, 0, :], bank(f"kks_{p}"), KK_LEAST, None, ALU.max), f"kks_{p}")

            def bonus(p):
                vec.wait_ge(*is_free(f"v_{p}"))
                if p >= 2:
                    vec.wait_ge(gn_done, p - 1)
                vec.wait_ge(*is_full(f"bon_{p}"))
                free_inc(vec.tensor_tensor(BV[p % 2], bank(f"bon_{p}"), V0, ALU.mult), f"bon_{p}")

            def blocks_r(p):
                vec.wait_ge(exps_done, p + 1)
                vec.tensor_copy(ELC[p % 2], EL[:, C - 1:S:C])
                vec.wait_ge(zeroed, 9 if p == 0 else 11)
                if p >= 2:
                    vec.wait_ge(*is_full(f"rp_{p - 2}_{NG - 1}"))
                blocks_of(RBD[p % 2], lambda o, r: vec.tensor_tensor(o, chunks(R0, r), chunks(EL, r), ALU.mult)
                          ).then_inc(r_ready, 1)

            def unit_key(p):
                vec.wait_ge(kk_rs, p + 1)
                scaled_product(KKN, K0, col("k_k", p), HR[:, 0, :]).then_inc(key_step, 1)

            def blocks_a(p):
                vec.wait_ge(key_step, 3 * p + 1)
                if p:
                    vec.wait_ge(*is_full(f"mrk_{p - 1}_{NG - 1}"))
                blocks_of(ABD, lambda o, r: vec.scalar_tensor_tensor(
                    out=o, in0=chunks(KKN, r), scalar=-1.0, in1=chunks(T1, r), op0=ALU.mult, op1=ALU.mult)
                          ).then_inc(key_step, 1)

            def blocks_b(p):
                vec.wait_ge(key_step, 3 * p + 2)
                vec.tensor_tensor(KKN, KKN, AV, ALU.mult).then_inc(key_step, 1)
                vec.wait_ge(key_step, 3 * p + 3)
                blocks_of(BBD, lambda o, r: vec.tensor_tensor(o, chunks(KKN, r), chunks(LG, r), ALU.mult)
                          ).then_inc(bd_ready, 1)

            def gn_centre(p):
                vec.wait_ge(*is_full(f"gm_{p}"))
                free_inc(scaled_sum(CAT[:, p, :], bank(f"gm_{p}"), -1.0 / DH, CAT[:, p, :]), f"gm_{p}")

            def gn_finish(p):
                o = CAT[:, p, :]
                vec.wait_ge(gn_rs, p + 1)
                link(scaled_product(o, o, col("lnx_g", p), HR[:, 1, :]))
                scaled_sum(o, o, col("lnx_b", p), BV[p % 2], ALU.add).then_inc(gn_done, 1)

            def gate(p):
                o = CAT[:, p, :]
                vec.wait_ge(gn_done, p + 1)
                vec.wait_ge(*is_full(f"gg_{p}"))
                free_inc(vec.tensor_tensor(o, bank(f"gg_{p}"), o, ALU.mult), f"gg_{p}")

            def mixed_low(n):
                k = CAT_ORDER[n]
                vec.wait_ge(cat_high, n + 1)
                vec.tensor_tensor(CATL[:, k, :], CAT[:, k, :], CATH[:, k, :].bitcast(F32), ALU.subtract
                                  ).then_inc(cat_low, 1)

            def weights_low(q):
                b = BLOCK_AT[SPLIT[q]]
                vec.wait_ge(w_high, q + 1)
                vec.tensor_tensor(WL[:, q % 2, :], ring[:, b % RING, :], WH[:, q % 2, :].bitcast(F32), ALU.subtract
                                  ).then_inc(w_low, 1)

            for p in range(2):
                denominator(f"w_{p}")
                denominator(f"A_{p}")
                running_sums(p)
                pair_input(p, "k")
                pair_input(p, "r")
                changed_key(p)
                least_norm(p)
                if p == 0:
                    pair_input(0, "v")
                    bonus(0)
                    blocks_r(0)
                    unit_key(0)
                    blocks_a(0)
                    blocks_b(0)
                else:
                    blocks_r(1)
            for p in range(NP):
                for g in range(NG):
                    vec.wait_ge(*is_full(f"nt_{p}_{g}"))
                    free_inc(vec.tensor_tensor(NT[g], bank4(f"nt_{p}_{g}"), tab4("before"), ALU.mult), f"nt_{p}_{g}")
                for g in range(NG):
                    vec.wait_ge(*is_full(f"nn_{p}_{g}"))
                    free_inc(vec.tensor_tensor(XN[g], bank4(f"nn_{p}_{g}"), tab4("m1"), ALU.mult), f"nn_{p}_{g}")
                    vec.wait_ge(*is_free(f"nt_{p}_{g}"))
                    link(vec.tensor_tensor(XT[g], NT[g], tab4("m1t"), ALU.mult))
                    vec.tensor_tensor(XN[g], XN[g], tab4("ident"), ALU.add)
                    vec.tensor_tensor(XT[g], XT[g], tab4("ident"), ALU.add).then_inc(x_first, 1)
                for x, out, mask in (("mak", MAK, "before"), ("mrb", MRB, "upto"), ("mrk", MRK, "upto")):
                    for g in range(NG):
                        vec.wait_ge(*is_full(f"{x}_{p}_{g}"))
                        free_inc(vec.tensor_tensor(out[g], bank4(f"{x}_{p}_{g}"), tab4(mask), ALU.mult),
                                 f"{x}_{p}_{g}")
                for b in LEVELS:
                    for g in range(NG):
                        name = f"xp{b}_{p}_{g}"
                        vec.wait_ge(*is_full(name))
                        free_inc(vec.tensor_tensor(XP[g], bank4(name), tab4(f"m{b}"), ALU.mult), name)
                    if p and b == LEVELS[0]:
                        gn_centre(p - 1)
                    if p + 1 < NP and b == LEVELS[1]:
                        blocks_a(p + 1)
                    if p and b == LEVELS[2]:
                        gn_finish(p - 1)
                    if p + 1 < NP and b == LEVELS[3]:
                        blocks_b(p + 1)
                    for g in range(NG):
                        if b != LEVELS[-1]:
                            name = f"xn{b}_{p}_{g}"
                            vec.wait_ge(*is_full(name))
                            free_inc(vec.tensor_tensor(XN[g], bank4(name), XN[g], ALU.add), name)
                        name = f"xt{b}_{p}_{g}"
                        vec.wait_ge(*is_full(name))
                        free_inc(vec.tensor_tensor(XT[g], bank4(name), XT[g], ALU.add), name)
                    if p and b == LEVELS[3]:
                        gate(p - 1)
                    if p + 1 < NP:
                        if b == LEVELS[0]:
                            unit_key(p + 1)
                        if b == LEVELS[1]:
                            pair_input(p + 1, "v")
                        if b == LEVELS[2]:
                            bonus(p + 1)
                for g in range(NG):
                    vec.wait_ge(*is_full(f"gt_{p}_{g}"))
                    free_inc(vec.tensor_tensor(GT[g], bank4(f"gt_{p}_{g}"), tab4("ident"), ALU.add), f"gt_{p}_{g}")
                for g in range(NG):
                    vec.wait_ge(*is_full(f"rp_{p}_{g}"))
                    free_inc(vec.tensor_tensor(RP[g], bank4(f"rp_{p}_{g}"), RBD[p % 2][:, g * G:(g + 1) * G, :], ALU.add),
                             f"rp_{p}_{g}")
                for g in range(NG):
                    vec.wait_ge(*is_full(f"f_{p}_{g}"))
                    free_inc(vec.tensor_tensor(FB[g], bank4(f"f_{p}_{g}"),
                                               ELC[p % 2][:, g * G:(g + 1) * G, None].to_broadcast([P, G, P]), ALU.mult),
                             f"f_{p}_{g}")
                    vec.wait_ge(*is_free(f"f_{p}_{g}"))
                def outputs(g):
                    name = f"y_{p}_{g}"
                    vec.wait_ge(*is_full(name))
                    y = CAT[:, p, g * G * C:(g + 1) * G * C].rearrange("p (c t) -> p c t", c=G)
                    vec.tensor_copy(y[0:DH], bank4(name)[0:DH, :, 0:DH])
                    free_inc(vec.tensor_copy(y[DH:P], bank4(name)[DH:P, :, DH:P]), name)

                for n in range(NC - 1):
                    name = f"h_{p}_{n}"
                    vec.wait_ge(*is_full(name))
                    g, c = divmod(n, G)
                    g1, c1 = divmod(n + 1, G)
                    free_inc(scaled_sum(H[g1][:, c1, :], bank(name, P), ELC[p % 2][:, n:n + 1], FB[g][:, c, :]), name)
                    if n == G + 1:
                        outputs(0)
                    if p == NP - 1:
                        mixed_low(n)
                    if p + 2 < NP:
                        if n == 0:
                            denominator(f"w_{p + 2}")
                        if n == 1:
                            denominator(f"A_{p + 2}")
                        if n == 3:
                            running_sums(p + 2)
                        if n == 4:
                            pair_input(p + 2, "k")
                if p + 2 < NP:
                    pair_input(p + 2, "r")
                outputs(1)
                if p + 2 < NP:
                    changed_key(p + 2)
                    least_norm(p + 2)
                    blocks_r(p + 2)
            gn_centre(NP - 1)
            gn_finish(NP - 1)
            gate(NP - 1)
            weights_low(0)
            mixed_low(DK - 1)
            for q in range(len(SPLIT) + 1):
                name = SPLIT[q - 1] if q else ""
                if name.startswith("mix"):
                    m = int(name[3:])
                    vec.wait_ge(*is_full(name))
                    free_inc(vec.tensor_tensor(X[:, m, :], bank(name), X[:, m, :], ALU.add), name)
                    if m == DK - 1:
                        normalise(5, 1, "g_ffn")
                        for k in range(DK):
                            vec.wait_ge(u_high, k + 1)
                            vec.tensor_tensor(UL[:, k, :], U[:, k, :], UH[:, k, :].bitcast(F32), ALU.subtract
                                              ).then_inc(u_low, 1)
                if name.startswith("up"):
                    m = int(name[2:])
                    t = m % FH_TILES
                    vec.wait_ge(h_high, m + 1)
                    vec.tensor_tensor(FL[:, t, :], FS[:, t, :], FH[:, t, :].bitcast(F32), ALU.subtract
                                      ).then_inc(h_low, 1)
                if name.endswith(f"_{DOWN_BLOCKS - 1}"):
                    product = name.rsplit("_", 1)[0]
                    m = int(product.split("_")[1])
                    vec.wait_ge(*is_full(product))
                    free_inc(vec.tensor_tensor(X[:, m, :], bank(product), X[:, m, :], ALU.add), product)
                if q + 1 < len(SPLIT):
                    weights_low(q + 1)


def tables_of_shapes():
    t = {}
    tok = np.arange(S)
    dim = np.arange(P) % DH
    half = DH // 2
    freq = (10000.0 ** (-(np.arange(0, half, 2, dtype=np.float32)) / np.float32(half))).astype(np.float32)
    pos = np.where((dim < half)[:, None], (tok // GRID_W)[None, :], (tok % GRID_W)[None, :]).astype(np.float32)
    ang = pos * freq[dim % (half // 2)][:, None]
    t["cos"], t["sin"] = np.cos(ang), np.sin(ang)
    t["reset"] = np.broadcast_to((tok % C != 0).astype(np.float32), (P, S))
    rot = np.zeros((P, P), np.float32)
    for d in range(P):
        if d % half < half // 2:
            rot[d + half // 2, d] = -1.0
            rot[d, d + half // 2] = 1.0
    t["rot"] = rot
    r, c = np.arange(P)[:, None], np.arange(P)[None, :]
    same = r // DH == c // DH
    t["heads"] = same
    t["ones"] = np.ones((P, P))
    t["ident"] = r == c
    t["before"] = same & (r < c)
    t["upto"] = same & (r <= c)

    def band(b):
        return (r // (2 * b) == c // (2 * b)) & (r // b % 2 == 1) & (c // b % 2 == 0)

    t["m1"], t["m1t"] = band(1), band(1).T
    for b in LEVELS:
        t[f"m{b}"] = band(b)
    return np.ascontiguousarray(np.concatenate([np.asarray(t[k], np.float32) for k, _ in TAB], axis=1))


def feature_major(x):
    return np.ascontiguousarray(x.T.reshape(-1, P, x.shape[0]).transpose(1, 0, 2))


def stationary(w, rows=None):
    w = w if rows is None else w[rows]
    return w.reshape(-1, P, w.shape[1]).transpose(1, 0, 2).reshape(P, -1)


def kernel(**inputs):
    import concourse.bacc as bacc
    from concourse.bass_utils import run_bass_kernel_spmd

    a = {k: np.asarray(v) for k, v in inputs.items()}
    w_in, w_mod, rw_in = a["w_in"][0], a["w_mod"][0], a["rw_in_2"][0]
    w_pw, w_out, w_kv = a["w_pw"][0], a["w_out"][0], a["w_mem_kv_2"]
    w_mix, w_up, w_down = a["w_out_2"][0], a["w_ff1_2"][0], a["w_ff2_2"][0]
    DA = NQ * P
    K_AT, V_AT, ZA_AT = DA, DA + P, DA + 2 * P
    A_AT = ZA_AT + DA
    G_AT, ZC_AT = A_AT + CK * P, A_AT + 2 * CK * P
    MW = NP * P

    def pair(j):
        return np.concatenate([np.arange(j * DH, (j + 1) * DH), np.arange((NQ + j) * DH, (NQ + j + 1) * DH)])

    out_rows = np.concatenate([pair(j) for j in range(NQ)] + [np.arange(DA, D)])

    def block(name):
        if name.startswith("kmem"):
            return stationary(w_kv[:, int(name[4]) * P:(int(name[4]) + 1) * P])
        if name.startswith("vmem"):
            h = int(name[4])
            return stationary(w_kv[h * 4 * P:(h + 1) * 4 * P, SM:2 * SM])
        for i, g in enumerate(("shift", "scale", "gate")):
            if name.startswith(g):
                k = int(name[len(g):])
                return w_mod[k * P:(k + 1) * P, i * D:(i + 1) * D]
        if name == "wdad":
            return stationary(rw_in[:, 3 * MW:3 * MW + P])
        if name == "gd":
            return stationary(rw_in[:, 3 * MW + P:3 * MW + 2 * P])
        if name[:2] == "qm":
            at = 3 * MW + (2 + int(name[2])) * P
            return stationary(rw_in[:, at:at + P])
        if name[1:2] == "_":
            at = "krv".index(name[0])
            at = (1, 0, 2)[at] * MW + int(name[2]) * P
            return stationary(rw_in[:, at:at + P])
        if name == "k":
            return stationary(w_in[:, K_AT:K_AT + P])
        if name == "v":
            return stationary(w_in[:, V_AT:V_AT + P])
        if name[:2] == "zc":
            at = ZC_AT + int(name[2]) * P
            return stationary(w_in[:, at:at + P])
        if name[:2] == "za":
            return stationary(w_in[:, ZA_AT + pair(int(name[2]))])
        if name[:2] == "pw":
            i = int(name[2])
            return np.concatenate([stationary(w_pw[:, m * P:(m + 1) * P]) for m in (2 * i, 2 * i + 1)], axis=1)
        if name.startswith("out"):
            m = int(name[3])
            return stationary(w_out[:, m * P:(m + 1) * P], out_rows)
        if name.startswith("mix"):
            m = int(name[3])
            return stationary(w_mix[:, m * P:(m + 1) * P])
        if name.startswith("up"):
            m = int(name[2:])
            return stationary(w_up[:, m * P:(m + 1) * P])
        if name.startswith("down"):
            h, m, b = map(int, name[4:].split("_"))
            k = h * DOWN_BLOCKS + b
            return stationary(w_down[k * D:(k + 1) * D, m * P:(m + 1) * P])
        if name[0] == "q":
            return stationary(w_in[:, pair(int(name[1]))])
        at = (A_AT if name[0] == "a" else G_AT) + int(name[1]) * P
        return stationary(w_in[:, at:at + P])

    weights = np.stack([block(n) for n in BLOCKS])

    def columns(x):
        return x.reshape(-1, P).T

    two = np.concatenate
    mu = a["rw_mu_2"][0]
    mus = [mu[3 * MW:3 * MW + P], mu[3 * MW + P:3 * MW + 2 * P]]
    for p in range(NP):
        mus += [mu[at * MW + p * P:at * MW + (p + 1) * P] for at in (1, 0, 2)]
    b_mod = a["b_mod"][0]
    conv_w = a["conv_w"][0]
    vec = {
        "norm_w": columns(a["norm_w"][0]), "b_shift": columns(b_mod[0:D]), "b_scale": columns(b_mod[D:2 * D]),
        "b_gate": columns(b_mod[2 * D:]), "qn": columns(two([a["q_norm_w"][0]] * 2)),
        "kn": columns(two([a["k_norm_w"][0]] * 2)), "conv_b": columns(a["conv_b"][0]),
        "ln_w": columns(a["conv_ln_w"][0]), "ln_b": columns(a["conv_ln_b"][0]), "b_pw": columns(a["b_pw"][0]),
        "conv_w": conv_w.T.reshape(CK, P, TAPS).transpose(1, 0, 2).reshape(P, -1),
        "mu": np.stack(mus, axis=1), "w0": columns(a["rw_w0_2"][0]), "a0": columns(a["rw_a0_2"][0]),
        "k_k": columns(a["rw_k_k_2"][0]), "k_a": columns(a["rw_k_a_2"][0]),
        "r_k": columns(a["rw_r_k_2"][0].reshape(-1)), "lnx_g": columns(a["rw_lnx_g_2"][0]),
        "lnx_b": columns(a["rw_lnx_b_2"][0]), "g_mix": columns(a["norm_mix_g_2"][0]),
        "g_ffn": columns(a["norm_ffn_g_2"][0]), "g_mem": columns(a["mem_norm_g_2"]),
        "mqn": columns(two([a["mem_q_norm_g_2"][0]] * 2)), "mkn": columns(two([a["mem_k_norm_g_2"][0]] * 2)),
        "cc": np.stack([a["c"][0], a["c_ctx"]], axis=1).reshape(DK, P, 2).transpose(1, 0, 2).reshape(P, -1),
    }
    lora = two([a["rw_w2_2"][0], a["rw_a2_2"][0]], axis=0)
    small = two([vec[k] for k, _ in VEC] + [lora, a["rw_g2_2"][0]], axis=1)
    sent = {"small": small, "tables": tables_of_shapes(), "xT": feature_major(a["x"][0]),
            "ctxT": feature_major(a["ctx"][0]), "memT": feature_major(a["mem_2"][0]), "weights": weights}
    sent = {k: np.ascontiguousarray(v) for k, v in sent.items()}
    nc = bacc.Bacc("TRN2", target_bir_lowering=False, num_devices=1)
    args = {k: nc.dram_tensor(k, v.shape, F32, kind="ExternalInput").ap() for k, v in sent.items()}
    out = nc.dram_tensor("outT", (P, DK, S), F32, kind="ExternalOutput").ap()
    build(nc, outT=out, **args)
    r = run_bass_kernel_spmd(nc, [sent], core_ids=[0])
    got = r.results[0]["outT"]
    return np.ascontiguousarray(got.transpose(1, 0, 2).reshape(D, S).T)[None]
```

```python
from contextlib import ExitStack

import numpy as np

import concourse.bass as bass
from concourse import mybir

F32 = mybir.dt.float32
F32R = mybir.dt.float32r
ALU = mybir.AluOpType
ACT = mybir.ActivationFunctionType
AX = mybir.AxisListType.X

P = 128
D = 1024
DK = D // P
S = 512
SC = 256
SM = 256
DH = 64
NQ = 4
CK = 4
TAPS = 31
PAD = (TAPS - 1) // 2
SKEYS = SC + S
KT = SKEYS // P
MT = SM // P
NP = 6
C = 64
NC = S // C
G = 4
NG = NC // G
LEVELS = (2, 4, 8, 16, 32)
FF = 4096 // P
HALVES = 2
FH_TILES = FF // HALVES
DOWN_BLOCKS = FH_TILES // DK
GRID_W = 64
EPS = 1e-6
GN_EPS = 64e-5
DECAY = float(np.exp(-0.5))
KK_LEAST = 1e-24
KK_SCALE = 2.0 ** 16
SIG_MOST = 1e18
RING = 6
SBUF_AT, SBUF_WORDS = 4128, 57344
UNITS = NQ * 2 * (S // P)
MUNITS = 2 * 2 * (S // P)
MU_CHAIN = 2 * len(LEVELS)
ROTATE_7 = -1
AHEAD = 2
MAHEAD = 3
IN_TAPS = [0] + [5] * 8 + [9, 6, 2, 2, 2, 1, 3, 4, 4, 4, 4, 3, 3]
assert sum(IN_TAPS) <= 3 * TAPS
BESIDE_ATTENTION = {3: "gate_t", 12: "cmean", 16: "cvar", 23: "pw0", 24: "pw1", 25: "pw2", 26: "pw3"}

VEC = [("norm_w", 8), ("b_shift", 8), ("b_scale", 8), ("b_gate", 8), ("qn", 1), ("kn", 1),
       ("conv_b", 4), ("ln_w", 4), ("ln_b", 4), ("b_pw", 4), ("conv_w", 4 * TAPS), ("mu", 20),
       ("w0", 6), ("a0", 6), ("k_k", 6), ("k_a", 6), ("r_k", 6), ("lnx_g", 6), ("lnx_b", 6),
       ("g_mix", 8), ("g_ffn", 8), ("g_mem", 8), ("mqn", 1), ("mkn", 1), ("cc", 16)]
AT = {}
_n = 0
for _k, _w in VEC:
    AT[_k] = _n
    _n += _w
NVEC = _n
LORA_AT, G2_AT = NVEC, NVEC + 768
NSMALL = NVEC + 2 * 768
MU_WDAD, MU_GD, MU_PAIR = 0, 1, 2

TAB = [("cos", S), ("sin", S), ("reset", S), ("rot", P), ("heads", P), ("ones", P), ("ident", P),
       ("before", P), ("upto", P), ("m1", P)] + [(f"m{b}", P) for b in LEVELS]
TAT = {}
_n = 0
for _k, _w in TAB:
    TAT[_k] = (_n, _w)
    _n += _w
NTAB = _n

BLOCKS = (["kmem0", "kmem1"]
          + [f"shift{k}" for k in range(DK)] + [f"scale{k}" for k in range(DK)] + ["vmem0", "vmem1"]
          + [f"{x}{i}" for i in range(CK) for x in "ag"]
          + ["k", "v"] + [f"q{j}" for j in range(NQ)] + [f"zc{i}" for i in range(CK)]
          + [f"za{j}" for j in range(NQ)] + [f"gate{k}" for k in range(DK)] + ["pw0", "pw1"]
          + [f"out{m}" for m in range(DK)]
          + ["wdad", "gd"] + [f"{x}_{p}" for p in range(NP) for x in "krv"] + ["qm0", "qm1"]
          + [f"mix{m}" for m in range(DK)]
          + [n for h in range(HALVES)
             for n in ([f"up{m}" for m in range(h * FH_TILES, (h + 1) * FH_TILES)]
                       + [f"down{h}_{m}_{b}" for m in range(DK) for b in range(DOWN_BLOCKS)])])
BLOCK_AT = {n: i for i, n in enumerate(BLOCKS)}
IN_BLOCKS = BLOCKS[BLOCK_AT["a0"]:BLOCK_AT["gate0"]]
PAIR_BLOCKS = BLOCKS[BLOCK_AT["wdad"]:BLOCK_AT["mix0"]]
SPLIT = IN_BLOCKS + BLOCKS[BLOCK_AT["out0"]:]
SPLIT_AT = {n: i for i, n in enumerate(SPLIT)}
SLOT = [b % RING for b in range(BLOCK_AT["wdad"])]
SLOT += [n % 2 for n in range(len(PAIR_BLOCKS))]
SLOT += [(SLOT[-1] + 1 + n) % RING for n in range(len(BLOCKS) - len(SLOT))]
USES = [SLOT[:b + 1].count(SLOT[b]) for b in range(len(BLOCKS))]
BEFORE = [max((a for a in range(b) if SLOT[a] == SLOT[b]), default=None) for b in range(len(BLOCKS))]
OUT_ORDER = (4, 5, 6, 7, 0, 1, 2, 3)
CAT_ORDER = (0, 1, 2, 3, 4, 6, 7, 5)


BESIDE_CHAIN = [[("k", 0, 2)], [("k", 2, 4)], [("k", 4, 6)], [("k", 6, DK)], [("r", 0, 1)], [("r", 1, 4)],
                [("r", 4, DK)]]
assert len(BESIDE_CHAIN) == NC - 1 and MU_CHAIN + NC - 1 + 3 == MUNITS + MAHEAD + 1


def beside_chain(p, x):
    return f"{x}_{p + 2}" if p + 2 < NP else {"k": "qm0", "r": "qm1"}[x]


def beside_level(p, b):
    last = {LEVELS[0]: ["gm"], LEVELS[1]: ["gv"], LEVELS[3]: ["gg"]}.get(b, []) if p else []
    following = {LEVELS[1]: ["v"], LEVELS[3]: ["bon"]}.get(b, []) if p + 1 < NP else []
    return [f"{x}_{p - 1}" for x in last] + [f"{x}_{p + 1}" for x in following]


QZ_BLOCKS = [f"q{j}" for j in range(NQ)] + [f"zc{i}" for i in range(CK)] + [f"za{j}" for j in range(NQ)]


def psum_order():
    o = [(n, 1, None) for n in ("mem_sum", "ctx_sum", "kmem0", "kmem1", "hs0", "hs1")]

    rotation = [None]

    def add(*names):
        o.extend((n, 1, rotation[0]) for n in names)

    add("shift_lo", "shift_hi", "x_sum", "scale_lo", "scale_hi", "shift_t", "scale_t", "vmem")
    for i in range(CK):
        add(f"a{i}", f"g{i}")
    add("kx", "kc", "hs2", "rot0", "hs3", "vx", "v_lo")
    for n, x in enumerate(QZ_BLOCKS):
        add(x)
        if n == 0:
            add("v_hi")
        elif n <= NQ:
            add(f"hs{3 + n}", f"rot{n}")
    add("gate_lo", "gate_hi")
    pair = 0
    for i in range(UNITS + AHEAD + 1):
        if i < UNITS:
            o.append((f"s{i}", 2, pair % 3 * 2))
            pair += 1
        if 0 <= i - AHEAD < UNITS:
            o.append((f"pt{i - AHEAD}", 2, pair % 3 * 2))
            pair += 1
        if i in BESIDE_ATTENTION:
            o.append((BESIDE_ATTENTION[i], 1, 6 if BESIDE_ATTENTION[i] in ("cmean", "cvar") else 7))
        v = i - AHEAD - 1
        if v >= 0 and v % 8 == 0:
            o.append((f"o{v // 8}", 1, 6 + v // 8 % 2))
    add(*(f"out{m}" for m in range(DK)), "h1_sum", "wdad", "gd")

    def memory_unit(i):
        if i < MUNITS:
            add(f"e{i}")
        if 0 <= i - MAHEAD < MUNITS:
            add(f"et{i - MAHEAD}")
        v = i - MAHEAD - 1
        if v >= 0 and v % 8 == 0:
            o.append((f"mo{v // 8}", 1, 7))

    add(*(f"{x}_0" for x in "kwArv"), "kks_0", "bon_0", *(f"{x}_1" for x in "wAkr"), "kks_1")
    for p in range(NP):
        final = p == NP - 1
        if final:
            rotation[0] = ROTATE_7
        for x in ("nt", "nn", "ta", "tb", "tk", "tv", "mak", "mrb", "mrk"):
            add(*(f"{x}_{p}_{g}" for g in range(NG)))
        for n, b in enumerate(LEVELS):
            add(*(f"{x}{b}_{p}_{g}" for g in range(NG) for x in ("xp", "xt")), *beside_level(p, b))
            if final:
                memory_unit(2 * n)
            add(*(f"{'xn' if b != LEVELS[-1] else 'xf'}{b}_{p}_{g}" for g in range(NG)))
            if final:
                memory_unit(2 * n + 1)
        for x in ("mv", "w", "u", "gt", "rp", "f"):
            add(*(f"{x}_{p}_{g}" for g in range(NG)))
        if p + 2 < NP:
            add(f"w_{p + 2}", f"A_{p + 2}")
        for n in range(NC - 1):
            add(f"h_{p}_{n}")
            if n == G and p == NP - 2:
                add("hs8")
            if n == G:
                add(f"y_{p}_0")
            add(*(beside_chain(p, x) for x, lo, hi in BESIDE_CHAIN[n] if lo == 0 and not final))
            if final:
                memory_unit(MU_CHAIN + n)
        add(f"y_{p}_1")
        if p + 2 < NP:
            add(f"kks_{p + 2}")
        elif not final:
            add("hs9")
    for n, x in enumerate(("gm", "gv", "gg")):
        memory_unit(MU_CHAIN + NC - 1 + n)
        add(f"{x}_{NP - 1}")
    rotation[0] = None
    add(*(f"mix{m}" for m in range(DK)), "h2_sum")
    for h in range(HALVES):
        add(*(f"up{m}" for m in range(h * FH_TILES, (h + 1) * FH_TILES)), *(f"down{h}_{m}" for m in range(DK)))
    return o


def psum_plan():
    last, count, at, plan = [None] * 8, [0] * 8, 0, {}
    for name, n, pinned in psum_order():
        here = at % 8 if pinned is None else at % 8 % 7 if pinned == ROTATE_7 else pinned
        count[here] += 1
        before = []
        for b in range(here, here + n):
            if last[b] is not None and last[b] not in before:
                before.append(last[b])
            last[b] = name
        assert name not in plan, name
        plan[name] = (here, n, count[here], before)
        at = here + n
    return plan


def last_product(block):
    for g in ("shift", "scale", "gate"):
        if block.startswith(g):
            return f"{g}_hi" if block.endswith(str(DK - 1)) else None
    return {"vmem0": "vmem", "vmem1": "vmem", "k": "kc", "v": "v_lo", "pw0": "pw1",
            "pw1": "pw3"}.get(block, block)


def build(nc, small, tables, xT, ctxT, memT, weights, saved, outT):
    plan = psum_plan()
    with ExitStack() as ctx:
        room = [SBUF_AT]
        placed = {}

        def sb(name, *shape):
            words = int(np.prod(shape[1:]))
            placed[name] = room[0]
            t = nc.alloc_sbuf_tensor_at(name, list(shape), F32, offset=4 * room[0])
            room[0] += -(-words // 8) * 8
            assert room[0] <= SBUF_WORDS
            return t

        def over(name, base, at, *shape):
            return nc.alloc_sbuf_tensor_at(name, list(shape), F32R, offset=4 * (placed[base] + at))

        def sem(name):
            return ctx.enter_context(nc.semaphore(name))

        ring = sb("ring", P, RING, D)
        X = sb("residual", P, DK, S)
        U = sb("normed", P, DK, S)
        CAT = sb("mixed", P, DK, S)
        TB = sb("tables_sb", P, NTAB)
        SV = sb("small_sb", P, NSMALL)
        KVM = sb("memory_keys_values", P, (2 + MT) * SM)
        KMEM = KVM[:, 0:2 * SM].rearrange("p (a b) -> p a b", a=2)
        VMEM = KVM[:, 2 * SM:].rearrange("p (a b) -> p a b", a=MT)
        SG = sb("sigmoids", P, 2, S)
        HS = sb("head_squares", P, 2, S)
        HR = sb("head_rstd", P, 2, S)
        RS = sb("rstd", P, 2, S)
        QW = sb("weighted", P, S)
        T12 = sb("t1_t2", P, 2, S)
        T1, T2 = T12[:, 0, :], T12[:, 1, :]
        MOD = sb("mod_cols", P, 3, DK, 2)
        SMALLT = sb("small_temps", P, 256)
        WORKW = 22656
        work = sb("work", P, WORKW)
        psum = ctx.enter_context(nc.psum_tensor("psum", [P, 8 * S], F32))

        def region(at, *shape):
            n = int(np.prod(shape))
            v = work[:, at:at + n]
            assert at + n <= WORKW
            if len(shape) == 2:
                return v.rearrange("p (a b) -> p a b", a=shape[0])
            if len(shape) == 3:
                return v.rearrange("p (a b c) -> p a b c", a=shape[0], b=shape[1])
            return v

        SQ = region(0, DK, S)
        CV = region(4 * S, CK, S)
        MEM = region(8 * S, DK, SM)
        CTX = region(12 * S, DK, SC)
        PR = region(8 * S, AHEAD + 1, SKEYS)
        PT = region(8 * S + (AHEAD + 1) * SKEYS, 2, SKEYS)
        at = 16 * S
        GLU = region(at, CK, S + 2 * PAD); at += CK * (S + 2 * PAD)
        QZ = region(at, 2, NQ, S); at += 2 * NQ * S
        KTT = region(at, SKEYS); at += SKEYS
        VT = region(at, KT, P); at += SKEYS
        ZC = region(at, CK, S); at += CK * S
        ZA = region(at, NQ, S); at += NQ * S
        CT = region(at, S); at += S
        MODROW = [T12[:].rearrange("p a b -> p (a b)"), region(at, D)]
        at = 0
        ABD, BBD, KBD, RBD0, VBD = (region(i * NC * P, NC, P) for i in range(5)); at += 5 * NC * P
        RBD = [RBD0, RS[:].rearrange("p a (c b) -> p (a c) b", b=P)]
        K0, R0, V0, LG, EL, AV, KKN, BV0 = (region(at + i * S, S) for i in range(8)); at += 8 * S
        TZ = region(at, 2, S); at += 2 * S
        SGD = region(at, S); at += S
        BV = [BV0, TB[:, TAT["cos"][0]:TAT["cos"][0] + S]]
        H = [region(at, G, P), TB[:, TAT["sin"][0]:TAT["sin"][0] + S].rearrange("p (a b) -> p a b", a=G)]
        at += G * P
        half = at
        HB = [[region(half + (g * 11 + i) * G * P, G, P) for i in range(11)] for g in range(NG)]
        NT, MAK, MRB, MRK, TA, TBT, TK, TV, XN, XT, XP = (
            [HB[g][i] for g in range(NG)] for i in range(11))
        MV, WB, UB, FB, GT, RP = XP, NT, XN, XT, MAK, TA
        inputs = 5 * NC * P
        QMZ = region(inputs, 2, 2, S)
        MPR = region(inputs + 4 * S, MAHEAD + 1, SM)
        MPT = region(inputs + 6 * S, 2, SM)
        CATH = over("mixed_high", "work", 0, P, DK, S)
        CATL = over("mixed_low", "work", half, P, DK, S)
        SQ2 = region(inputs, DK, S)
        WH = [over("in_weights_high", "work", 0, P, 2, D)]
        WL = [over("in_weights_low", "work", DK * S, P, 2, D)]
        WH.append(over("out_weights_high", "work", 0, P, 2, D))
        WL.append(over("out_weights_low", "work", 16 * S, P, 2, D))
        WH.append(over("pair_weights_high", "ring", 2 * D, P, 2, D))
        WL.append(over("pair_weights_low", "ring", 4 * D, P, 2, D))
        WH.append(over("weights_high", "work", 2 * FH_TILES * S, P, 2, D))
        WL.append(over("weights_low", "work", 2 * FH_TILES * S + 2 * D, P, 2, D))
        OUTH = over("gated_high", "normed", 0, P, DK, S)
        OUTL = over("gated_low", "work", DK * S, P, DK, S)
        SQ1 = QZ.rearrange("p a b c -> p (a b) c")
        FS = region(0, FH_TILES, S)
        FL = over("hidden_low", "work", 0, P, FH_TILES, S)
        FH = over("hidden_high", "work", FH_TILES * S, P, FH_TILES, S)
        UH = over("normed_high", "mixed", 0, P, DK, S)
        UL = over("normed_low", "normed", 0, P, DK, S)
        UHX = over("pair_normed_high", "residual", 0, P, DK, S)
        assert half + DK * S <= 2 * FH_TILES * S and 2 * FH_TILES * S + 4 * D <= WORKW

        def col(name, i=0, rows=slice(0, P)):
            return SV[rows, AT[name] + i:AT[name] + i + 1]

        def cols(name, i, n):
            return SV[:, AT[name] + i:AT[name] + i + n]

        def tab(name):
            return TB[:, TAT[name][0]:TAT[name][0] + TAT[name][1]]

        def tab4(name):
            return tab(name)[:, None, :].to_broadcast([P, G, P])

        NEG = SMALLT[:, 0:12]
        KA1 = SMALLT[:, 12:18]
        MU1 = SMALLT[:, 18:38]
        SILU_C = SMALLT[:, 38:54].rearrange("p (k w) -> p k w", k=DK)
        SILU_E = SMALLT[:, 54:70]
        ROWMAX, NEGMAX, ROWSUM, ROWINV = (SMALLT[:, 72 + 4 * i:76 + 4 * i] for i in range(4))
        ELC = [SMALLT[:, 96 + i * NC:96 + (i + 1) * NC] for i in range(2)]

        full = [sem(f"psum_full{b}") for b in range(8)]
        free = [sem(f"psum_free{b}") for b in range(8)]
        slot = [sem(f"slot_loaded{i}") for i in range(RING)]
        tables_in, small_in, mem_in, x_in, ctx_in = map(
            sem, ("tables_in", "small_in", "mem_in", "x_in", "ctx_in"))
        x_saved = sem("residual_saved")
        token_tables_in = sem("token_tables_in")
        mod_block_used = sem("mod_block_used")
        squares, rstd, normed = sem("squares_ready"), sem("rstd_ready"), sem("normed_ready")
        res_squares, tiles_summed = sem("residual_squares_ready"), sem("squares_summed_over_tiles")
        c_exp, c_den, c_sig, c_ready = map(sem, ("c_exp", "c_den", "c_sigmoid", "c_silu_ready"))
        mod_ready = sem("modulation_ready")
        consts_ready = sem("derived_columns_ready")
        sig_exp, sig_den, sig_out = map(sem, ("sigmoid_exp", "sigmoid_denominator", "sigmoid_ready"))
        head_sq, head_rs = sem("head_squares_ready"), sem("head_rstd_ready")
        q_ready, k_ready = sem("q_ready"), sem("k_ready")
        zeroed = sem("zeroed")
        negmax, probs_scaled = sem("negmax_ready"), sem("probs_scaled")
        conv_out, conv_sq, conv_rs, conv_ln, conv_act = map(
            sem, ("conv_out", "conv_squares", "conv_rstd", "conv_normed", "conv_act"))
        partial = sem("shift_partial")
        low_used = sem("tanh_placed")
        scan_done, exps_done = sem("log_decays_ready"), sem("decays_ready")
        kk_sq, kk_rs, bonus_in = sem("kk_squares"), sem("kk_rstd"), sem("bonus_in")
        bd_ready, v_ready = sem("a_b_blocks_ready"), sem("v_blocks_ready")
        k_blocks, r_ready, key_step, gn_done = map(sem, ("k_blocks_ready", "r_blocks_ready", "key_step", "gn_done"))
        x_first = sem("inverse_started")
        gn_sq, gn_rs = sem("gn_squares"), sem("gn_rstd")
        w_high, w_low, half_used = map(sem, ("weights_high_ready", "weights_low_ready", "first_down_block_used"))
        cat_high, cat_low = sem("mixed_high_ready"), sem("mixed_low_ready")
        out_high, out_low = sem("gated_high_ready"), sem("gated_low_ready")
        u_high, u_low = sem("normed_high_ready"), sem("normed_low_ready")
        h_relu, h_high, h_low = map(sem, ("hidden_relu", "hidden_high_ready", "hidden_low_ready"))
        out_stored = sem("out_stored")
        act_step, vec_step = sem("act_step"), sem("vec_step")

        def bank(name, w=None, rows=slice(0, P)):
            b, n, _, _ = plan[name]
            return psum[rows, b * S:b * S + (w or n * S)]

        def bank4(name):
            return bank(name).rearrange("p (g t) -> p g t", g=G)

        def is_full(name):
            return full[plan[name][0]], plan[name][2]

        def is_free(name):
            return free[plan[name][0]], plan[name][2]

        def group(q):
            return sum(q >= SPLIT_AT[n] for n in ("out0", "wdad", "mix0"))

        def split_used(q):
            name = SPLIT[q]
            if not name.startswith("down"):
                return is_full({"k": "kx", "v": "vx"}.get(name, name))
            product, b = name.rsplit("_", 1)
            if int(b) == DOWN_BLOCKS - 1:
                return is_full(product)
            firsts = [n for n in SPLIT if n.startswith("down") and not n.endswith(f"_{DOWN_BLOCKS - 1}")]
            return half_used, firsts.index(name) + 1

        def full_inc(ins, name):
            ins.then_inc(full[plan[name][0]], 1)

        def free_inc(ins, name):
            ins.then_inc(free[plan[name][0]], 1)

        sigmoids = ([(f"g{i}", True, is_free(f"a{i}")) for i in range(CK)]
                    + [(f"zc{i}", False, is_free(f"zc{i}")) for i in range(CK)]
                    + [(f"za{j}", False, is_free(f"za{j}")) for j in range(NQ)]
                    + [(f"conv{i}", False, (conv_act, i + 1)) for i in range(CK)]
                    + [("wd", False, (low_used, 1)), ("gd_sig", False, None)]
                    + [(f"{x}_{p}", True, None) for p in range(NP) for x in "wA"])
        sig_at, kept = {}, 0
        for n, (name, frees, _) in enumerate(sigmoids):
            kept += not frees
            sig_at[name] = (n, is_free(name) if frees else (sig_exp, kept))
        heads = ([("kmem0", is_free("kmem0")), ("kmem1", is_free("kmem1")), ("kx", (k_ready, 1)),
                  ("kc", is_free("kc"))] + [(f"q{j}", (q_ready, j + 1)) for j in range(NQ)]
                 + [("qm0", is_free("qm0")), ("qm1", is_free("qm1"))])
        head_at = {name: n for n, (name, _) in enumerate(heads)}

        block = ctx.enter_context(nc.Block())

        @block.sync
        def _(sp):
            sp.dma_start(MEM, memT).then_inc(mem_in, 16)
            sp.dma_start(TB[:, 3 * S:], tables[:, 3 * S:]).then_inc(tables_in, 16)
            sp.dma_start(SV[:], small).then_inc(small_in, 16)
            sp.dma_start(CTX, ctxT).then_inc(ctx_in, 16)
            mod_seen = 0
            for b, name in enumerate(BLOCKS):
                if b == BLOCK_AT["shift4"]:
                    sp.dma_start(X[:], xT).then_inc(x_in, 16)
                if b == BLOCK_AT["scale4"]:
                    sp.dma_start(TB[:, 0:3 * S], tables[:, 0:3 * S]).then_inc(token_tables_in, 16)
                if b == BLOCK_AT["k_0"]:
                    for m in range(DK):
                        sp.wait_ge(*is_free(f"out{m}"))
                        sp.dma_start(saved[:, m, :], X[:, m, :]).then_inc(x_saved, 16)
                if b == BLOCK_AT["mix0"]:
                    sp.wait_ge(*is_full("qm1"))
                    sp.wait_ge(x_saved, 16 * DK)
                    sp.dma_start(X[:], saved).then_inc(x_in, 16)
                if BEFORE[b] is not None:
                    before = last_product(BLOCKS[BEFORE[b]])
                    if before in SPLIT_AT and BLOCKS[BEFORE[b]] not in ("k", "v"):
                        sp.wait_ge(w_low, SPLIT_AT[before] + 1)
                    elif before is None:
                        mod_seen += 1
                        sp.wait_ge(mod_block_used, mod_seen)
                    else:
                        sp.wait_ge(*is_full(before))
                sp.dma_start(ring[:, SLOT[b], :], weights[b]).then_inc(slot[SLOT[b]], 16)
            for m in range(DK):
                sp.wait_ge(*is_free(f"down{HALVES - 1}_{m}"))
                sp.dma_start(outT[:, m, :], X[:, m, :]).then_inc(out_stored, 16)
            sp.wait_ge(out_stored, 16 * DK)

        @block.gpsimd
        def _(pool):
            pool.memset(GLU, 0.0).then_inc(zeroed, 1)
            pool.memset(QZ, 0.0).then_inc(zeroed, 1)
            pool.wait_ge(*is_free(f"out{DK - 1}"))
            pool.memset(TZ, 0.0).then_inc(zeroed, 1)
            pool.wait_ge(*is_full("h1_sum"))
            for z in (ABD, BBD, KBD, RBD[0], VBD, H[0][:, 0, :]):
                pool.memset(z, 0.0).then_inc(zeroed, 1)
            pool.wait_ge(normed, 2 + 2 * DK)
            pool.memset(RBD[1], 0.0).then_inc(zeroed, 1)
            pool.wait_ge(zeroed, 10)
            for p in range(NP):
                pool.wait_ge(bonus_in, p + 1)
                pool.wait_ge(exps_done, p + 1)
                if p:
                    pool.wait_ge(*is_full(f"mrk_{p - 1}_{NG - 1}"))
                for rows, cs in ((slice(0, DH), slice(0, DH)), (slice(DH, P), slice(DH, P))):
                    k3, l3 = (x[rows, :].rearrange("p (c t) -> p c t", c=NC) for x in (QW[:], LG))
                    ins = pool.tensor_tensor(KBD[rows, :, cs], k3, l3, ALU.mult)
                ins.then_inc(k_blocks, 1)
            pool.wait_ge(k_blocks, NP)
            pool.wait_ge(bd_ready, NP)
            pool.wait_ge(r_ready, NP)
            pool.wait_ge(v_ready, NP)
            pool.wait_ge(*is_free(f"bon_{NP - 1}"))
            pool.memset(QMZ, 0.0).then_inc(zeroed, 1)

        @block.tensor
        def _(pe):
            order = iter(psum_order())

            def take(name, w=None, rows=slice(0, P)):
                assert next(order)[0] == name, name
                for before in plan[name][3]:
                    pe.wait_ge(*is_free(before))
                return bank(name, w, rows)

            def loaded(name):
                b = BLOCK_AT[name]
                pe.wait_ge(slot[SLOT[b]], 16 * USES[b])
                return ring[:, SLOT[b], :]

            def sum_over(name, src, n, w, each=None):
                out = take(name, w)
                for k in range(n):
                    if each:
                        pe.wait_ge(each[0], each[1] + k)
                    last = pe.matmul(out, tab("ones"), src(k), start=k == 0, stop=k == n - 1)
                full_inc(last, name)

            def project(block_name, name, src, w=S, each=None):
                wt = loaded(block_name)
                out = take(name, w)
                for k in range(DK):
                    if each:
                        pe.wait_ge(each[0], each[1] + k)
                    last = pe.matmul(out, wt[:, k * P:(k + 1) * P], src(k), start=k == 0, stop=k == DK - 1)
                full_inc(last, name)

            def split_product(block_name, out, high, low, order=range(DK), first=True, last=True, each=None):
                q = SPLIT_AT[block_name]
                pe.wait_ge(w_high, q + 1)
                pe.wait_ge(w_low, q + 1)
                for n, k in enumerate(order):
                    if each:
                        each(n, k)
                    wh, wl = (w[group(q)][:, q % 2, k * P:(k + 1) * P] for w in (WH, WL))
                    pe.matmul(out, wh, high(k), start=first and n == 0, stop=False)
                    pe.matmul(out, wh, low(k), start=False, stop=False)
                    ins = pe.matmul(out, wl, high(k), start=False, stop=last and n == len(order) - 1)
                return ins

            def in_product(block_name, name, each=None):
                full_inc(split_product(block_name, take(name), lambda k: UH[:, k, :], lambda k: UL[:, k, :],
                                       each=each), name)

            def one(name, stationary, moving, w=S):
                full_inc(pe.matmul(take(name, w), stationary, moving, start=True, stop=True), name)

            def head_sums(n, w=S):
                pe.wait_ge(head_sq, n + 1)
                one(f"hs{n}", tab("heads"), HS[:, n % 2, 0:w], w)

            def rotate(n, name):
                pe.wait_ge(*is_free(name))
                one(f"rot{n}", tab("rot"), QW[:])

            def modulation(g):
                lo, hi = take(f"{g}_lo", rows=slice(0, 2)), take(f"{g}_hi", rows=slice(0, 2))
                for k in range(DK):
                    wt = loaded(f"{g}{k}")
                    a = pe.matmul(lo, SILU_C[:, k, :], wt[:, 0:S], start=k == 0, stop=k == DK - 1)
                    b = pe.matmul(hi, SILU_C[:, k, :], wt[:, S:D], start=k == 0, stop=k == DK - 1)
                    if k < DK - 1:
                        b.then_inc(mod_block_used, 1)
                full_inc(a, f"{g}_lo")
                full_inc(b, f"{g}_hi")

            def modulation_turn(g, rows):
                pe.wait_ge(*is_free(f"{g}_lo"))
                pe.wait_ge(*is_free(f"{g}_hi"))
                out = take(f"{g}_t", 2 * DK)
                for k in range(DK):
                    last = pe.transpose(out[:, 2 * k:2 * k + 2], rows[0:2, k * P:(k + 1) * P],
                                        tab("ident")[0:2, 0:2])
                full_inc(last, f"{g}_t")

            pe.wait_ge(tables_in, 16)
            pe.wait_ge(squares, 1)
            sum_over("mem_sum", lambda k: SQ[:, k, 0:SM], DK, SM)
            pe.wait_ge(squares, 2)
            sum_over("ctx_sum", lambda k: SQ[:, k, SM:SM + SC], DK, SC)
            pe.wait_ge(normed, 1)
            for i in range(2):
                project(f"kmem{i}", f"kmem{i}", lambda k: MEM[:, k, :], SM)
            head_sums(0, SM)
            head_sums(1, SM)
            pe.wait_ge(c_ready, 1)
            modulation("shift")
            pe.wait_ge(tiles_summed, 1)
            one("x_sum", tab("ones"), SQ[:, 0, :])
            modulation("scale")
            modulation_turn("shift", MODROW[0])
            modulation_turn("scale", MODROW[1])
            out = take("vmem")
            wts = [loaded("vmem0"), loaded("vmem1")]
            for t in range(MT):
                for k in range(DK):
                    last = pe.matmul(out[:, t * SM:(t + 1) * SM], MEM[:, k, t * P:(t + 1) * P],
                                     wts[k // 4][:, (k % 4) * SM:(k % 4 + 1) * SM],
                                     start=k == 0, stop=k == DK - 1)
            full_inc(last, "vmem")
            def modulated_tile(n, k):
                pe.wait_ge(u_low, n + 1)

            for i in range(CK):
                in_product(f"a{i}", f"a{i}", each=modulated_tile if i == 0 else None)
                in_product(f"g{i}", f"g{i}")
            in_product("k", "kx")
            pe.wait_ge(normed, 2 + DK)
            project("k", "kc", lambda k: CTX[:, k, :], SC)
            head_sums(2)
            rotate(0, "kx")
            head_sums(3, SC)
            in_product("v", "vx")
            wt = loaded("v")
            out = take("v_lo", SC)
            for t in range(SC // P):
                for k in range(DK):
                    last = pe.matmul(out[:, t * P:(t + 1) * P], CTX[:, k, t * P:(t + 1) * P],
                                     wt[:, k * P:(k + 1) * P], start=k == 0, stop=k == DK - 1)
            full_inc(last, "v_lo")
            for n, x in enumerate(QZ_BLOCKS):
                in_product(x, x)
                if n == 0:
                    pe.wait_ge(*is_free("vx"))
                    out = take("v_hi")
                    for t in range(S // P):
                        last = pe.transpose(out[:, t * P:(t + 1) * P], RS[:, 0, t * P:(t + 1) * P], tab("ident"))
                    full_inc(last, "v_hi")
                elif n <= NQ:
                    head_sums(3 + n)
                    rotate(n, f"q{n - 1}")

            def turn(name, tiles, src):
                out = take(name, tiles * P)
                for t in range(tiles):
                    last = pe.transpose(out[:, t * P:(t + 1) * P], src[:, t * P:(t + 1) * P], tab("ident"))
                full_inc(last, name)

            def beside_attention(i):
                name = BESIDE_ATTENTION.get(i)
                if name == "gate_t":
                    modulation_turn("gate", MODROW[0])
                if name == "cmean":
                    pe.wait_ge(conv_out, CK)
                    sum_over("cmean", lambda k: CV[:, k, :], CK, S)
                if name == "cvar":
                    pe.wait_ge(conv_sq, 1)
                    sum_over("cvar", lambda k: SQ[:, k, :], CK, S)
                if name in [f"pw{n}" for n in range(CK)]:
                    n = int(name[2])
                    pe.wait_ge(conv_act, CK)
                    wt = loaded(f"pw{n // 2}")
                    out = take(name)
                    for k in range(CK):
                        at = (n % 2 * CK + k) * P
                        last = pe.matmul(out, wt[:, at:at + P], CV[:, k, :], start=k == 0, stop=k == CK - 1)
                    full_inc(last, name)

            modulation("gate")
            pe.wait_ge(k_ready, 1)
            pe.wait_ge(*is_free("kc"))
            pe.wait_ge(*is_free("v_hi"))
            for i in range(UNITS + AHEAD + 1):
                if i < UNITS:
                    j, h, qt = i // 8, i // 4 % 2, i % 4
                    pe.wait_ge(q_ready, j + 1)
                    s = take(f"s{i}")
                    q = QZ[:, h, j, qt * P:(qt + 1) * P]
                    pe.matmul(s[:, 0:S], q, KTT[:, 0:S], start=True, stop=True)
                    full_inc(pe.matmul(s[:, S:SKEYS], q, KTT[:, S:SKEYS], start=True, stop=True), f"s{i}")
                v = i - AHEAD
                if 0 <= v < UNITS:
                    pe.wait_ge(probs_scaled, v + 1)
                    turn(f"pt{v}", KT, PR[:, v % (AHEAD + 1), :])
                beside_attention(i)
                v = i - AHEAD - 1
                if v >= 0:
                    j, h, qt = v // 8, v // 4 % 2, v % 4
                    if v % 8 == 0:
                        o = take(f"o{j}")
                    pe.wait_ge(*is_free(f"pt{v}"))
                    for t in range(KT):
                        last = pe.matmul(o[h * DH:(h + 1) * DH, qt * P:(qt + 1) * P],
                                         VT[:, t, h * DH:(h + 1) * DH],
                                         PT[:, v % 2, t * P:(t + 1) * P], start=t == 0, stop=t == KT - 1)
                    if v % 8 == 7:
                        full_inc(last, f"o{j}")
            def gated_tile(n, k):
                pe.wait_ge(out_low, n + 1)

            for m in range(DK):
                full_inc(split_product(f"out{m}", take(f"out{m}"), lambda k: OUTH[:, k, :], lambda k: OUTL[:, k, :],
                                       order=OUT_ORDER, each=gated_tile if m == 0 else None), f"out{m}")

            pe.wait_ge(tiles_summed, 2)
            one("h1_sum", tab("ones"), SQ1[:, 0, :])
            def pair_tile(n, k):
                pe.wait_ge(u_low, DK + n + 1)

            for x in ("wdad", "gd"):
                full_inc(split_product(x, take(x), lambda k: UHX[:, k, :], lambda k: UL[:, k, :],
                                       each=pair_tile if x == "wdad" else None), x)

            def memory_unit(i):
                if i < MUNITS:
                    j, h, qt = i // 8, i // 4 % 2, i % 4
                    pe.wait_ge(*is_free(f"qm{j}"))
                    one(f"e{i}", QMZ[:, h, j, qt * P:(qt + 1) * P], KMEM[:, j, :], SM)
                v = i - MAHEAD
                if 0 <= v < MUNITS:
                    pe.wait_ge(probs_scaled, UNITS + v + 1)
                    turn(f"et{v}", MT, MPR[:, v % (MAHEAD + 1), :])
                v = i - MAHEAD - 1
                if v >= 0:
                    j, h, qt = v // 8, v // 4 % 2, v % 4
                    if v % 8 == 0:
                        outs["mo"] = take(f"mo{j}")
                    pe.wait_ge(*is_free(f"et{v}"))
                    for t in range(MT):
                        last = pe.matmul(outs["mo"][h * DH:(h + 1) * DH, qt * P:(qt + 1) * P],
                                         VMEM[:, t, (2 * j + h) * DH:(2 * j + h + 1) * DH],
                                         MPT[:, v % 2, t * P:(t + 1) * P], start=t == 0, stop=t == MT - 1)
                    if v % 8 == 7:
                        full_inc(last, f"mo{j}")

            outs = {}

            def project_part(name, lo, hi):
                x = name[0]
                if lo == 0:
                    outs[x] = take(name)
                last = split_product(name, outs[x], lambda k: UHX[:, k, :], lambda k: UL[:, k, :], order=range(lo, hi),
                                     first=lo == 0, last=hi == DK)
                if hi == DK:
                    full_inc(last, name)

            def low_rank(p):
                pe.wait_ge(low_used, 1)
                for x, src in (("w", TZ[:, 0, :]), ("A", TZ[:, 1, :])):
                    one(f"{x}_{p}", SV[:, LORA_AT + p * P:LORA_AT + (p + 1) * P], src)

            def kk_sum(p):
                pe.wait_ge(kk_sq, p + 1)
                one(f"kks_{p}", tab("heads"), HS[:, 0, :])

            def bonus_sum(p):
                pe.wait_ge(bonus_in, p + 1)
                one(f"bon_{p}", tab("heads"), T2)

            def gn_mean(p):
                pe.wait_ge(*is_free(f"y_{p}_{NG - 1}"))
                one(f"gm_{p}", tab("heads"), CAT[:, p, :])

            def gn_square(p):
                pe.wait_ge(gn_sq, p + 1)
                one(f"gv_{p}", tab("heads"), HS[:, 1, :])

            def gate_low_rank(p):
                pe.wait_ge(sig_out, sig_at["gd_sig"][0] + 1)
                one(f"gg_{p}", SV[:, G2_AT + p * P:G2_AT + (p + 1) * P], SGD)

            def four(name, *terms):
                out = take(name).rearrange("p (g t) -> p g t", g=G)
                for c in range(G):
                    for n, (stationary, moving) in enumerate(terms):
                        last = pe.matmul(out[:, c, :], stationary[:, c, :], moving[:, c, :],
                                         start=n == 0, stop=n == len(terms) - 1)
                full_inc(last, name)

            def turn4(name, src):
                out = take(name).rearrange("p (g t) -> p g t", g=G)
                for c in range(G):
                    last = pe.transpose(out[:, c, :], src[:, c, :], tab("ident"))
                full_inc(last, name)

            def part(x, g):
                return x[:, g * G:(g + 1) * G, :]

            project_part("k_0", 0, DK)
            low_rank(0)
            project_part("r_0", 0, DK)
            project_part("v_0", 0, DK)
            kk_sum(0)
            bonus_sum(0)
            low_rank(1)
            project_part("k_1", 0, DK)
            project_part("r_1", 0, DK)
            kk_sum(1)
            for p in range(NP):
                pe.wait_ge(bd_ready, p + 1)
                pe.wait_ge(k_blocks, p + 1)
                pe.wait_ge(r_ready, p + 1)
                for x, a, b in (("nt", BBD, ABD), ("nn", ABD, BBD)):
                    for g in range(NG):
                        four(f"{x}_{p}_{g}", (part(a, g), part(b, g)))
                for x, a in (("ta", ABD), ("tb", BBD), ("tk", KBD), ("tv", VBD)):
                    if x == "tv":
                        pe.wait_ge(v_ready, p + 1)
                    for g in range(NG):
                        turn4(f"{x}_{p}_{g}", part(a, g))
                for x, a, b in (("mak", KBD, ABD), ("mrb", BBD, RBD[p % 2]), ("mrk", KBD, RBD[p % 2])):
                    for g in range(NG):
                        four(f"{x}_{p}_{g}", (part(a, g), part(b, g)))
                prev = None
                for b in LEVELS:
                    for g in range(NG):
                        if prev is None:
                            pe.wait_ge(x_first, NG * p + g + 1)
                        else:
                            pe.wait_ge(*is_free(f"xn{prev}_{p}_{g}"))
                        four(f"xp{b}_{p}_{g}", (NT[g], XN[g]))
                        turn4(f"xt{b}_{p}_{g}", XN[g])
                    if p and b == LEVELS[0]:
                        gn_mean(p - 1)
                    if p and b == LEVELS[1]:
                        gn_square(p - 1)
                    if p and b == LEVELS[3]:
                        gate_low_rank(p - 1)
                    if p + 1 < NP and b == LEVELS[1]:
                        project_part(f"v_{p + 1}", 0, DK // 2)
                    if p + 1 < NP and b == LEVELS[3]:
                        bonus_sum(p + 1)
                    if p == NP - 1:
                        memory_unit(2 * LEVELS.index(b))
                    for g in range(NG):
                        pe.wait_ge(*is_free(f"xp{b}_{p}_{g}"))
                        pe.wait_ge(*is_free(f"xt{b}_{p}_{g}"))
                        if b != LEVELS[-1]:
                            four(f"xn{b}_{p}_{g}", (XT[g], XP[g]))
                        else:
                            four(f"xf{b}_{p}_{g}", (XP[g], XT[g]))
                        if p + 1 < NP and b == LEVELS[1] and g == 0:
                            project_part(f"v_{p + 1}", DK // 2, DK)
                    if p == NP - 1:
                        memory_unit(2 * LEVELS.index(b) + 1)
                    prev = b
                for g in range(NG):
                    pe.wait_ge(*is_free(f"mak_{p}_{g}"))
                    pe.wait_ge(*is_free(f"tv_{p}_{g}"))
                    four(f"mv_{p}_{g}", (MAK[g], TV[g]))
                for g in range(NG):
                    pe.wait_ge(*is_free(f"xf{LEVELS[-1]}_{p}_{g}"))
                    pe.wait_ge(*is_free(f"ta_{p}_{g}"))
                    four(f"w_{p}_{g}", (XT[g], TA[g]))
                for g in range(NG):
                    pe.wait_ge(*is_free(f"mv_{p}_{g}"))
                    four(f"u_{p}_{g}", (XT[g], MV[g]))
                for g in range(NG):
                    pe.wait_ge(*is_free(f"w_{p}_{g}"))
                    pe.wait_ge(*is_free(f"tb_{p}_{g}"))
                    four(f"gt_{p}_{g}", (WB[g], TBT[g]))
                for g in range(NG):
                    pe.wait_ge(*is_free(f"mrb_{p}_{g}"))
                    four(f"rp_{p}_{g}", (WB[g], MRB[g]))
                for g in range(NG):
                    pe.wait_ge(*is_free(f"u_{p}_{g}"))
                    pe.wait_ge(*is_free(f"tk_{p}_{g}"))
                    four(f"f_{p}_{g}", (TBT[g], UB[g]), (TK[g], TV[g]))
                def outputs(g):
                    pe.wait_ge(*is_free(f"rp_{p}_{g}"))
                    pe.wait_ge(*is_free(f"mrk_{p}_{g}"))
                    four(f"y_{p}_{g}", (H[g], RP[g]), (UB[g], MRB[g]), (TV[g], MRK[g]))

                if p + 2 < NP:
                    low_rank(p + 2)
                for n in range(NC - 1):
                    g, c = divmod(n, G)
                    if c == 0:
                        pe.wait_ge(*is_free(f"gt_{p}_{g}"))
                    if n:
                        pe.wait_ge(*is_free(f"h_{p}_{n - 1}"))
                    else:
                        pe.wait_ge(zeroed, 9)
                    one(f"h_{p}_{n}", GT[g][:, c, :], H[g][:, c, :], P)
                    if n == G and p == NP - 2:
                        head_sums(8)
                    if n == G:
                        outputs(0)
                    if p + 1 < NP:
                        for x, lo, hi in BESIDE_CHAIN[n]:
                            project_part(beside_chain(p, x), lo, hi)
                    else:
                        memory_unit(MU_CHAIN + n)
                pe.wait_ge(*is_free(f"h_{p}_{NC - 2}"))
                outputs(1)
                if p + 2 < NP:
                    kk_sum(p + 2)
                elif p + 1 < NP:
                    head_sums(9)
            for n, step in enumerate((gn_mean, gn_square, gate_low_rank)):
                memory_unit(MU_CHAIN + NC - 1 + n)
                step(NP - 1)

            def mixed_tile(n, k):
                pe.wait_ge(cat_low, n + 1)

            def normed_tile(n, k):
                pe.wait_ge(u_low, 2 * DK + n + 1)

            for m in range(DK):
                full_inc(split_product(f"mix{m}", take(f"mix{m}"), lambda k: CATH[:, k, :], lambda k: CATL[:, k, :],
                                       order=CAT_ORDER, each=mixed_tile if m == 0 else None), f"mix{m}")
            pe.wait_ge(tiles_summed, 3)
            one("h2_sum", tab("ones"), SQ2[:, 0, :])
            for h in range(HALVES):
                for m in range(h * FH_TILES, (h + 1) * FH_TILES):
                    full_inc(split_product(f"up{m}", take(f"up{m}"), lambda k: UH[:, k, :], lambda k: UL[:, k, :],
                                           each=normed_tile if m == 0 else None), f"up{m}")
                for m in range(DK):
                    out = take(f"down{h}_{m}")
                    for b in range(DOWN_BLOCKS):
                        def hidden_tile(n, k):
                            pe.wait_ge(h_low, h * FH_TILES + b * DK + n + 1)

                        ins = split_product(f"down{h}_{m}_{b}", out, lambda k: FH[:, b * DK + k, :],
                                            lambda k: FL[:, b * DK + k, :], first=b == 0, last=b == DOWN_BLOCKS - 1,
                                            each=hidden_tile if m == 0 else None)
                        if b < DOWN_BLOCKS - 1:
                            ins.then_inc(half_used, 1)
                    full_inc(ins, f"down{h}_{m}")

        @block.scalar
        def _(act):
            steps = [0]

            def link(ins):
                steps[0] += 1
                ins.then_inc(act_step, 1)
                act.wait_ge(act_step, steps[0])

            def rms(name, out, w, scale, eps, done):
                act.wait_ge(*is_full(name))
                free_inc(act.activation(out, bank(name, w), ACT.Ln, bias=eps, scale=scale), name)
                act.wait_ge(*is_free(name))
                act.activation(out, out, ACT.Exp, scale=-0.5).then_inc(done, 1)

            def sigmoid(name, src, out=None, bias=0.0, scale=-1.0, rows=slice(0, P)):
                n, exp_done = sig_at[name]
                e = SG[rows, n % 2, :]
                if n >= 2 and sigmoids[n - 2][2] is not None:
                    act.wait_ge(*sigmoids[n - 2][2])
                act.activation(e, src, ACT.Exp, bias=bias, scale=scale).then_inc(exp_done[0], 1)
                act.wait_ge(sig_den, n + 1)
                link(act.activation(e, e, ACT.Ln))
                act.activation(e if out is None else out, e, ACT.Exp, scale=-1.0).then_inc(sig_out, 1)

            def head_norm(name, w=S, weight=None, rot_before=None):
                head_squares(name, w, weight, rot_before)
                head_rstd(name, w)

            def head_squares(name, w=S, weight=None, rot_before=None):
                n = head_at[name]
                act.wait_ge(*is_full(name))
                act.activation(HS[:, n % 2, 0:w], bank(name, w), ACT.Square).then_inc(head_sq, 1)
                if weight is not None:
                    if rot_before is not None:
                        act.wait_ge(*is_free(rot_before))
                    free_inc(act.activation(QW[:, 0:w], bank(name, w), ACT.Copy, scale=weight), name)

            def head_rstd(name, w=S):
                n = head_at[name]
                if n >= 2:
                    act.wait_ge(*heads[n - 2][1])
                rms(f"hs{n}", HR[:, n % 2, 0:w], w, 1.0 / DH, EPS, head_rs)

            def copy_out(name, out, w=None, before=None):
                act.wait_ge(*is_full(name))
                free_inc(act.activation(out, bank(name, w) if len(out.shape) == 2 else bank4(name), ACT.Copy), name)

            act.preload_act_table_set("natural_log_exp_and_others")
            act.wait_ge(mem_in, 16)
            act.activation(SQ[:, :, 0:SM], MEM, ACT.Square).then_inc(squares, 1)
            act.wait_ge(ctx_in, 16)
            act.activation(SQ[:, :, SM:SM + SC], CTX, ACT.Square).then_inc(squares, 1)
            act.wait_ge(small_in, 16)
            act.activation(SILU_E, cols("cc", 0, 2 * DK), ACT.Exp, scale=-1.0).then_inc(c_exp, 1)
            rms("mem_sum", RS[:, 0, 0:SM], SM, 1.0 / D, EPS, rstd)
            rms("ctx_sum", RS[:, 1, 0:SC], SC, 1.0 / D, EPS, rstd)
            act.wait_ge(c_den, 1)
            link(act.activation(SILU_E, SILU_E, ACT.Ln))
            act.activation(SILU_E, SILU_E, ACT.Exp, scale=-1.0).then_inc(c_sig, 1)
            head_norm("kmem0", SM)
            head_norm("kmem1", SM)
            for k in range(DK):
                act.wait_ge(x_in, 16)
                act.activation(SQ[:, k, :], X[:, k, :], ACT.Square).then_inc(squares, 1)
            act.wait_ge(normed, 1)

            def modulation_rows(g, rows):
                for i, h in enumerate(("lo", "hi")):
                    act.wait_ge(*is_full(f"{g}_{h}"))
                    free_inc(act.activation(rows[0:2, i * S:(i + 1) * S], bank(f"{g}_{h}", S, slice(0, 2)),
                                            ACT.Copy), f"{g}_{h}")

            modulation_rows("shift", MODROW[0])
            rms("x_sum", RS[:, 0, :], S, 1.0 / D, EPS, rstd)
            modulation_rows("scale", MODROW[1])

            def weights_high(q):
                first = q < 2 or group(q) != group(q - 2)
                if not first:
                    act.wait_ge(*split_used(q - 2))
                elif group(q) == 0:
                    act.wait_ge(*is_full("x_sum"))
                elif group(q) == 1:
                    act.wait_ge(*is_full("cvar"))
                elif group(q) == 2:
                    act.wait_ge(w_low, SPLIT_AT["out7"] + 1)
                else:
                    act.wait_ge(*is_full(f"y_{NP - 1}_{NG - 1}"))
                b = BLOCK_AT[SPLIT[q]]
                act.wait_ge(slot[SLOT[b]], 16 * USES[b])
                act.activation(WH[group(q)][:, q % 2, :], ring[:, SLOT[b], :], ACT.Copy).then_inc(w_high, 1)

            weights_high(0)
            weights_high(1)
            for k in range(DK):
                act.wait_ge(normed, 2 + k)
                act.activation(UH[:, k, :], U[:, k, :], ACT.Copy).then_inc(u_high, 1)
            copy_out("vmem", VMEM.rearrange("p a b -> p (a b)"))
            for n, x in enumerate(IN_BLOCKS):
                if n + 2 < len(IN_BLOCKS):
                    weights_high(n + 2)
                if x[0] == "g":
                    act.wait_ge(*is_full(x))
                    sigmoid(x, bank(x))
                if x == "k":
                    head_norm("kx", weight=col("kn"))
                    head_norm("kc", SC)
                if x == "v":
                    copy_out("vx", RS[:, 0, :])
                    flat = VT.rearrange("p a b -> p (a b)")
                    copy_out("v_lo", flat[:, 0:SC], SC)
                if x == "q0":
                    copy_out("v_hi", flat[:, SC:SKEYS], S)
                if x[0] == "q":
                    head_squares(x, weight=col("qn"), rot_before=f"rot{x[1]}")
                if n > SPLIT_AT["q0"] and n <= SPLIT_AT["q0"] + NQ:
                    head_rstd(IN_BLOCKS[n - 1])
                if x[0] == "z":
                    act.wait_ge(*is_full(x))
                    sigmoid(x, bank(x))

            def exp_scores(i, base, s_name, t_name, probs, n, w):
                act.wait_ge(negmax, base + i + 1)
                if i >= n:
                    act.wait_ge(*is_full(f"{t_name}{i - n}"))
                free_inc(act.activation(probs[:, i % n, :], bank(f"{s_name}{i}", w), ACT.Exp,
                                        bias=NEGMAX[:, i % 4:i % 4 + 1], scale=DH ** -0.5,
                                        accum_out=ROWSUM[:, i % 4:i % 4 + 1]), f"{s_name}{i}")

            act.wait_ge(q_ready, NQ)
            modulation_rows("gate", MODROW[0])
            for i in range(UNITS + AHEAD):
                if i < UNITS:
                    exp_scores(i, 0, "s", "pt", PR, AHEAD + 1, SKEYS)
                if i >= AHEAD:
                    copy_out(f"pt{i - AHEAD}", PT[:, i % 2, :], SKEYS)
                if i == 14:
                    act.wait_ge(*is_free("cmean"))
                    act.activation(SQ[:, 0:CK, :], CV, ACT.Square).then_inc(conv_sq, 1)
                if i == 16:
                    rms("cvar", RS[:, 1, :], S, 1.0 / (CK * P), EPS, conv_rs)
                if 18 <= i < 18 + CK:
                    act.wait_ge(conv_ln, i - 17)
                    sigmoid(f"conv{i - 18}", CV[:, i - 18, :])

            weights_high(SPLIT_AT["out0"])
            weights_high(SPLIT_AT["out0"] + 1)
            for k in OUT_ORDER:
                act.wait_ge(*is_free(f"o{k}" if k < NQ else f"pw{k - NQ}"))
                act.activation(OUTH[:, k, :], CAT[:, k, :], ACT.Copy).then_inc(out_high, 1)

            for m in range(DK):
                if m + 2 < DK:
                    weights_high(SPLIT_AT["out0"] + m + 2)
                act.wait_ge(*is_free(f"out{m}"))
                act.activation(SQ1[:, m, :], X[:, m, :], ACT.Square).then_inc(res_squares, 1)
            weights_high(SPLIT_AT["wdad"])
            weights_high(SPLIT_AT["gd"])
            rms("h1_sum", RS[:, 0, :], S, 1.0 / D, EPS, rstd)
            act.wait_ge(x_saved, 16 * DK)
            for k in range(DK):
                act.wait_ge(normed, 3 + DK + k)
                act.activation(UHX[:, k, :], U[:, k, :], ACT.Copy).then_inc(u_high, 1)

            def shift_start(name, n, out):
                act.wait_ge(*is_full(name))
                act.activation(out, bank(name), ACT.Copy, scale=MU1[:, n:n + 1]).then_inc(partial, 1)
                if group(SPLIT_AT[name] + 2) == 2:
                    weights_high(SPLIT_AT[name] + 2)

            act.wait_ge(consts_ready, 1)
            shift_start("wdad", MU_WDAD, T1)
            shift_start("gd", MU_GD, T2)
            act.wait_ge(*is_free("wdad"))
            sigmoid("wd", T1[0:DH, :], scale=-2.0, rows=slice(0, DH))
            act.wait_ge(*is_free("gd"))
            sigmoid("gd_sig", T2, out=SGD)

            def memory_unit(i):
                if i < MUNITS:
                    exp_scores(i, UNITS, "e", "et", MPR, MAHEAD + 1, SM)
                if 0 <= i - MAHEAD < MUNITS:
                    copy_out(f"et{i - MAHEAD}", MPT[:, (i - MAHEAD) % 2, :], SM)

            def pair_inputs(p):
                if p:
                    act.wait_ge(bd_ready, p)
                    act.wait_ge(r_ready, p)
                for i, (x, out) in enumerate((("w", EL), ("A", AV))):
                    act.wait_ge(*is_full(f"{x}_{p}"))
                    sigmoid(f"{x}_{p}", bank(f"{x}_{p}"), out=out, bias=NEG[:, i * NP + p:i * NP + p + 1])
                shift_start(f"k_{p}", MU_PAIR + 3 * p, K0)
                act.wait_ge(scan_done, p + 1)
                act.activation(T1, T1, ACT.Exp, scale=-DECAY)
                link(act.activation(EL, LG, ACT.Exp, scale=-DECAY))
                act.activation(LG, LG, ACT.Exp, scale=DECAY).then_inc(exps_done, 1)
                act.wait_ge(*is_free(f"k_{p}"))
                if p:
                    act.wait_ge(*is_full(f"kks_{p - 1}"))
                act.activation(HS[:, 0, :], K0, ACT.Square, scale=col("k_k", p)).then_inc(kk_sq, 1)
                shift_start(f"r_{p}", MU_PAIR + 3 * p + 1, R0)
                act.wait_ge(*is_free(f"kks_{p}"))
                link(act.activation(HR[:, 0, :], HR[:, 0, :], ACT.Ln, scale=KK_SCALE))
                act.activation(HR[:, 0, :], HR[:, 0, :], ACT.Exp, scale=-0.5,
                               bias=float(0.5 * np.log(KK_SCALE))).then_inc(kk_rs, 1)

            def pair_values(p):
                if p:
                    act.wait_ge(v_ready, p)
                shift_start(f"v_{p}", MU_PAIR + 3 * p + 2, V0)

            def value_blocks(p):
                act.wait_ge(*is_free(f"v_{p}"))
                if p:
                    act.wait_ge(*is_full(f"tv_{p - 1}_{NG - 1}"))
                else:
                    act.wait_ge(zeroed, 8)
                v3 = V0.rearrange("p (c t) -> p c t", c=NC)
                act.activation(VBD[0:DH, :, 0:DH], v3[0:DH], ACT.Copy)
                act.activation(VBD[DH:P, :, DH:P], v3[DH:P], ACT.Copy).then_inc(v_ready, 1)

            def gn_squares(p):
                act.wait_ge(*is_free(f"gm_{p}"))
                act.activation(HS[:, 1, :], CAT[:, p, :], ACT.Square).then_inc(gn_sq, 1)

            def gn_rstd(p):
                rms(f"gv_{p}", HR[:, 1, :], S, 1.0 / DH, GN_EPS, gn_rs)

            pair_inputs(0)
            pair_values(0)
            value_blocks(0)
            pair_inputs(1)
            for p in range(NP):
                for x, out in (("ta", TA), ("tb", TBT), ("tk", TK), ("tv", TV)):
                    for g in range(NG):
                        copy_out(f"{x}_{p}_{g}", out[g])
                for b in LEVELS:
                    for g in range(NG):
                        copy_out(f"xt{b}_{p}_{g}", XT[g])
                    if p == NP - 1:
                        memory_unit(2 * LEVELS.index(b))
                        memory_unit(2 * LEVELS.index(b) + 1)
                    if p and b == LEVELS[0]:
                        gn_squares(p - 1)
                    if p and b == LEVELS[1]:
                        gn_rstd(p - 1)
                    if p + 1 < NP and b == LEVELS[1]:
                        pair_values(p + 1)
                    if p + 1 < NP and b == LEVELS[2]:
                        value_blocks(p + 1)
                for x, out in (("mv", MV), ("w", WB), ("u", UB)):
                    for g in range(NG):
                        copy_out(f"{x}_{p}_{g}", out[g])
                if p + 2 < NP:
                    pair_inputs(p + 2)
                elif p + 1 < NP:
                    head_norm("qm0")
                    head_norm("qm1")

            def mixed_high(k):
                act.activation(CATH[:, k, :], CAT[:, k, :], ACT.Copy).then_inc(cat_high, 1)

            act.wait_ge(*is_full(f"mrk_{NP - 1}_{NG - 1}"))
            for n in range(NC - 1):
                memory_unit(MU_CHAIN + n)
                if n < NP - 1:
                    act.wait_ge(*is_free(f"gg_{n}"))
                    mixed_high(n)
            weights_high(SPLIT_AT["mix0"])
            memory_unit(MU_CHAIN + NC - 1)
            gn_squares(NP - 1)
            memory_unit(MU_CHAIN + NC)
            gn_rstd(NP - 1)
            for j in range(2):
                act.wait_ge(*is_free(f"mo{j}"))
                mixed_high(NP + j)
            act.wait_ge(*is_free(f"gg_{NP - 1}"))
            mixed_high(CAT_ORDER[-1])
            for q in range(SPLIT_AT["mix0"], len(SPLIT)):
                name = SPLIT[q - 1]
                if name.startswith("mix"):
                    m = int(name[3:])
                    act.wait_ge(*is_free(name))
                    act.activation(SQ2[:, m, :], X[:, m, :], ACT.Square).then_inc(res_squares, 1)
                    if m == DK - 1:
                        rms("h2_sum", RS[:, 1, :], S, 1.0 / D, EPS, rstd)
                        for k in range(DK):
                            act.wait_ge(normed, 3 + 2 * DK + k)
                            act.activation(UH[:, k, :], U[:, k, :], ACT.Copy).then_inc(u_high, 1)
                if name.startswith("up"):
                    m = int(name[2:])
                    t = m % FH_TILES
                    act.wait_ge(*is_full(name))
                    free_inc(act.activation(FS[:, t, :], bank(name), ACT.Relu), name)
                    act.wait_ge(*is_free(name))
                    act.activation(FS[:, t, :], FS[:, t, :], ACT.Square).then_inc(h_relu, 1)
                    act.wait_ge(h_relu, m + 1)
                    act.activation(FH[:, t, :], FS[:, t, :], ACT.Copy).then_inc(h_high, 1)
                if q + 1 < len(SPLIT):
                    weights_high(q + 1)

        @block.vector
        def _(vec):
            steps = [0]

            def link(ins):
                steps[0] += 1
                ins.then_inc(vec_step, 1)
                vec.wait_ge(vec_step, steps[0])

            def scaled_product(out, a, scalar, b, op=ALU.mult):
                return vec.scalar_tensor_tensor(out=out, in0=a, scalar=scalar, in1=b, op0=op, op1=ALU.mult)

            def scaled_sum(out, a, scalar, b, op=ALU.mult):
                return vec.scalar_tensor_tensor(out=out, in0=a, scalar=scalar, in1=b, op0=op, op1=ALU.add)

            def denominator(name, rows=slice(0, P)):
                n, exp_done = sig_at[name]
                vec.wait_ge(*exp_done)
                e = SG[rows, n % 2, :]
                vec.tensor_scalar(e, e, SIG_MOST, 1.0, ALU.min, ALU.add).then_inc(sig_den, 1)

            def sigmoid_of(name, rows=slice(0, P)):
                n, _ = sig_at[name]
                vec.wait_ge(sig_out, n + 1)
                return SG[rows, n % 2, :]

            def add_squares(tiles, m, ready):
                vec.wait_ge(*ready)
                if m > 1:
                    vec.wait_ge(vec_step, steps[0])
                ins = vec.tensor_tensor(tiles[:, 0, :], tiles[:, 0, :], tiles[:, m, :], ALU.add)
                if m == DK - 1:
                    ins.then_inc(tiles_summed, 1)
                else:
                    steps[0] += 1
                    ins.then_inc(vec_step, 1)

            vec.wait_ge(small_in, 16)
            link(vec.tensor_scalar(NEG, cols("w0", 0, 2 * NP), -1.0, None, ALU.mult))
            link(vec.tensor_scalar(KA1, cols("k_a", 0, NP), -1.0, 1.0, ALU.mult, ALU.add))
            vec.tensor_scalar(MU1, cols("mu", 0, 20), -1.0, 1.0, ALU.mult, ALU.add).then_inc(consts_ready, 1)
            vec.wait_ge(c_exp, 1)
            vec.tensor_scalar(SILU_E, SILU_E, SIG_MOST, 1.0, ALU.min, ALU.add).then_inc(c_den, 1)
            vec.wait_ge(rstd, 1)
            for k in range(DK):
                ins = scaled_product(MEM[:, k, :], MEM[:, k, :], col("g_mem", k), RS[:, 0, 0:SM])
            ins.then_inc(normed, 1)
            vec.wait_ge(c_sig, 1)
            vec.tensor_tensor(SILU_C, cols("cc", 0, 2 * DK).rearrange("p (k w) -> p k w", k=DK),
                              SILU_E.rearrange("p (k w) -> p k w", k=DK), ALU.mult).then_inc(c_ready, 1)
            vec.wait_ge(rstd, 2)
            for k in range(DK):
                vec.tensor_tensor(CTX[:, k, :], CTX[:, k, :], RS[:, 1, 0:SC], ALU.mult)
            for i in range(2):
                vec.wait_ge(head_rs, i + 1)
                free_inc(scaled_product(KMEM[:, i, :], bank(f"kmem{i}", SM), col("mkn"), HR[:, i, 0:SM]), f"kmem{i}")
            for k in range(1, DK):
                add_squares(SQ, k, (squares, 3 + k))
            vec.wait_ge(rstd, 3)
            for k in range(DK):
                ins = vec.tensor_tensor(U[:, k, :], X[:, k, :], RS[:, 0, :], ALU.mult)
            link(ins)

            def modulation_columns(g, i, bias):
                vec.wait_ge(*is_full(f"{g}_t"))
                b = cols(bias, 0, DK)[:, :, None].to_broadcast([P, DK, 2])
                free_inc(vec.tensor_tensor(MOD[:, i], bank(f"{g}_t", 2 * DK).rearrange("p (k w) -> p k w", k=DK),
                                           b, ALU.add), f"{g}_t")

            modulation_columns("shift", 0, "b_shift")
            modulation_columns("scale", 1, "b_scale")
            vec.wait_ge(*is_free("scale_t"))
            link(scaled_product(MOD[:, 1], MOD[:, 1], 1.0,
                                cols("norm_w", 0, DK)[:, :, None].to_broadcast([P, DK, 2]), ALU.add))

            def weights_low(q):
                b = BLOCK_AT[SPLIT[q]]
                vec.wait_ge(w_high, q + 1)
                vec.tensor_tensor(WL[group(q)][:, q % 2, :], ring[:, SLOT[b], :],
                                  WH[group(q)][:, q % 2, :].bitcast(F32), ALU.subtract).then_inc(w_low, 1)

            def normed_low(n, k):
                vec.wait_ge(u_high, n * DK + k + 1)
                vec.tensor_tensor(UL[:, k, :], U[:, k, :], (UH, UHX, UH)[n][:, k, :].bitcast(F32), ALU.subtract).then_inc(u_low, 1)

            for k in range(DK + 1):
                if k < DK:
                    vec.tensor_scalar(U[:, k, :], U[:, k, :], MOD[:, 1, k, 0:1], MOD[:, 0, k, 0:1], ALU.mult,
                                      ALU.add).then_inc(normed, 1)
                if k:
                    normed_low(0, k - 1)
                if k == DK // 2 + 1:
                    vec.wait_ge(*is_full("vmem"))
                    weights_low(0)
            weights_low(1)
            for k in range(DK):
                ins = vec.tensor_scalar(CTX[:, k, :], CTX[:, k, :], MOD[:, 1, k, 1:2], MOD[:, 0, k, 1:2],
                                        ALU.mult, ALU.add)
            ins.then_inc(normed, 1)
            vec.wait_ge(zeroed, 1)

            def glu(i):
                denominator(f"g{i}")
                s = sigmoid_of(f"g{i}")
                vec.wait_ge(*is_full(f"a{i}"))
                free_inc(vec.tensor_tensor(GLU[:, i, PAD:PAD + S], bank(f"a{i}"), s, ALU.mult), f"a{i}")

            def convolve(i, lo, hi):
                vec.wait_ge(*is_free(f"a{i}"))
                sums = (CV[:, i, :], CT)
                for t in range(lo, hi):
                    w = col("conv_w", i * TAPS + t)
                    src = GLU[:, i, t:t + S]
                    if t == 1 and i:
                        vec.wait_ge(conv_out, i)
                    if t >= 2:
                        vec.wait_ge(vec_step, steps[0] - 1)
                    if t == 0:
                        ins = vec.tensor_scalar(sums[0], src, w, col("conv_b", i), ALU.mult, ALU.add)
                    elif t == 1:
                        ins = vec.tensor_scalar(sums[1], src, w, None, ALU.mult)
                    else:
                        ins = scaled_sum(sums[t % 2], src, w, sums[t % 2])
                    ins.then_inc(vec_step, 1)
                    steps[0] += 1
                if hi == TAPS:
                    vec.wait_ge(vec_step, steps[0])
                    vec.tensor_tensor(CV[:, i, :], CV[:, i, :], CT, ALU.add).then_inc(conv_out, 1)

            def rotary(n, rs):
                link(vec.tensor_tensor(T1, QW[:], tab("cos"), ALU.mult))
                vec.wait_ge(*is_full(f"rot{n}"))
                free_inc(vec.tensor_tensor(T2, bank(f"rot{n}"), tab("sin"), ALU.mult), f"rot{n}")
                vec.wait_ge(*is_free(f"rot{n}"))
                link(vec.tensor_tensor(T1, T1, T2, ALU.add))
                vec.wait_ge(head_rs, rs + 1)

            def queries(j):
                vec.wait_ge(*((q_ready, j) if j else (k_ready, 1)))
                vec.wait_ge(*is_free(f"q{j}"))
                rotary(1 + j, 4 + j)
                vec.tensor_tensor(QZ[0:DH, 0, j, :], T1[0:DH, :], HR[0:DH, j % 2, :], ALU.mult)
                vec.tensor_tensor(QZ[DH:P, 1, j, :], T1[DH:P, :], HR[DH:P, j % 2, :], ALU.mult).then_inc(q_ready, 1)

            taps = 0
            for n, x in enumerate(IN_BLOCKS):
                if n + 2 < len(IN_BLOCKS):
                    weights_low(n + 2)
                if x[0] == "g":
                    glu(int(x[1]))
                if x == "k":
                    vec.wait_ge(token_tables_in, 16)
                    vec.wait_ge(*is_free("kx"))
                    rotary(0, 2)
                    vec.tensor_tensor(KTT[:, SC:SKEYS], T1, HR[:, 0, :], ALU.mult).then_inc(k_ready, 1)
                    vec.wait_ge(head_rs, 4)
                    free_inc(scaled_product(KTT[:, 0:SC], bank("kc", SC), col("kn"), HR[:, 1, 0:SC]), "kc")
                    vec.wait_ge(zeroed, 2)
                if n > SPLIT_AT["q0"] and n <= SPLIT_AT["q0"] + NQ:
                    queries(int(IN_BLOCKS[n - 1][1]))
                if x[0] == "z":
                    denominator(x)
                    s = sigmoid_of(x)
                    out = ZC if x[1] == "c" else ZA
                    free_inc(vec.tensor_tensor(out[:, int(x[2]), :], bank(x), s, ALU.mult), x)
                more = min(IN_TAPS[n], CK * TAPS - taps)
                while more:
                    lo = taps % TAPS
                    hi = min(lo + more, TAPS)
                    convolve(taps // TAPS, lo, hi)
                    taps += hi - lo
                    more -= hi - lo
            convolve(2, taps - 2 * TAPS, TAPS)

            def row_max(i, s_name, w):
                vec.wait_ge(*is_full(f"{s_name}{i}"))
                one = slice(i % 4, i % 4 + 1)
                link(vec.tensor_reduce(ROWMAX[:, one], bank(f"{s_name}{i}", w), AX, ALU.max))
                vec.tensor_scalar(NEGMAX[:, one], ROWMAX[:, one], -DH ** -0.5, None, ALU.mult).then_inc(negmax, 1)

            def divide(i, s_name, probs, n):
                vec.wait_ge(*is_free(f"{s_name}{i}"))
                one = slice(i % 4, i % 4 + 1)
                link(vec.reciprocal(ROWINV[:, one], ROWSUM[:, one]))
                vec.tensor_scalar(probs[:, i % n, :], probs[:, i % n, :], ROWINV[:, one], None,
                                  ALU.mult).then_inc(probs_scaled, 1)

            def gated_heads(j):
                vec.wait_ge(*is_full(f"o{j}"))
                free_inc(vec.tensor_tensor(CAT[:, j, :], bank(f"o{j}"), ZA[:, j, :], ALU.mult), f"o{j}")

            vec.wait_ge(*is_free("za3"))
            for i in range(UNITS + 1):
                if 24 <= i < 24 + CK:
                    n = i - 24
                    vec.wait_ge(*is_full(f"pw{n}"))
                    free_inc(scaled_product(CAT[:, NQ + n, :], bank(f"pw{n}"), col("b_pw", n), ZC[:, n, :], ALU.add),
                             f"pw{n}")
                if i < UNITS:
                    row_max(i, "s", SKEYS)
                if i:
                    divide(i - 1, "s", PR, AHEAD + 1)
                if i >= 8 + AHEAD + 1 and (i - AHEAD - 1) % 8 == 0:
                    gated_heads((i - AHEAD - 1) // 8 - 1)
                if i <= 10:
                    convolve(3, 3 * i, min(3 * i + 3, TAPS))
                if i == 4:
                    modulation_columns("gate", 2, "b_gate")
                if 13 <= i < 15:
                    vec.wait_ge(*is_full("cmean"))
                    for n in range(2 * (i - 13), 2 * (i - 12)):
                        ins = scaled_sum(CV[:, n, :], bank("cmean"), -1.0 / (CK * P), CV[:, n, :])
                    if i == 14:
                        free_inc(ins, "cmean")
                if 17 <= i < 17 + CK:
                    n = i - 17
                    vec.wait_ge(conv_rs, 1)
                    link(scaled_product(CV[:, n, :], CV[:, n, :], col("ln_w", n), RS[:, 1, :]))
                    vec.tensor_scalar(CV[:, n, :], CV[:, n, :], col("ln_b", n), None, ALU.add).then_inc(conv_ln, 1)
                if 19 <= i < 19 + CK:
                    n = i - 19
                    denominator(f"conv{n}")
                    s = sigmoid_of(f"conv{n}")
                    vec.tensor_tensor(CV[:, n, :], CV[:, n, :], s, ALU.mult).then_inc(conv_act, 1)
            gated_heads(NQ - 1)
            vec.wait_ge(conv_out, CK)
            weights_low(SPLIT_AT["out0"])
            for n, k in enumerate(OUT_ORDER):
                vec.wait_ge(out_high, n + 1)
                vec.tensor_tensor(OUTL[:, k, :], CAT[:, k, :], OUTH[:, k, :].bitcast(F32), ALU.subtract
                                  ).then_inc(out_low, 1)
            weights_low(SPLIT_AT["out0"] + 1)
            vec.wait_ge(*is_free("gate_t"))
            for m in range(DK):
                if m + 2 < DK:
                    weights_low(SPLIT_AT["out0"] + m + 2)
                vec.wait_ge(*is_full(f"out{m}"))
                free_inc(scaled_sum(X[:, m, :], bank(f"out{m}"), MOD[:, 2, m, 0:1], X[:, m, :]), f"out{m}")
                if m > 1:
                    add_squares(SQ1, m - 1, (res_squares, m))
            add_squares(SQ1, DK - 1, (res_squares, DK))

            def normalise(n, row, gain, behind=None):
                vec.wait_ge(rstd, n)
                for k in range(DK + 1):
                    if k < DK:
                        scaled_product(U[:, k, :], X[:, k, :], col(gain, k), RS[:, row, :]).then_inc(normed, 1)
                    if k and behind:
                        behind(k - 1)

            weights_low(SPLIT_AT["wdad"])
            weights_low(SPLIT_AT["gd"])
            normalise(4, 0, "g_mix", lambda k: normed_low(1, k))

            def shift_end(name, n, m, out):
                vec.wait_ge(partial, n)
                return scaled_sum(out[:, 1:S], bank(name)[:, 0:S - 1], col("mu", m), out[:, 1:S])

            free_inc(shift_end("wdad", 1, MU_WDAD, T1), "wdad")
            weights_low(SPLIT_AT["wdad"] + 2)
            vec.wait_ge(*is_free("wdad"))
            vec.wait_ge(zeroed, 3)
            vec.tensor_copy(TZ[DH:P, 1, :], T1[DH:P, :])
            free_inc(shift_end("gd", 2, MU_GD, T2), "gd")
            weights_low(SPLIT_AT["gd"] + 2)
            denominator("wd", slice(0, DH))
            s = sigmoid_of("wd", slice(0, DH))
            vec.tensor_scalar(TZ[0:DH, 0, :], s, 2.0, -1.0, ALU.mult, ALU.add).then_inc(low_used, 1)
            denominator("gd_sig")

            def memory_queries(i):
                vec.wait_ge(zeroed, 11)
                vec.wait_ge(head_rs, 9 + i)
                scaled_product(QMZ[0:DH, 0, i, :], bank(f"qm{i}", S, slice(0, DH)), col("mqn", 0, slice(0, DH)),
                               HR[0:DH, i, :])
                free_inc(scaled_product(QMZ[DH:P, 1, i, :], bank(f"qm{i}", S, slice(DH, P)),
                                        col("mqn", 0, slice(DH, P)), HR[DH:P, i, :]), f"qm{i}")

            def memory_heads(j):
                vec.wait_ge(*is_full(f"mo{j}"))
                free_inc(vec.tensor_copy(CAT[:, NP + j, :], bank(f"mo{j}")), f"mo{j}")

            def memory_unit(i):
                if i == 8 + MAHEAD + 1:
                    memory_heads(0)
                if i < MUNITS:
                    row_max(i, "e", SM)
                if 1 <= i <= MUNITS:
                    divide(i - 1, "e", MPR, MAHEAD + 1)

            def pair_input(p, x):
                i = "krv".index(x)
                free_inc(shift_end(f"{x}_{p}", 3 + 3 * p + i, MU_PAIR + 3 * p + i, (K0, R0, V0)[i]), f"{x}_{p}")

            def weights_after(p, x):
                if group(SPLIT_AT[f"{x}_{p}"] + 2) == 2:
                    weights_low(SPLIT_AT[f"{x}_{p}"] + 2)

            def blocks_of(out, make):
                a = make(out[0:DH, :, 0:DH], slice(0, DH))
                return make(out[DH:P, :, DH:P], slice(DH, P))

            def chunks(x, rows):
                return x[rows, :].rearrange("p (c t) -> p c t", c=NC)

            def running_sums(p):
                vec.wait_ge(sig_out, sig_at[f"w_{p}"][0] + 1)
                if p:
                    vec.wait_ge(k_blocks, p)
                link(vec.tensor_tensor_scan(LG, tab("reset"), EL, 0.0, ALU.mult, ALU.add))
                vec.tensor_tensor(T1, LG, EL, ALU.subtract).then_inc(scan_done, 1)

            def changed_key(p):
                vec.wait_ge(sig_out, sig_at[f"A_{p}"][0] + 1)
                link(vec.tensor_scalar(QW[:], AV, col("k_a", p), KA1[:, p:p + 1], ALU.mult, ALU.add))
                vec.wait_ge(*is_free(f"k_{p}"))
                link(vec.tensor_tensor(QW[:], QW[:], K0, ALU.mult))
                vec.wait_ge(*is_free(f"r_{p}"))
                scaled_product(T2, R0, col("r_k", p), QW[:]).then_inc(bonus_in, 1)

            def least_norm(p):
                vec.wait_ge(*is_full(f"kks_{p}"))
                free_inc(vec.tensor_scalar(HR[:, 0, :], bank(f"kks_{p}"), KK_LEAST, None, ALU.max), f"kks_{p}")

            def bonus(p):
                vec.wait_ge(*is_free(f"v_{p}"))
                if p >= 2:
                    vec.wait_ge(gn_done, p - 1)
                vec.wait_ge(*is_full(f"bon_{p}"))
                free_inc(vec.tensor_tensor(BV[p % 2], bank(f"bon_{p}"), V0, ALU.mult), f"bon_{p}")

            def blocks_r(p):
                vec.wait_ge(exps_done, p + 1)
                vec.tensor_copy(ELC[p % 2], EL[:, C - 1:S:C])
                vec.wait_ge(zeroed, 8 if p == 0 else 10)
                if p >= 2:
                    vec.wait_ge(*is_full(f"rp_{p - 2}_{NG - 1}"))
                blocks_of(RBD[p % 2], lambda o, r: vec.tensor_tensor(o, chunks(R0, r), chunks(EL, r), ALU.mult)
                          ).then_inc(r_ready, 1)

            def unit_key(p):
                vec.wait_ge(kk_rs, p + 1)
                scaled_product(KKN, K0, col("k_k", p), HR[:, 0, :]).then_inc(key_step, 1)

            def blocks_a(p):
                vec.wait_ge(key_step, 3 * p + 1)
                if p:
                    vec.wait_ge(*is_full(f"mrk_{p - 1}_{NG - 1}"))
                blocks_of(ABD, lambda o, r: vec.scalar_tensor_tensor(
                    out=o, in0=chunks(KKN, r), scalar=-1.0, in1=chunks(T1, r), op0=ALU.mult, op1=ALU.mult)
                          ).then_inc(key_step, 1)

            def blocks_b(p):
                vec.wait_ge(key_step, 3 * p + 2)
                vec.tensor_tensor(KKN, KKN, AV, ALU.mult).then_inc(key_step, 1)
                vec.wait_ge(key_step, 3 * p + 3)
                blocks_of(BBD, lambda o, r: vec.tensor_tensor(o, chunks(KKN, r), chunks(LG, r), ALU.mult)
                          ).then_inc(bd_ready, 1)

            def gn_centre(p):
                vec.wait_ge(*is_full(f"gm_{p}"))
                free_inc(scaled_sum(CAT[:, p, :], bank(f"gm_{p}"), -1.0 / DH, CAT[:, p, :]), f"gm_{p}")

            def gn_finish(p):
                o = CAT[:, p, :]
                vec.wait_ge(gn_rs, p + 1)
                link(scaled_product(o, o, col("lnx_g", p), HR[:, 1, :]))
                scaled_sum(o, o, col("lnx_b", p), BV[p % 2], ALU.add).then_inc(gn_done, 1)

            def gate(p):
                o = CAT[:, p, :]
                vec.wait_ge(gn_done, p + 1)
                vec.wait_ge(*is_full(f"gg_{p}"))
                free_inc(vec.tensor_tensor(o, bank(f"gg_{p}"), o, ALU.mult), f"gg_{p}")

            def mixed_low(n):
                k = CAT_ORDER[n]
                vec.wait_ge(cat_high, n + 1)
                vec.tensor_tensor(CATL[:, k, :], CAT[:, k, :], CATH[:, k, :].bitcast(F32), ALU.subtract
                                  ).then_inc(cat_low, 1)

            for p in range(2):
                denominator(f"w_{p}")
                denominator(f"A_{p}")
                running_sums(p)
                for x in "kr":
                    pair_input(p, x)
                    weights_after(p, x)
                changed_key(p)
                least_norm(p)
                if p == 0:
                    pair_input(0, "v")
                    weights_after(0, "v")
                    bonus(0)
                    blocks_r(0)
                    unit_key(0)
                    blocks_a(0)
                    blocks_b(0)
                else:
                    blocks_r(1)
            for p in range(NP):
                for g in range(NG):
                    vec.wait_ge(*is_full(f"nt_{p}_{g}"))
                    free_inc(vec.tensor_tensor(NT[g], bank4(f"nt_{p}_{g}"), tab4("before"), ALU.mult), f"nt_{p}_{g}")
                for g in range(NG):
                    vec.wait_ge(*is_full(f"nn_{p}_{g}"))
                    free_inc(vec.tensor_tensor(XN[g], bank4(f"nn_{p}_{g}"), tab4("m1"), ALU.mult), f"nn_{p}_{g}")
                    vec.wait_ge(*is_free(f"nn_{p}_{g}"))
                    vec.tensor_tensor(XN[g], XN[g], tab4("ident"), ALU.add).then_inc(x_first, 1)
                for x, out, mask in (("mak", MAK, "before"), ("mrb", MRB, "upto"), ("mrk", MRK, "upto")):
                    for g in range(NG):
                        vec.wait_ge(*is_full(f"{x}_{p}_{g}"))
                        free_inc(vec.tensor_tensor(out[g], bank4(f"{x}_{p}_{g}"), tab4(mask), ALU.mult),
                                 f"{x}_{p}_{g}")
                for b in LEVELS:
                    for g in range(NG):
                        name = f"xp{b}_{p}_{g}"
                        vec.wait_ge(*is_full(name))
                        free_inc(vec.tensor_tensor(XP[g], bank4(name), tab4(f"m{b}"), ALU.mult), name)
                    if p and b == LEVELS[0]:
                        gn_centre(p - 1)
                    if p == NP - 1:
                        memory_unit(2 * LEVELS.index(b))
                    if p + 1 < NP and b == LEVELS[1]:
                        blocks_a(p + 1)
                    if p + 1 < NP and b == LEVELS[2]:
                        pair_input(p + 1, "v")
                    if p + 1 < NP and b == LEVELS[3]:
                        blocks_b(p + 1)
                    for g in range(NG):
                        name, x, odd = ((f"xn{b}_{p}_{g}", XN[g], 0) if b != LEVELS[-1]
                                        else (f"xf{b}_{p}_{g}", XT[g], 1))
                        vec.wait_ge(*is_full(name))
                        new, old = (y.rearrange("p g (n two b) -> p (g n) two b", two=2, b=b)[:, :, odd, :]
                                    for y in (bank4(name), x))
                        free_inc(vec.tensor_tensor(old, new, old, ALU.add), name)
                    if p == NP - 1:
                        memory_unit(2 * LEVELS.index(b) + 1)
                    if p and b == LEVELS[2]:
                        gn_finish(p - 1)
                    if p and b == LEVELS[3]:
                        gate(p - 1)
                    if p + 1 < NP:
                        if b == LEVELS[2]:
                            weights_after(p + 1, "v")
                        if b == LEVELS[0]:
                            unit_key(p + 1)
                        if b == LEVELS[3]:
                            bonus(p + 1)
                for g in range(NG):
                    vec.wait_ge(*is_full(f"gt_{p}_{g}"))
                    free_inc(vec.tensor_tensor(GT[g], bank4(f"gt_{p}_{g}"), tab4("ident"), ALU.add), f"gt_{p}_{g}")
                for g in range(NG):
                    vec.wait_ge(*is_full(f"rp_{p}_{g}"))
                    free_inc(vec.tensor_tensor(RP[g], bank4(f"rp_{p}_{g}"), RBD[p % 2][:, g * G:(g + 1) * G, :], ALU.add),
                             f"rp_{p}_{g}")
                for g in range(NG):
                    vec.wait_ge(*is_full(f"f_{p}_{g}"))
                    free_inc(vec.tensor_tensor(FB[g], bank4(f"f_{p}_{g}"),
                                               ELC[p % 2][:, g * G:(g + 1) * G, None].to_broadcast([P, G, P]), ALU.mult),
                             f"f_{p}_{g}")
                    vec.wait_ge(*is_free(f"f_{p}_{g}"))
                def outputs(g):
                    name = f"y_{p}_{g}"
                    vec.wait_ge(*is_full(name))
                    y = CAT[:, p, g * G * C:(g + 1) * G * C].rearrange("p (c t) -> p c t", c=G)
                    vec.tensor_copy(y[0:DH], bank4(name)[0:DH, :, 0:DH])
                    free_inc(vec.tensor_copy(y[DH:P], bank4(name)[DH:P, :, DH:P]), name)

                for n in range(NC - 1):
                    name = f"h_{p}_{n}"
                    vec.wait_ge(*is_full(name))
                    g, c = divmod(n, G)
                    g1, c1 = divmod(n + 1, G)
                    free_inc(scaled_sum(H[g1][:, c1, :], bank(name, P), ELC[p % 2][:, n:n + 1], FB[g][:, c, :]), name)
                    if n == G + 1:
                        outputs(0)
                    if p == NP - 1:
                        memory_unit(MU_CHAIN + n)
                    if p == NP - 2 and n == G:
                        memory_queries(0)
                    if p + 2 < NP:
                        if n == 0:
                            denominator(f"w_{p + 2}")
                        if n == 1:
                            denominator(f"A_{p + 2}")
                        if n == 3:
                            running_sums(p + 2)
                        if n == 4:
                            pair_input(p + 2, "k")
                        if n == 5:
                            weights_after(p + 2, "k")
                if p + 2 < NP:
                    pair_input(p + 2, "r")
                outputs(1)
                if p + 2 < NP:
                    weights_after(p + 2, "r")
                if p + 2 < NP:
                    changed_key(p + 2)
                    least_norm(p + 2)
                    blocks_r(p + 2)
                elif p + 1 < NP:
                    memory_queries(1)
            gn_centre(NP - 1)
            for n in range(3):
                mixed_low(n)
            weights_low(SPLIT_AT["mix0"])
            gn_finish(NP - 1)
            gate(NP - 1)
            memory_heads(1)
            for n in range(3, DK - 1):
                mixed_low(n)
            mixed_low(DK - 1)
            vec.wait_ge(x_in, 32)
            for q in range(SPLIT_AT["mix0"], len(SPLIT) + 1):
                name = SPLIT[q - 1]
                if name.startswith("mix"):
                    m = int(name[3:])
                    vec.wait_ge(*is_full(name))
                    free_inc(vec.tensor_tensor(X[:, m, :], bank(name), X[:, m, :], ALU.add), name)
                    if m > 1:
                        add_squares(SQ2, m - 1, (res_squares, DK + m))
                    if m == DK - 1:
                        add_squares(SQ2, m, (res_squares, DK + m + 1))
                        normalise(5, 1, "g_ffn", lambda k: normed_low(2, k))
                if name.startswith("up"):
                    m = int(name[2:])
                    t = m % FH_TILES
                    vec.wait_ge(h_high, m + 1)
                    vec.tensor_tensor(FL[:, t, :], FS[:, t, :], FH[:, t, :].bitcast(F32), ALU.subtract
                                      ).then_inc(h_low, 1)
                if name.endswith(f"_{DOWN_BLOCKS - 1}"):
                    product = name.rsplit("_", 1)[0]
                    m = int(product.split("_")[1])
                    vec.wait_ge(*is_full(product))
                    free_inc(vec.tensor_tensor(X[:, m, :], bank(product), X[:, m, :], ALU.add), product)
                if q + 1 < len(SPLIT):
                    weights_low(q + 1)


def tables_of_shapes():
    t = {}
    tok = np.arange(S)
    dim = np.arange(P) % DH
    half = DH // 2
    freq = (10000.0 ** (-(np.arange(0, half, 2, dtype=np.float32)) / np.float32(half))).astype(np.float32)
    pos = np.where((dim < half)[:, None], (tok // GRID_W)[None, :], (tok % GRID_W)[None, :]).astype(np.float32)
    ang = pos * freq[dim % (half // 2)][:, None]
    t["cos"], t["sin"] = np.cos(ang), np.sin(ang)
    t["reset"] = np.broadcast_to((tok % C != 0).astype(np.float32), (P, S))
    rot = np.zeros((P, P), np.float32)
    for d in range(P):
        if d % half < half // 2:
            rot[d + half // 2, d] = -1.0
            rot[d, d + half // 2] = 1.0
    t["rot"] = rot
    r, c = np.arange(P)[:, None], np.arange(P)[None, :]
    same = r // DH == c // DH
    t["heads"] = same
    t["ones"] = np.ones((P, P))
    t["ident"] = r == c
    t["before"] = same & (r < c)
    t["upto"] = same & (r <= c)

    def band(b):
        return (r // (2 * b) == c // (2 * b)) & (r // b % 2 == 1) & (c // b % 2 == 0)

    t["m1"] = band(1)
    for b in LEVELS:
        t[f"m{b}"] = band(b)
    return np.ascontiguousarray(np.concatenate([np.asarray(t[k], np.float32) for k, _ in TAB], axis=1))


def feature_major(x):
    return np.ascontiguousarray(x.T.reshape(-1, P, x.shape[0]).transpose(1, 0, 2))


def stationary(w, rows=None):
    w = w if rows is None else w[rows]
    return w.reshape(-1, P, w.shape[1]).transpose(1, 0, 2).reshape(P, -1)


def kernel(**inputs):
    import concourse.bacc as bacc
    from concourse.bass_utils import run_bass_kernel_spmd

    a = {k: np.asarray(v) for k, v in inputs.items()}
    w_in, w_mod, rw_in = a["w_in"][0], a["w_mod"][0], a["rw_in_2"][0]
    w_pw, w_out, w_kv = a["w_pw"][0], a["w_out"][0], a["w_mem_kv_2"]
    w_mix, w_up, w_down = a["w_out_2"][0], a["w_ff1_2"][0], a["w_ff2_2"][0]
    DA = NQ * P
    K_AT, V_AT, ZA_AT = DA, DA + P, DA + 2 * P
    A_AT = ZA_AT + DA
    G_AT, ZC_AT = A_AT + CK * P, A_AT + 2 * CK * P
    MW = NP * P

    def pair(j):
        return np.concatenate([np.arange(j * DH, (j + 1) * DH), np.arange((NQ + j) * DH, (NQ + j + 1) * DH)])

    out_rows = np.concatenate([pair(j) for j in range(NQ)] + [np.arange(DA, D)])

    def block(name):
        if name.startswith("kmem"):
            return stationary(w_kv[:, int(name[4]) * P:(int(name[4]) + 1) * P])
        if name.startswith("vmem"):
            h = int(name[4])
            return stationary(w_kv[h * 4 * P:(h + 1) * 4 * P, SM:2 * SM])
        for i, g in enumerate(("shift", "scale", "gate")):
            if name.startswith(g):
                k = int(name[len(g):])
                return w_mod[k * P:(k + 1) * P, i * D:(i + 1) * D]
        if name == "wdad":
            return stationary(rw_in[:, 3 * MW:3 * MW + P])
        if name == "gd":
            return stationary(rw_in[:, 3 * MW + P:3 * MW + 2 * P])
        if name[:2] == "qm":
            at = 3 * MW + (2 + int(name[2])) * P
            return stationary(rw_in[:, at:at + P])
        if name[1:2] == "_":
            at = "krv".index(name[0])
            at = (1, 0, 2)[at] * MW + int(name[2]) * P
            return stationary(rw_in[:, at:at + P])
        if name == "k":
            return stationary(w_in[:, K_AT:K_AT + P])
        if name == "v":
            return stationary(w_in[:, V_AT:V_AT + P])
        if name[:2] == "zc":
            at = ZC_AT + int(name[2]) * P
            return stationary(w_in[:, at:at + P])
        if name[:2] == "za":
            return stationary(w_in[:, ZA_AT + pair(int(name[2]))])
        if name[:2] == "pw":
            i = int(name[2])
            return np.concatenate([stationary(w_pw[:, m * P:(m + 1) * P]) for m in (2 * i, 2 * i + 1)], axis=1)
        if name.startswith("out"):
            m = int(name[3])
            return stationary(w_out[:, m * P:(m + 1) * P], out_rows)
        if name.startswith("mix"):
            m = int(name[3])
            return stationary(w_mix[:, m * P:(m + 1) * P])
        if name.startswith("up"):
            m = int(name[2:])
            return stationary(w_up[:, m * P:(m + 1) * P])
        if name.startswith("down"):
            h, m, b = map(int, name[4:].split("_"))
            k = h * DOWN_BLOCKS + b
            return stationary(w_down[k * D:(k + 1) * D, m * P:(m + 1) * P])
        if name[0] == "q":
            return stationary(w_in[:, pair(int(name[1]))])
        at = (A_AT if name[0] == "a" else G_AT) + int(name[1]) * P
        return stationary(w_in[:, at:at + P])

    weights = np.stack([block(n) for n in BLOCKS])

    def columns(x):
        return x.reshape(-1, P).T

    two = np.concatenate
    mu = a["rw_mu_2"][0]
    mus = [mu[3 * MW:3 * MW + P], mu[3 * MW + P:3 * MW + 2 * P]]
    for p in range(NP):
        mus += [mu[at * MW + p * P:at * MW + (p + 1) * P] for at in (1, 0, 2)]
    b_mod = a["b_mod"][0]
    conv_w = a["conv_w"][0]
    vec = {
        "norm_w": columns(a["norm_w"][0]), "b_shift": columns(b_mod[0:D]), "b_scale": columns(b_mod[D:2 * D]),
        "b_gate": columns(b_mod[2 * D:]), "qn": columns(two([a["q_norm_w"][0]] * 2)),
        "kn": columns(two([a["k_norm_w"][0]] * 2)), "conv_b": columns(a["conv_b"][0]),
        "ln_w": columns(a["conv_ln_w"][0]), "ln_b": columns(a["conv_ln_b"][0]), "b_pw": columns(a["b_pw"][0]),
        "conv_w": conv_w.T.reshape(CK, P, TAPS).transpose(1, 0, 2).reshape(P, -1),
        "mu": np.stack(mus, axis=1), "w0": columns(a["rw_w0_2"][0]), "a0": columns(a["rw_a0_2"][0]),
        "k_k": columns(a["rw_k_k_2"][0]), "k_a": columns(a["rw_k_a_2"][0]),
        "r_k": columns(a["rw_r_k_2"][0].reshape(-1)), "lnx_g": columns(a["rw_lnx_g_2"][0]),
        "lnx_b": columns(a["rw_lnx_b_2"][0]), "g_mix": columns(a["norm_mix_g_2"][0]),
        "g_ffn": columns(a["norm_ffn_g_2"][0]), "g_mem": columns(a["mem_norm_g_2"]),
        "mqn": columns(two([a["mem_q_norm_g_2"][0]] * 2)), "mkn": columns(two([a["mem_k_norm_g_2"][0]] * 2)),
        "cc": np.stack([a["c"][0], a["c_ctx"]], axis=1).reshape(DK, P, 2).transpose(1, 0, 2).reshape(P, -1),
    }
    lora = two([a["rw_w2_2"][0], a["rw_a2_2"][0]], axis=0)
    small = two([vec[k] for k, _ in VEC] + [lora, a["rw_g2_2"][0]], axis=1)
    sent = {"small": small, "tables": tables_of_shapes(), "xT": feature_major(a["x"][0]),
            "ctxT": feature_major(a["ctx"][0]), "memT": feature_major(a["mem_2"][0]), "weights": weights}
    sent = {k: np.ascontiguousarray(v) for k, v in sent.items()}
    nc = bacc.Bacc("TRN2", target_bir_lowering=False, num_devices=1)
    args = {k: nc.dram_tensor(k, v.shape, F32, kind="ExternalInput").ap() for k, v in sent.items()}
    out = nc.dram_tensor("outT", (P, DK, S), F32, kind="ExternalOutput").ap()
    saved = nc.dram_tensor("residual_saved", (P, DK, S), F32, kind="Internal").ap()
    build(nc, saved=saved, outT=out, **args)
    r = run_bass_kernel_spmd(nc, [sent], core_ids=[0])
    got = r.results[0]["outT"]
    return np.ascontiguousarray(got.transpose(1, 0, 2).reshape(D, S).T)[None]
```
